# Optimizing a Trainium2 kernel written in Bass

```python
import jax
import jax.numpy as jnp
from jax import lax
import numpy as np

D_MODEL = 1024
BATCH = 1
SEQ = 1024
DEPTH = 1

GRID_W = 64
CTX_LEN = 256

N_HEADS_MLA = 8
Q_LORA = 384
KV_LORA = 256
QK_NOPE = 64
QK_ROPE = 32
QK_HEAD = QK_NOPE + QK_ROPE
V_HEAD = 64
W_MLA = N_HEADS_MLA * V_HEAD
ROPE_THETA = 10000.0
Q_BLOCK = 128
ATTN_SCALE = QK_HEAD ** -0.5

CONV_W = 512
CONV_K = 3

RWKV_HEADS = 8
RWKV_HEAD = 64
W_RWKV = RWKV_HEADS * RWKV_HEAD
W_LORA = 64
A_LORA = 64

N_BRANCH = 3
IN_SIZES = (Q_LORA, KV_LORA, QK_ROPE, W_MLA,
            CONV_W, CONV_W, CONV_W, CONV_W,
            W_RWKV, W_RWKV, W_RWKV,
            W_LORA, W_LORA, A_LORA, A_LORA,
            W_RWKV,
            N_BRANCH * D_MODEL)
D_IN = sum(IN_SIZES)

RMS_EPS = 1e-6
GN_EPS = 64e-5
L2_EPS = 1e-12

kernel_name = 'hybrid_mla_shortconv_rwkv7_dit'

def rms_norm(x, g):
    xf = x.astype(jnp.float32)
    y = xf * lax.rsqrt(jnp.mean(xf * xf, axis=-1, keepdims=True) + RMS_EPS)
    return (y * g.astype(jnp.float32)).astype(x.dtype)

def ada_mod(cvec, w_mod, b_mod):
    m = jax.nn.silu(cvec) @ w_mod + b_mod
    shift, scale, gate = jnp.split(m, 3, axis=-1)
    return shift[..., None, :], scale[..., None, :], gate[..., None, :]

def project_in(h_res, mod, g_pre, w_in):
    shift, scale, _ = mod
    h = rms_norm(h_res, g_pre) * (1 + scale) + shift
    return jnp.split(h @ w_in, np.cumsum(IN_SIZES)[:-1].tolist(), axis=-1)

def axial_rope_tables(length):
    n_rows = length // GRID_W
    row = jnp.repeat(jnp.arange(n_rows), GRID_W).astype(jnp.float32)
    col = jnp.tile(jnp.arange(GRID_W), n_rows).astype(jnp.float32)
    n_freq = QK_ROPE // 4
    inv = ROPE_THETA ** (-jnp.arange(n_freq, dtype=jnp.float32) / n_freq)
    ang = jnp.concatenate([row[:, None] * inv, col[:, None] * inv], axis=-1)
    return jnp.cos(ang), jnp.sin(ang)

def apply_rope(x, cos, sin):
    xf = x.astype(jnp.float32)
    x1, x2 = xf[..., 0::2], xf[..., 1::2]
    out = jnp.stack([x1 * cos - x2 * sin, x1 * sin + x2 * cos], axis=-1).reshape(x.shape)
    return out.astype(x.dtype)

def mla_queries(q_lat, g_q, w_uq, rope):
    bsz, length = q_lat.shape[:2]
    q = (rms_norm(q_lat, g_q) @ w_uq).reshape(bsz, length, N_HEADS_MLA, QK_HEAD)
    q_nope, q_rot = q[..., :QK_NOPE], q[..., QK_NOPE:]
    if rope is not None:
        q_rot = apply_rope(q_rot, rope[0][:, None, :], rope[1][:, None, :])
    return jnp.concatenate([q_nope, q_rot], axis=-1)

def mla_keys_values(kv_lat, k_rope, g_kv, w_ukv, rope):
    bsz, length = kv_lat.shape[:2]
    kv = (rms_norm(kv_lat, g_kv) @ w_ukv).reshape(bsz, length, N_HEADS_MLA, QK_NOPE + V_HEAD)
    k_nope, v = kv[..., :QK_NOPE], kv[..., QK_NOPE:]
    if rope is not None:
        k_rope = apply_rope(k_rope, rope[0], rope[1])
    k_rot = jnp.broadcast_to(k_rope[:, :, None, :], (bsz, length, N_HEADS_MLA, QK_ROPE))
    return jnp.concatenate([k_nope, k_rot], axis=-1), v

def softmax_attention(q, k, v):
    s = jnp.einsum('bqhd,bkhd->bhqk', q.astype(jnp.float32), k.astype(jnp.float32)) * ATTN_SCALE
    p = jax.nn.softmax(s, axis=-1)
    return jnp.einsum('bhqk,bkhd->bqhd', p, v.astype(jnp.float32))

def blocked_attention(q, k, v):
    bsz, length, heads, dk = q.shape
    qb = jnp.moveaxis(q.reshape(bsz, length // Q_BLOCK, Q_BLOCK, heads, dk), 1, 0)
    out = lax.map(lambda qi: softmax_attention(qi, k, v), qb)
    return jnp.moveaxis(out, 0, 1).reshape(bsz, length, heads * V_HEAD).astype(v.dtype)

def short_conv(x_in, b_gate, c_gate, conv_w, conv_b):
    u = c_gate * x_in
    up = jnp.pad(u, ((0, 0), (1, 1), (0, 0)))
    y = up[:, :-2] * conv_w[0] + up[:, 1:-1] * conv_w[1] + up[:, 2:] * conv_w[2] + conv_b
    return b_gate * y

def wkv_scan(state0, r, decay, k, v, kk, a, reverse, emit):
    xs = tuple(jnp.moveaxis(t, 1, 0) for t in (r, decay, k, v, kk, a))

    def step(S, inp):
        r_t, w_t, k_t, v_t, kk_t, a_t = inp
        s_kk = jnp.einsum('bhvk,bhk->bhv', S, kk_t)
        S = S * w_t[:, :, None, :] - s_kk[..., None] * (kk_t * a_t)[:, :, None, :] + v_t[..., None] * k_t[:, :, None, :]
        y = jnp.einsum('bhvk,bhk->bhv', S, r_t) if emit else None
        return S, y

    S, ys = lax.scan(step, state0, xs, reverse=reverse)
    return S, (jnp.moveaxis(ys, 0, 1) if emit else None)

def head_group_norm(y, g, b):
    mu = jnp.mean(y, axis=-1, keepdims=True)
    var = jnp.mean(jnp.square(y - mu), axis=-1, keepdims=True)
    yn = (y - mu) * lax.rsqrt(var + GN_EPS)
    shp = (RWKV_HEADS, RWKV_HEAD)
    return yn * g.astype(jnp.float32).reshape(shp) + b.astype(jnp.float32).reshape(shp)

def rwkv_direction(d, r, k, v, kk, wd, ad, p, state0, emit):
    f32 = jnp.float32
    shp = r.shape
    logw = -jax.nn.softplus(-(p['w0'][d] + jnp.tanh(wd) @ p['w_up'][d]).astype(f32)) - 0.5
    decay = jnp.exp(-jnp.exp(logw)).reshape(shp)
    a = jax.nn.sigmoid((p['a0'][d] + ad @ p['a_up'][d]).astype(f32)).reshape(shp)
    k_d = k * (1 + (a - 1) * p['k_a'].astype(f32).reshape(RWKV_HEADS, RWKV_HEAD))
    S, y = wkv_scan(state0, r, decay, k_d, v, kk, a, reverse=(d == 1), emit=emit)
    bonus = jnp.sum(r * k_d * p['r_k'].astype(f32), axis=-1, keepdims=True) * v if emit else None
    return S, y, bonus

def rwkv_branch(parts, p, states0, emit):
    r, k, v, wd_f, wd_b, ad_f, ad_b = parts
    bsz, length = r.shape[:2]
    shp = (bsz, length, RWKV_HEADS, RWKV_HEAD)
    r, k, v = (t.astype(jnp.float32).reshape(shp) for t in (r, k, v))
    kk = k * p['k_k'].astype(jnp.float32).reshape(RWKV_HEADS, RWKV_HEAD)
    kk = kk * lax.rsqrt(jnp.sum(kk * kk, axis=-1, keepdims=True) + L2_EPS)
    S_f, y_f, bonus_f = rwkv_direction(0, r, k, v, kk, wd_f, ad_f, p, states0[0], emit)
    S_b, y_b, bonus_b = rwkv_direction(1, r, k, v, kk, wd_b, ad_b, p, states0[1], emit)
    if not emit:
        return (S_f, S_b), None
    y = head_group_norm(y_f + y_b, p['gn_g'], p['gn_b']) + bonus_f + bonus_b
    return (S_f, S_b), y.reshape(bsz, length, W_RWKV).astype(wd_f.dtype)

def merge_branches(h_res, mod, y_mla, y_conv, y_rwkv, g_mla, g_conv, g_rwkv, gate_logits, p):
    _, _, ada_gate = mod
    br_mla = (y_mla * jax.nn.silu(g_mla)) @ p['w_br_mla']
    br_conv = (y_conv * jax.nn.silu(g_conv)) @ p['w_br_conv']
    br_rwkv = (y_rwkv * jax.nn.silu(g_rwkv)) @ p['w_br_rwkv']
    s_mla, s_conv, s_rwkv = jnp.split(jax.nn.sigmoid(gate_logits), 3, axis=-1)
    merged = s_mla * br_mla + s_conv * br_conv + s_rwkv * br_rwkv
    return h_res + ada_gate * rms_norm(merged @ p['w_out'], p['g_post'])

def trunk_layer(x, ctx, c, c_ctx, p, rope, update_ctx):
    mod_x = ada_mod(c, p['w_mod'], p['b_mod'])
    mod_c = ada_mod(c_ctx, p['w_mod'], p['b_mod'])
    (q_lat_x, kv_lat_x, kr_x, g_mla_x, cv_in_x, cv_b_x, cv_c_x, g_conv_x,
     r_x, k_x, v_x, wdf_x, wdb_x, adf_x, adb_x, g_rwkv_x, gl_x) = project_in(x, mod_x, p['g_pre'], p['w_in'])
    (q_lat_c, kv_lat_c, kr_c, g_mla_c, cv_in_c, cv_b_c, cv_c_c, g_conv_c,
     r_c, k_c, v_c, wdf_c, wdb_c, adf_c, adb_c, g_rwkv_c, gl_c) = project_in(ctx, mod_c, p['g_pre'], p['w_in'])

    key_c, val_c = mla_keys_values(kv_lat_c, kr_c, p['g_kv'], p['w_ukv'], None)
    bsz = ctx.shape[0]
    zero_state = jnp.zeros((bsz, RWKV_HEADS, RWKV_HEAD, RWKV_HEAD), jnp.float32)
    ctx_states, y_rwkv_c = rwkv_branch((r_c, k_c, v_c, wdf_c, wdb_c, adf_c, adb_c), p,
                                       (zero_state, zero_state), emit=update_ctx)

    q_x = mla_queries(q_lat_x, p['g_q'], p['w_uq'], rope)
    key_x, val_x = mla_keys_values(kv_lat_x, kr_x, p['g_kv'], p['w_ukv'], rope)
    y_mla_x = blocked_attention(q_x, jnp.concatenate([key_c, key_x], axis=1),
                                jnp.concatenate([val_c, val_x], axis=1))
    y_conv_x = short_conv(cv_in_x, cv_b_x, cv_c_x, p['conv_w'], p['conv_b'])
    _, y_rwkv_x = rwkv_branch((r_x, k_x, v_x, wdf_x, wdb_x, adf_x, adb_x), p, ctx_states, emit=True)
    x_new = merge_branches(x, mod_x, y_mla_x, y_conv_x, y_rwkv_x, g_mla_x, g_conv_x, g_rwkv_x, gl_x, p)
    if not update_ctx:
        return x_new, None

    q_c = mla_queries(q_lat_c, p['g_q'], p['w_uq'], None)
    y_mla_c = softmax_attention(q_c, key_c, val_c).reshape(bsz, ctx.shape[1], W_MLA).astype(ctx.dtype)
    y_conv_c = short_conv(cv_in_c, cv_b_c, cv_c_c, p['conv_w'], p['conv_b'])
    ctx_new = merge_branches(ctx, mod_c, y_mla_c, y_conv_c, y_rwkv_c, g_mla_c, g_conv_c, g_rwkv_c, gl_c, p)
    return x_new, ctx_new

def setup_inputs(seed: int = 0) -> dict:
    key = jax.random.key(seed)
    ks = jax.random.split(key, 32)

    def nrm(k, shape, scale):
        return jax.random.normal(k, shape, jnp.float32) * scale

    D = D_MODEL
    return {
        'x': nrm(ks[0], (BATCH, SEQ, D), 1.0),
        'c': nrm(ks[1], (BATCH, D), 1.0),
        'ctx': nrm(ks[2], (BATCH, CTX_LEN, D), 1.0),
        'c_ctx': nrm(ks[3], (D,), 1.0),
        'w_mod': nrm(ks[4], (DEPTH, D, 3 * D), D ** -0.5),
        'b_mod': nrm(ks[5], (DEPTH, 3 * D), 0.02),
        'g_pre': 1.0 + nrm(ks[6], (DEPTH, D), 0.05),
        'g_post': 1.0 + nrm(ks[7], (DEPTH, D), 0.05),
        'w_in': nrm(ks[8], (DEPTH, D, D_IN), D ** -0.5),
        'g_q': 1.0 + nrm(ks[9], (DEPTH, Q_LORA), 0.05),
        'g_kv': 1.0 + nrm(ks[10], (DEPTH, KV_LORA), 0.05),
        'w_uq': nrm(ks[11], (DEPTH, Q_LORA, N_HEADS_MLA * QK_HEAD), Q_LORA ** -0.5),
        'w_ukv': nrm(ks[12], (DEPTH, KV_LORA, N_HEADS_MLA * (QK_NOPE + V_HEAD)), KV_LORA ** -0.5),
        'conv_w': nrm(ks[13], (DEPTH, CONV_K, CONV_W), CONV_K ** -0.5),
        'conv_b': nrm(ks[14], (DEPTH, CONV_W), 0.02),
        'w0': jax.random.uniform(ks[15], (DEPTH, 2, W_RWKV), jnp.float32, minval=-4.0, maxval=0.0),
        'w_up': nrm(ks[16], (DEPTH, 2, W_LORA, W_RWKV), W_LORA ** -0.5),
        'a0': nrm(ks[17], (DEPTH, 2, W_RWKV), 0.1),
        'a_up': nrm(ks[18], (DEPTH, 2, A_LORA, W_RWKV), 0.5 * A_LORA ** -0.5),
        'k_k': 0.85 + nrm(ks[19], (DEPTH, W_RWKV), 0.1),
        'k_a': 1.0 + nrm(ks[20], (DEPTH, W_RWKV), 0.1),
        'r_k': nrm(ks[21], (DEPTH, RWKV_HEADS, RWKV_HEAD), 0.1),
        'gn_g': 1.0 + nrm(ks[22], (DEPTH, W_RWKV), 0.05),
        'gn_b': nrm(ks[23], (DEPTH, W_RWKV), 0.02),
        'w_br_mla': nrm(ks[24], (DEPTH, W_MLA, D), W_MLA ** -0.5),
        'w_br_conv': nrm(ks[25], (DEPTH, CONV_W, D), CONV_W ** -0.5),
        'w_br_rwkv': nrm(ks[26], (DEPTH, W_RWKV, D), W_RWKV ** -0.5),
        'w_out': nrm(ks[27], (DEPTH, D, D), D ** -0.5),
    }

def reference(x, c, ctx, c_ctx, w_mod, b_mod, g_pre, g_post, w_in, g_q, g_kv, w_uq, w_ukv,
              conv_w, conv_b, w0, w_up, a0, a_up, k_k, k_a, r_k, gn_g, gn_b,
              w_br_mla, w_br_conv, w_br_rwkv, w_out):
    rope = axial_rope_tables(x.shape[1])
    for i in range(DEPTH):
        p = dict(w_mod=w_mod[i], b_mod=b_mod[i], g_pre=g_pre[i], g_post=g_post[i], w_in=w_in[i],
                 g_q=g_q[i], g_kv=g_kv[i], w_uq=w_uq[i], w_ukv=w_ukv[i],
                 conv_w=conv_w[i], conv_b=conv_b[i], w0=w0[i], w_up=w_up[i], a0=a0[i], a_up=a_up[i],
                 k_k=k_k[i], k_a=k_a[i], r_k=r_k[i], gn_g=gn_g[i], gn_b=gn_b[i],
                 w_br_mla=w_br_mla[i], w_br_conv=w_br_conv[i], w_br_rwkv=w_br_rwkv[i], w_out=w_out[i])
        x, ctx = trunk_layer(x, ctx, c, c_ctx, p, rope, update_ctx=(i < DEPTH - 1))
    return x


_drawn_inputs = setup_inputs


def setup_inputs(seed=0):
    import zlib

    import numpy as np

    out = dict(_drawn_inputs(seed))
    spreads = {}
    factors = {'ctx': 3.774,
     'g_q': 8.0,
     'g_kv': 8.0,
     'w_uq': 3.478,
     'conv_b': 50.093,
     'a0': 4.655,
     'gn_g': 23.881,
     'gn_b': 63.28}
    for name, (base, spread) in spreads.items():
        noise = np.random.default_rng([zlib.crc32(name.encode()), seed]).standard_normal(out[name].shape)
        drawn = base * np.exp(spread * noise) if base else spread * noise
        out[name] = jnp.asarray(drawn.astype(out[name].dtype))
    for name, factor in factors.items():
        out[name] = (out[name] * factor).astype(out[name].dtype)
    return out
```

```python
import math
from contextlib import ExitStack

import concourse.bass as bass
from concourse import mybir

ALU = mybir.AluOpType
ACT = mybir.ActivationFunctionType
AX = mybir.AxisListType
F32 = mybir.dt.float32
F32R = mybir.dt.float32r
U8 = mybir.dt.uint8
P = 128

D, SEQ, CTX = 1024, 1024, 256
KD = D // P
NTOK = SEQ + CTX
NT = NTOK // P
HEADS, HEAD = 8, 64
W = HEADS * HEAD
PAIRS = HEADS // 2
Q_LORA, KV_LORA, ROPE, NOPE = 384, 256, 32, 64
QK_HEAD = NOPE + ROPE
GRID_W, THETA = 64, 10000.0
SCALE = QK_HEAD ** -0.5
RMS_EPS, GN_EPS, L2_EPS = 1e-6, 64e-5, 1e-12
EPS = (RMS_EPS, GN_EPS, L2_EPS)
DECAY = math.exp(-0.5)

COLS = [("c", KD), ("c_ctx", KD), ("b_mod", 2 * KD), ("g_pre", KD), ("w0", 8), ("a0", 8), ("k_k", 4), ("k_a", 4),
        ("r_k", 4), ("gn_g", 4), ("gn_b", 4), ("conv_w", 12), ("conv_b", 4), ("g_q", 3), ("g_kv", 2)]
COL = {name: sum(n for _, n in COLS[:i]) for i, (name, _) in enumerate(COLS)}
NCOL = sum(n for _, n in COLS)
T_K, T_V, T_WD, T_AD, T_KV, T_KR, T_R, T_QL, T_F, T_GL = 0, 4, 8, 9, 10, 12, 14, 18, 21, 45


class Kept:
    pass


class Count:

    def __init__(self, sem):
        self.sem, self.n, self.before = sem, 0, 0

    def up(self, ins):
        ins.then_inc(self.sem, 1)
        self.n += 1
        return self.before + self.n

    def enter(self, i, per):
        self.start, self.per = self.n, per
        self.before, self.n = i * per + self.start, 0

    def leave(self, rounds):
        assert self.n == self.per, (self.n, self.per)
        self.before, self.n = 0, self.start + self.per * rounds


class Link(Count):

    def __init__(self, sem, eng):
        super().__init__(sem)
        self.eng = eng

    def __call__(self, ins):
        self.eng.wait_ge(self.sem, self.up(ins))


def memory(nc, stack):
    def sb(name, shape, dt=F32):
        return stack.enter_context(nc.sbuf_tensor(name, shape, dt))

    def ps(name, shape, dt=F32):
        return stack.enter_context(nc.psum_tensor(name, shape, dt))

    return sb, ps


def start(nc, sem, io, keep, stack):
    sb, ps = memory(nc, stack)
    space = keep.rk[:].rearrange("p f t -> p (f t)")
    x_in = space[:, 0:NT * D].rearrange("p (t c) -> p t c", c=D)
    wm = keep.r
    junk = space[:, NT * D:(NT + 1) * D]
    ss = sb("ss", [P, NT])
    rs = sb("rs", [P, NT])
    silu_t = sb("silu_t", [P, 2 * KD])
    silu_s = sb("silu_s", [P, 2 * KD])
    silu_c = keep.silu_c
    mod = sb("mod", [P, 2, 2 * KD])
    h_val = sb("h_val", [P, 2, 512])
    mod_ps = ps("mod_ps", [P, 512])
    tr_ps = ps("tr_ps", [P, 4, 512])
    cols, ident, hi, lo = keep.cols, keep.ident, keep.h_hi, keep.h_lo

    cols_in, x_land = sem("cols_in"), [sem(f"x_land{t}") for t in range(NT)]
    wm_land, wm_used = [sem(f"wm_land{b}") for b in range(4)], sem("wm_used")
    sq_done, rs_done, xn_done, id_done = sem("sq_done"), sem("rs_done"), sem("xn_done"), sem("id_done")
    silu_done, root_done, eps_done = sem("silu_done"), sem("root_done"), sem("eps_done")
    tr_done, val_done, hi_done, lo_done = sem("tr_done"), sem("val_done"), sem("hi_done"), sem("lo_done")
    pool_link, dve_link = sem("start_pool"), sem("start_dve")
    NF = 2 * KD
    groups = [(4 * g, min(4, NT - 4 * g)) for g in range((NT + 3) // 4)]
    order = [(g, k) for g in (2, 0, 1) for k in range(KD)]

    with nc.Block() as block:
        @block.sync
        def _(sp):
            sp.dma_start(cols[:], io["cols"]).then_inc(cols_in, 16)
            for f in range(4):
                sp.dma_start(wm[:, f, :], io["wm"][f]).then_inc(wm_land[f], 16)
            for t in (8, 9, 0, 1, 2, 3, 4, 5, 6, 7):
                src = io["ctx"][(t - 8) * P:(t - 7) * P, :] if t >= 8 else io["x"][t * P:(t + 1) * P, :]
                sp.dma_start(x_in[:, t, :], src).then_inc(x_land[t], 16)
                f = 4 + (t + 2) % 10
                if f < NF:
                    sp.wait_ge(wm_used, f - 3)
                    sp.dma_start(wm[:, f % 4, :], io["wm"][f]).then_inc(wm_land[f % 4], 16)
            for f in range(14, NF):
                sp.wait_ge(wm_used, f - 3)
                sp.dma_start(wm[:, f % 4, :], io["wm"][f]).then_inc(wm_land[f % 4], 16)

        @block.scalar
        def _(act):
            squares = Link(sq_done, act)
            act.wait_ge(cols_in, 16)
            act.wait_ge(eps_done, len(EPS))
            nc.scalar.activation(silu_t[:], cols[:, 0:2 * KD], ACT.Tanh, scale=0.5).then_inc(silu_done, 1)
            for t in (8, 9, 0, 1, 2, 3, 4, 5, 6, 7):
                act.wait_ge(x_land[t], 16)
                squares(nc.scalar.activation(junk, x_in[:, t, :], ACT.Square, accum_out=ss[:, t:t + 1]))
                nc.scalar.activation(ss[:, t:t + 1], ss[:, t:t + 1], ACT.Sqrt, scale=1.0 / D,
                                     bias=keep.eps[:, 0:1]).then_inc(root_done, 1)
            for n, (g, k) in enumerate(order):
                w = groups[g][1] * P
                act.wait_ge(val_done, n + 1)
                nc.scalar.activation(hi[:, k, g * 512:g * 512 + w], h_val[:, n % 2, 0:w], ACT.Copy).then_inc(hi_done, 1)

        @block.gpsimd
        def _(pool):
            link = Link(pool_link, pool)
            for e, value in enumerate(EPS):
                nc.gpsimd.memset(keep.eps[:, e:e + 1], value).then_inc(eps_done, 1)
            link(nc.gpsimd.memset(ident[:], 0.0))
            nc.gpsimd.affine_select(out=ident[:], in_=ident[:], compare_op=ALU.not_equal, fill=1.0, base=0,
                                    pattern=[[-1, P]], channel_multiplier=1).then_inc(id_done, 1)
            for n, t in enumerate((8, 9, 0, 1, 2, 3, 4, 5, 6, 7)):
                pool.wait_ge(rs_done, n + 1)
                nc.gpsimd.tensor_scalar(x_in[:, t, :], x_in[:, t, :], rs[:, t:t + 1], None, ALU.mult).then_inc(xn_done, 1)
            for n, (g, k) in enumerate(order):
                w = groups[g][1] * P
                pool.wait_ge(hi_done, n + 1)
                nc.gpsimd.tensor_tensor(lo[:, k, g * 512:g * 512 + w], h_val[:, n % 2, 0:w],
                                        hi[:, k, g * 512:g * 512 + w].bitcast(F32), ALU.subtract).then_inc(lo_done, 1)

        @block.vector
        def _(dve):
            link = Link(dve_link, dve)
            dve.wait_ge(silu_done, 1)
            link(nc.vector.tensor_scalar(silu_s[:], silu_t[:], 0.5, 0.5, ALU.mult, ALU.add))
            nc.vector.tensor_tensor(silu_c[:], silu_s[:].rearrange("p (s k) -> p k s", s=2),
                                    cols[:, 0:2 * KD].rearrange("p (s k) -> p k s", s=2), ALU.mult).then_inc(silu_done, 1)
            for n, t in enumerate((8, 9, 0, 1, 2, 3, 4, 5, 6, 7)):
                dve.wait_ge(root_done, n + 1)
                nc.vector.reciprocal(rs[:, t:t + 1], ss[:, t:t + 1]).then_inc(rs_done, 1)
            dve.wait_ge(wm_used, NF)
            bias = cols[:, COL["b_mod"]:COL["b_mod"] + NF]
            for s in range(2):
                link(nc.vector.tensor_tensor(mod[:, s, :], mod_ps[:, s:2 * NF:2], bias, ALU.add))
                link(nc.vector.scalar_tensor_tensor(mod[:, s, KD:NF], mod[:, s, KD:NF], 1.0,
                                                    cols[:, COL["g_pre"]:COL["g_pre"] + KD], ALU.add, ALU.mult))
            for n, (g, k) in enumerate(order):
                w, s = groups[g][1] * P, int(g == 2)
                dve.wait_ge(tr_done, n + 1)
                if n >= 2:
                    dve.wait_ge(lo_done, n - 1)
                nc.vector.tensor_scalar(h_val[:, n % 2, 0:w], tr_ps[:, n % 4, 0:w], mod[:, s, KD + k:KD + k + 1],
                                        mod[:, s, k:k + 1], ALU.mult, ALU.add).then_inc(val_done, 1)

        @block.tensor
        def _(pe):
            pe.wait_ge(silu_done, 2)
            for f in range(NF):
                pe.wait_ge(wm_land[f % 4], 16 * (f // 4 + 1))
                for k in range(KD):
                    last = nc.tensor.matmul(mod_ps[:, 2 * f:2 * f + 2], wm[:, f % 4, k * P:(k + 1) * P],
                                            silu_c[:, k, :], start=(k == 0), stop=(k == KD - 1))
                last.then_inc(wm_used, 1)
            pe.wait_ge(id_done, 1)
            for n, (g, k) in enumerate(order):
                pe.wait_ge(xn_done, 2 + groups[g][0] + groups[g][1] if g < 2 else 2)
                if n >= 4:
                    pe.wait_ge(val_done, n - 3)
                for j in range(groups[g][1]):
                    last = nc.tensor.transpose(tr_ps[:, n % 4, j * P:(j + 1) * P],
                                               x_in[:, groups[g][0] + j, k * P:(k + 1) * P], ident[:])
                last.then_inc(tr_done, 1)


class WeightRing:

    def __init__(self, nc, sem, stack, name, width=D, raws=2):
        sb, _ = memory(nc, stack)
        self.nc, self.raws = nc, raws
        self.raw = sb(f"{name}_raw", [P, raws, width])
        self.hi = sb(f"{name}_hi", [P, 2, width], F32R)
        self.lo = sb(f"{name}_lo", [P, 2, width], F32R)
        self.landed = [sem(f"{name}_landed{b}") for b in range(2)]
        self.hi_made, self.lo_made, self.used = sem(f"{name}_hi_made"), sem(f"{name}_lo_made"), sem(f"{name}_used")

    def load(self, sp, src, t, b):
        sp.wait_ge(self.lo_made, t + 3 - self.raws)
        sp.dma_start(self.raw[:, b % self.raws, :], src).then_inc(self.landed[b], 16)

    def split_hi(self, act, t, b, turn):
        act.wait_ge(self.landed[b], turn * 16 + 16)
        act.wait_ge(self.used, t + 1)
        self.nc.scalar.activation(self.hi[:, b, :], self.raw[:, b % self.raws, :], ACT.Copy).then_inc(self.hi_made, 1)

    def split_lo(self, pool, t, b):
        pool.wait_ge(self.hi_made, t + 1)
        self.nc.gpsimd.tensor_tensor(self.lo[:, b, :], self.raw[:, b % self.raws, :], self.hi[:, b, :].bitcast(F32),
                                     ALU.subtract).then_inc(self.lo_made, 1)

    def wait(self, pe, t):
        pe.wait_ge(self.lo_made, t + 3)

    def products(self, b, hi, lo, outs, at=0, tiles=KD):
        for k in range(tiles):
            for w, h in ((self.hi, hi), (self.hi, lo), (self.lo, hi)):
                for out, a, e in outs:
                    first, end = k == 0 and w is self.hi and h is hi, k == tiles - 1 and w is self.lo
                    last = self.nc.tensor.matmul(out, w[:, b, at + k * P:at + (k + 1) * P], h[:, k, a:e],
                                                 start=first, stop=end)
        return last


def project(nc, sem, io, keep, stack):
    sb, ps = memory(nc, stack)
    ring = WeightRing(nc, sem, stack, "in")
    out_ps = ps("in_ps", [P, 2, 3 * 512])
    stage = sb("lat_stage", [P, 2, NTOK])
    drained, staged, h_out = sem("in_drained"), sem("lat_staged"), sem("h_out")
    sent = [sem(f"lat_sent{b}") for b in range(2)]

    def send(act, t, n):
        if T_R <= t < T_QL:
            return n
        act.wait_ge(staged, n + 1)
        dst, e = (io["lat"][t - T_KV], NTOK) if t < T_R else (io["ql"][t - T_QL], SEQ)
        act.dma_start(dst, stage[:, n % 2, 0:e]).then_inc(sent[n % 2], 16)
        return n + 1

    with nc.Block() as block:
        @block.sync
        def _(sp):
            for part, h in enumerate((keep.h_hi, keep.h_lo)):
                sp.dma_start(io["h"][part], h[:, :, 0:SEQ].bitcast(F32)).then_inc(h_out, 16)
            with sp.Fori(0, T_F // 2) as i:
                for b in range(2):
                    ring.load(sp, io["w_in"][i * 2 + b, :, :], i * 2 + b, b)
            ring.load(sp, io["w_in"][T_F - 1, :, :], T_F - 1, 0)
            sp.wait_ge(h_out, 32)

        @block.scalar
        def _(act):
            with act.Fori(0, T_KV // 2) as i:
                for b in range(2):
                    ring.split_hi(act, i * 2 + b, b, i)
            n = 0
            for t in range(T_KV, T_F):
                ring.split_hi(act, t, t % 2, t // 2)
                if t >= T_KV + 2:
                    n = send(act, t - 2, n)
            for t in (T_F - 2, T_F - 1):
                n = send(act, t, n)
            for b in range(2):
                act.wait_ge(sent[b], 16 * ((n + 1 - b) // 2))

        @block.gpsimd
        def _(pool):
            pool.sem_inc(ring.lo_made, 2)
            with pool.Fori(0, T_KV // 2) as i:
                for b in range(2):
                    ring.split_lo(pool, i * 2 + b, b)
            for t in range(T_KV, T_F):
                ring.split_lo(pool, t, t % 2)

        @block.tensor
        def _(pe):
            pe.sem_inc(ring.used, 2)

            def tile(t, b, end):
                ring.wait(pe, t)
                pe.wait_ge(drained, t + 1)
                outs = [(out_ps[:, b, a:min(a + 512, end)], a, min(a + 512, end)) for a in range(0, end, 512)]
                ring.products(b, keep.h_hi, keep.h_lo, outs).then_inc(ring.used, 1)

            for first, end, tokens in ((T_K, T_R, NTOK), (T_R, T_F - 1, SEQ)):
                with pe.Fori(first // 2, end // 2) as i:
                    for b in range(2):
                        tile(i * 2 + b, b, tokens)
            tile(T_F - 1, 0, SEQ)

        @block.vector
        def _(dve):
            dve.sem_inc(drained, 2)

            def drain(t, b, end, dst):
                dve.wait_ge(ring.used, t + 3)
                nc.vector.tensor_copy(dst, out_ps[:, b, 0:end]).then_inc(drained, 1)

            def row(store, i):
                return store[:, bass.ds(i, 1), :].rearrange("p a t -> p (a t)")

            with dve.Fori(0, T_KV // 2) as i:
                for b in range(2):
                    drain(i * 2 + b, b, NTOK, row(keep.rk, i * 2 + b))
            n = 0
            for t in range(T_KV, T_F):
                if T_R <= t < T_QL:
                    drain(t, t % 2, SEQ, keep.r[:, t - T_R, :])
                    continue
                if n >= 2:
                    dve.wait_ge(sent[n % 2], 16 * (n // 2))
                end = NTOK if t < T_R else SEQ
                dve.wait_ge(ring.used, t + 3)
                nc.vector.tensor_copy(stage[:, n % 2, 0:end], out_ps[:, t % 2, 0:end]).then_inc(drained, 1)
                dve.wait_ge(drained, t + 3)
                dve.sem_inc(staged, 1)
                n += 1


def prepare_rwkv(nc, sem, io, keep, stack):
    sb, ps = memory(nc, stack)
    sq = sb("kk_sq", [P, NTOK])
    root = sb("kk_root", [P, NTOK])
    norm_ps = ps("kk_ps", [P, 3 * 512])
    work = sb("mask_work", [P, 2, P])
    rk, kk, cols = keep.rk, keep.kk, keep.cols
    sq_done, norm_mm, root_done, kk_done = sem("kk_sq_done"), sem("kk_mm"), sem("kk_root_done"), sem("kk_done")
    ones_done, up_in = sem("block_ones_done"), sem("up_in")
    pool_link, dve_link, act_link = sem("prep_pool"), sem("prep_dve"), sem("prep_act")
    with nc.Block() as block:
        @block.sync
        def _(sp):
            sp.dma_start(keep.up[:], io["up"]).then_inc(up_in, 16)
            sp.wait_ge(up_in, 16)

        @block.gpsimd
        def _(pool):
            link = Link(pool_link, pool)
            nc.gpsimd.memset(keep.ones[:], 1.0)
            nc.gpsimd.memset(keep.state[:], 0.0)
            for s in range(2):
                nc.gpsimd.memset(keep.bkz[s][:], 0.0)
                for buf in (keep.nt[s], keep.bt[s], keep.dt[s], keep.et[s], keep.x1t[s], *keep.wp[s]):
                    link(nc.gpsimd.memset(buf[:], 0.0))
                for buf in (keep.x1t[s], *keep.wp[s]):
                    nc.gpsimd.affine_select(out=buf[:], in_=buf[:], compare_op=ALU.not_equal, fill=1.0, base=0,
                                            pattern=[[0, 4], [-1, P]], channel_multiplier=1)

            def mask(dst, cuts, view):
                for d in range(2):
                    w = work[:, d, :]
                    link(nc.gpsimd.memset(w, 0.0))
                    part = view(w, d)
                    link(nc.gpsimd.memset(part, 1.0))
                    for base, pattern, mult in cuts[d]:
                        link(nc.gpsimd.affine_select(out=part, in_=part, compare_op=ALU.is_ge, fill=0.0, base=base,
                                                     pattern=pattern, channel_multiplier=mult))
                    for e in range(2):
                        link(nc.gpsimd.tensor_copy(dst[:, 2 * d + e, :], w))

            whole = lambda w, d: w
            mask(keep.m_strict, [[(-1, [[1, P]], -1)], [(-1, [[-1, P]], 1)]], whole)
            mask(keep.m_incl, [[(0, [[1, P]], -1)], [(0, [[-1, P]], 1)]], whole)
            for j in range(7):
                half = 1 << j
                n = P // (2 * half)

                def halves(w, d, second):
                    return w.rearrange("p (n two h) -> p n two h", two=2, h=half)[:, :, second, :]

                first_rows = [(0, [[-2 * half, n], [0, half]], 1), (half - 1, [[2 * half, n], [0, half]], -1)]
                second_rows = [(-half, [[-2 * half, n], [0, half]], 1), (2 * half - 1, [[2 * half, n], [0, half]], -1)]
                flip = j == 0
                rows = [first_rows, second_rows] if flip else [second_rows, first_rows]
                mask(keep.m_level[j], rows, lambda w, d: halves(w, d, (1 - d) if flip else d))

        @block.scalar
        def _(act):
            link = Link(act_link, act)
            link(nc.scalar.activation(rk[:, T_WD, :], rk[:, T_WD, :], ACT.Tanh))
            for p in range(PAIRS):
                if p:
                    act.wait_ge(norm_mm, p)
                nc.scalar.activation(sq[:], rk[:, T_K + p, :], ACT.Square,
                                     scale=cols[:, COL["k_k"] + p:COL["k_k"] + p + 1]).then_inc(sq_done, 1)
                act.wait_ge(norm_mm, p + 1)
                if p:
                    act.wait_ge(kk_done, p)
                nc.scalar.activation(root[:], norm_ps[:, 0:NTOK], ACT.Sqrt, bias=keep.eps[:, 2:3]).then_inc(root_done, 1)

        @block.tensor
        def _(pe):
            pe.wait_ge(ones_done, 1)
            for p in range(PAIRS):
                pe.wait_ge(sq_done, p + 1)
                if p:
                    pe.wait_ge(root_done, p)
                for a, e in ((0, 512), (512, 1024), (1024, NTOK)):
                    last = nc.tensor.matmul(norm_ps[:, a:e], keep.head_ones[:], sq[:, a:e], start=True, stop=True)
                last.then_inc(norm_mm, 1)

        @block.vector
        def _(dve):
            link = Link(dve_link, dve)
            link(nc.vector.memset(keep.head_ones[:], 0.0))
            nc.vector.memset(keep.head_ones[0:HEAD, 0:HEAD], 1.0)
            nc.vector.memset(keep.head_ones[HEAD:P, HEAD:P], 1.0).then_inc(ones_done, 1)
            nc.vector.tensor_scalar(keep.half_w0[:], cols[:, COL["w0"]:COL["w0"] + 8], 0.5, None, ALU.mult)
            nc.vector.tensor_scalar(keep.half_a0[:], cols[:, COL["a0"]:COL["a0"] + 8], 0.5, None, ALU.mult)
            ka = cols[:, COL["k_a"]:COL["k_a"] + 4]
            nc.vector.tensor_scalar(keep.half_ka[:], ka, 0.5, None, ALU.mult)
            nc.vector.tensor_scalar(keep.rest_ka[:], ka, -0.5, 1.0, ALU.mult, ALU.add)
            nc.vector.tensor_scalar(keep.rest_ka2[:], ka, -1.0, 2.0, ALU.mult, ALU.add)
            for p in range(PAIRS):
                dve.wait_ge(root_done, p + 1)
                link(nc.vector.reciprocal(root[:], root[:]))
                nc.vector.scalar_tensor_tensor(kk[:, p, :], rk[:, T_K + p, :],
                                               cols[:, COL["k_k"] + p:COL["k_k"] + p + 1], root[:],
                                               ALU.mult, ALU.mult).then_inc(kk_done, 1)


def recurrence(nc, sem, io, keep, stack):
    sb, ps = memory(nc, stack)
    rk, kk = keep.rk, keep.kk
    bank = [ps(f"bank{s}", [P, 4, 512]) for s in range(2)]
    th = [sb(f"th{s}", [P, 4, P]) for s in range(2)]
    ell = [sb(f"ell{s}", [P, 2, P]) for s in range(2)]
    cum = [sb(f"cum{s}", [P, 2, P]) for s in range(2)]
    exc = [sb(f"exc{s}", [P, 2, P]) for s in range(2)]
    mid = [sb(f"mid{s}", [P, 2, 2]) for s in range(2)]
    e_inv = [sb(f"e_inv{s}", [P, 2, P]) for s in range(2)]
    a_e, v_st = ell, cum
    g_e = [t[:, 0:2, :] for t in th]
    h = [sb(f"h{p}", [P, 2]) for p in range(PAIRS)]
    ar = [sb(f"ar{p}", [P, 2, 2, P]) for p in range(PAIRS)]
    tok = [sb(f"tok{p}", [P, 3, 2, P]) for p in range(PAIRS)]
    xm = [sb(f"xm{s}", [P, 4, P]) for s in range(2)]
    xt = [sb(f"xt{s}", [P, 4, P]) for s in range(2)]
    z = [sb(f"z{s}", [P, 2, P]) for s in range(2)]
    p1 = [sb(f"p1_{s}", [P, 2, P]) for s in range(2)]
    u = [sb(f"u{s}", [P, 2, P]) for s in range(2)]
    bk_both = [sb(f"bk_both{s}", [P, 2, 2, P]) for s in range(2)]
    rm, y_st = p1, u
    dve_link, passed = sem("rec_dve"), sem("rec_passed")
    two = lambda name: [sem(f"{name}{s}") for s in range(2)]
    up_mm, th_done, cum_done, exp_done, bk_done, ar_done = map(two, ("up_mm", "th_done", "cum_done", "exp_done", "bk_done", "ar_done"))
    bk_mm, bk_tok, v_mm, v_tok = map(two, ("bk_mm", "bk_tok", "v_mm", "v_tok"))
    score_mm, x1t_done, masked, x_mm, x_done = map(two, ("score_mm", "x1t_done", "masked", "x_mm", "x_done"))
    w_mm, w_done, xt_mm, xt_done = map(two, ("w_mm", "w_done", "xt_mm", "xt_done"))
    z_done, p_mm, p_done, u_mm, u_done, s_mm, s_done, y_mm, y_done, y_sent = map(
        two, ("z_done", "p_mm", "p_done", "u_mm", "u_done", "s_mm", "s_done", "y_mm", "y_done", "y_sent"))
    LEVELS = range(1, 7)
    UNITS = [(d, e) for d in range(2) for e in range(2)]

    def tokens(n):
        if isinstance(n, int) and n < 2:
            return SEQ + n * P, SEQ + CTX - P - n * P
        return (n - 2) * P, SEQ - P - (n - 2) * P

    def seg(buf, i, at):
        return buf[:, i, bass.ds(at, P)]

    def wait(eng, s, value):
        if not (isinstance(value, int) and value <= 0):
            eng.wait_ge(s, value)

    class Tensor:
        def __init__(self, eng):
            self.eng = eng

        def up(self, v, p, n):
            s, pe = p % 2, self.eng
            wait(pe, masked[s], v)
            at = tokens(n)
            for m, tile in ((0, T_WD), (1, T_AD)):
                for d in range(2):
                    last = nc.tensor.matmul(bank[s][:, 3, (2 * m + d) * P:(2 * m + d + 1) * P],
                                            keep.up[:, (2 * m + d) * W + p * P:(2 * m + d) * W + (p + 1) * P],
                                            seg(rk, tile, at[d]), start=True, stop=True)
            last.then_inc(up_mm[s], 1)

        def bk_turn(self, v, p):
            s, pe = p % 2, self.eng
            wait(pe, th_done[s], v + 1)
            wait(pe, bk_done[s], v + 1)
            for i in range(2):
                for d in range(2):
                    c = (2 * i + d) * P
                    last = nc.tensor.transpose(bank[s][:, 3, c:c + P], bk_both[s][:, i, d, :], keep.ident[:])
            last.then_inc(bk_mm[s], 1)

        def v_turn(self, v, p):
            s, pe = p % 2, self.eng
            wait(pe, bk_tok[s], v + 1)
            wait(pe, ar_done[s], v + 1)
            for d in range(2):
                last = nc.tensor.transpose(bank[s][:, 3, d * P:(d + 1) * P], v_st[s][:, d, :], keep.ident[:])
            last.then_inc(v_mm[s], 1)

        def scores(self, v, p, emit):
            s, pe = p % 2, self.eng
            wait(pe, bk_done[s], v + 1)
            wait(pe, ar_done[s], v + 1)
            wait(pe, v_tok[s], v + 1)
            wait(pe, p_done[s], v)
            wait(pe, u_done[s], v)
            wait(pe, s_done[s], v)
            wait(pe, y_done[s], v - 4)
            for i, (d, e) in enumerate(UNITS):
                for j in range(2):
                    m = 2 if emit else 1
                    last = nc.tensor.matmul(bank[s][:, i, 2 * j * P:(2 * j + m) * P], keep.bkz[s][:, j, d, e, :],
                                            ar[p][:, d, 0:m, :], start=True, stop=True)
            last.then_inc(score_mm[s], 1)

        def x1_turn(self, v, p):
            s, pe = p % 2, self.eng
            wait(pe, x1t_done[s], v + 1)
            wait(pe, masked[s], v + 1)
            for i in range(4):
                last = nc.tensor.transpose(bank[s][:, 1, i * P:(i + 1) * P], keep.x1t[s][:, i, :], keep.ident[:])
            last.then_inc(x_mm[s], 1)

        def level_w(self, v, p, j):
            s, pe = p % 2, self.eng
            wait(pe, x_done[s], v * 6 + j)
            for i in range(4):
                last = nc.tensor.matmul(bank[s][:, 0, i * P:(i + 1) * P], keep.nt[s][:, i, :], xm[s][:, i, :],
                                        start=True, stop=True)
            last.then_inc(w_mm[s], 1)

        def level_x(self, v, p, j):
            s, pe = p % 2, self.eng
            wait(pe, w_done[s], v * 6 + j)
            if j > 1:
                wait(pe, xt_done[s], v * 6 + j - 1)
            xt_now = keep.x1t[s] if j == 1 else xt[s]
            if j < 6:
                for i in range(4):
                    last = nc.tensor.matmul(bank[s][:, 1, i * P:(i + 1) * P], xt_now[:, i, :],
                                            keep.wp[s][j - 1][:, i, :], start=True, stop=True)
                last.then_inc(x_mm[s], 1)
            for i in range(4):
                last = nc.tensor.matmul(bank[s][:, 2, i * P:(i + 1) * P], keep.wp[s][j - 1][:, i, :],
                                        xt_now[:, i, :], start=True, stop=True)
            last.then_inc(xt_mm[s], 1)

        def rhs(self, v, p, fronted):
            s, pe = p % 2, self.eng
            wait(pe, z_done[s], v + 1)
            wait(pe, v_tok[s], v + 1 + fronted)
            for d in range(2):
                nc.tensor.matmul(bank[s][:, 3, d * P:(d + 1) * P], ar[p][:, d, 0, :], z[s][:, d, :],
                                 start=True, stop=False, skip_group_check=True)
                for e in range(2):
                    c = d * P + e * HEAD
                    last = nc.tensor.matmul(bank[s][:, 3, c:c + HEAD], keep.bt[s][:, 2 * d + e, :],
                                            tok[p][:, 2, d, e * HEAD:(e + 1) * HEAD], start=False, stop=True,
                                            skip_group_check=True)
            last.then_inc(p_mm[s], 1)

        def solve(self, v, p):
            s, pe = p % 2, self.eng
            wait(pe, p_done[s], v + 1)
            wait(pe, xt_done[s], v * 6 + 6)
            for i, (d, e) in enumerate(UNITS):
                c = d * P + e * HEAD
                last = nc.tensor.matmul(bank[s][:, 0, c:c + HEAD], xt[s][:, i, :],
                                        p1[s][:, d, e * HEAD:(e + 1) * HEAD], start=True, stop=True)
            last.then_inc(u_mm[s], 1)

        def ends(self, v, p, emit):
            s, pe = p % 2, self.eng
            wait(pe, u_done[s], v + 1)
            for d in range(2):
                for i, src in ((0, u[s][:, d, :]), (1, tok[p][:, 2, d, :])):
                    last = nc.tensor.matmul(bank[s][:, 1, d * P:(d + 1) * P], tok[p][:, i, d, :], src,
                                            start=(i == 0), stop=(i == 1))
            last.then_inc(s_mm[s], 1)
            if not emit:
                return
            for d in range(2):
                c = d * P
                nc.tensor.matmul(bank[s][:, 2, c:c + P], z[s][:, d, :], ar[p][:, d, 1, :], start=True, stop=False,
                                 skip_group_check=True)
                for e in range(2):
                    part = slice(e * HEAD, (e + 1) * HEAD)
                    nc.tensor.matmul(bank[s][part, 2, c:c + P], u[s][:, d, part], keep.dt[s][:, 2 * d + e, :],
                                     start=False, stop=False, skip_group_check=True)
                    last = nc.tensor.matmul(bank[s][part, 2, c:c + P], tok[p][:, 2, d, part],
                                            keep.et[s][:, 2 * d + e, :], start=False, stop=True, skip_group_check=True)
            last.then_inc(y_mm[s], 1)

    class Scalar:
        def __init__(self, eng):
            self.eng = eng

        def gates(self, v, p):
            s, act = p % 2, self.eng
            wait(act, up_mm[s], v + 1)
            wait(act, bk_done[s], v)
            for m, half in ((0, keep.half_w0), (1, keep.half_a0)):
                for d in range(2):
                    i = 2 * m + d
                    last = nc.scalar.activation(th[s][:, i, :], bank[s][:, 3, i * P:(i + 1) * P], ACT.Tanh,
                                                scale=0.5, bias=half[:, d * 4 + p:d * 4 + p + 1])
            last.then_inc(th_done[s], 1)

        def exps(self, v, p):
            s, act = p % 2, self.eng
            wait(act, cum_done[s], v + 1)
            wait(act, ar_done[s], v)
            wait(act, bk_done[s], v)
            minus, plus = mid[s][:, 0, :], mid[s][:, 1, :]
            now, before, inv = ar[p][:, :, 1, :], ar[p][:, :, 0, :], e_inv[s]
            for dst, d, src, up in ((inv, 0, cum, 0), (inv, 1, exc, 1), (before, 0, exc, 1), (before, 1, cum, 0),
                                    (now, 0, cum, 1), (now, 1, exc, 0)):
                nc.scalar.activation(dst[:, d, :], src[s][:, d, :], ACT.Exp, scale=1.0 if up else -1.0,
                                     bias=(minus if up else plus)[:, d:d + 1])
            nc.scalar.activation(h[p][:], plus, ACT.Exp).then_inc(exp_done[s], 1)

        def bk(self, v, p):
            s, act = p % 2, self.eng
            wait(act, bk_mm[s], v + 1)
            nc.scalar.activation(tok[p][:, 0:2, :, :], bank[s][:, 3, :].rearrange("p (i d t) -> p i d t", i=2, d=2),
                                 ACT.Copy).then_inc(bk_tok[s], 1)

        def v(self, v, p):
            s, act = p % 2, self.eng
            wait(act, v_mm[s], v + 1)
            nc.scalar.activation(tok[p][:, 2, :, :], bank[s][:, 3, 0:2 * P].rearrange("p (d t) -> p d t", d=2),
                                 ACT.Copy).then_inc(v_tok[s], 1)

        def x(self, v, p, j):
            s, act = p % 2, self.eng
            if j < 7:
                wait(act, x_mm[s], v * 6 + j)
                nc.scalar.activation(xm[s][:], bank[s][:, 1, :].rearrange("p (u t) -> p u t", u=4),
                                     ACT.Copy).then_inc(x_done[s], 1)
            if j > 1:
                wait(act, xt_mm[s], v * 6 + j - 1)
                nc.scalar.activation(xt[s][:], bank[s][:, 2, :].rearrange("p (u t) -> p u t", u=4),
                                     ACT.Copy).then_inc(xt_done[s], 1)

        def rhs(self, v, p):
            s, act = p % 2, self.eng
            wait(act, p_mm[s], v + 1)
            nc.scalar.activation(p1[s][:], bank[s][:, 3, 0:2 * P].rearrange("p (d t) -> p d t", d=2),
                                 ACT.Copy).then_inc(p_done[s], 1)

        def solve(self, v, p):
            s, act = p % 2, self.eng
            wait(act, u_mm[s], v + 1)
            wait(act, y_sent[s], (v - 4) * 32)
            nc.scalar.activation(u[s][:], bank[s][:, 0, 0:2 * P].rearrange("p (d t) -> p d t", d=2),
                                 ACT.Copy).then_inc(u_done[s], 1)

        def y(self, v, p):
            s, act = p % 2, self.eng
            wait(act, y_mm[s], v - 3)
            nc.scalar.activation(y_st[s][:], bank[s][:, 2, 0:2 * P].rearrange("p (d t) -> p d t", d=2),
                                 ACT.Copy).then_inc(y_done[s], 1)

    class Vector:
        def __init__(self, eng, link):
            self.eng, self.link = eng, link

        def cumulate(self, v, p):
            s, dve, link = p % 2, self.eng, self.link
            wait(dve, th_done[s], v + 1)
            link(nc.vector.tensor_scalar(ell[s][:], th[s][:, 0:2, :], -0.5 * DECAY, -0.5 * DECAY, ALU.mult, ALU.add))
            for d in range(2):
                last = nc.vector.tensor_tensor_scan(cum[s][:, d, :], keep.ones[:], ell[s][:, d, :], 0.0, ALU.mult, ALU.add)
            link(last)
            nc.vector.tensor_scalar(mid[s][:, 0, :], cum[s][:, :, P - 1], -0.5, None, ALU.mult)
            nc.vector.tensor_scalar(mid[s][:, 1, :], cum[s][:, :, P - 1], 0.5, None, ALU.mult)
            nc.vector.tensor_tensor(exc[s][:], cum[s][:], ell[s][:], ALU.subtract).then_inc(cum_done[s], 1)
            link(nc.vector.tensor_scalar(g_e[s], th[s][:, 2:4, :], keep.half_ka[:, p:p + 1], keep.rest_ka[:, p:p + 1],
                                         ALU.mult, ALU.add))

        def operands(self, v, p, n):
            s, dve, link = p % 2, self.eng, self.link
            wait(dve, exp_done[s], v + 1)
            nc.vector.scalar_tensor_tensor(a_e[s][:], th[s][:, 2:4, :], 1.0, e_inv[s][:], ALU.add, ALU.mult)
            link(nc.vector.tensor_tensor(g_e[s], g_e[s], e_inv[s][:], ALU.mult))
            at = tokens(n)
            for d in range(2):
                nc.vector.scalar_tensor_tensor(bk_both[s][:, 0, d, :], seg(kk, p, at[d]), -0.5, a_e[s][:, d, :],
                                               ALU.mult, ALU.mult)
                last = nc.vector.tensor_tensor(bk_both[s][:, 1, d, :], seg(rk, T_K + p, at[d]), g_e[s][:, d, :], ALU.mult)
            link(last)
            for e in range(2):
                part = slice(e * HEAD, (e + 1) * HEAD)
                last = nc.vector.tensor_copy(keep.bkz[s][part, :, :, e, :], bk_both[s][part, :, :, :])
            last.then_inc(bk_done[s], 1)

        def scores(self, v, p, emit):
            s, dve = p % 2, self.eng
            wait(dve, score_mm[s], v + 1)
            dve.sem_inc(passed, 1)
            part = lambda j: bank[s][:, :, j * P:(j + 1) * P]
            nc.vector.copy_predicated(keep.x1t[s][:], keep.m_level[0][:], part(0)).then_inc(x1t_done[s], 1)
            kept = [(keep.nt, keep.m_strict, 0), (keep.bt, keep.m_strict, 2)]
            if emit:
                kept += [(keep.dt, keep.m_incl, 1), (keep.et, keep.m_incl, 3)]
            for dst, m, j in kept:
                last = nc.vector.copy_predicated(dst[s][:], m[:], part(j))
            last.then_inc(masked[s], 1)

        def level(self, v, p, j):
            s, dve = p % 2, self.eng
            wait(dve, w_mm[s], v * 6 + j)
            dve.sem_inc(passed, 1)
            nc.vector.copy_predicated(keep.wp[s][j - 1][:], keep.m_level[j][:],
                                      bank[s][:, 0, :].rearrange("p (u t) -> p u t", u=4)).then_inc(w_done[s], 1)

        def z(self, v, p):
            s, dve, link = p % 2, self.eng, self.link
            for d in range(2):
                last = nc.vector.tensor_scalar(z[s][:, d, :], keep.state[:, 2 * p + d, :], h[p][:, d:d + 1], None, ALU.mult)
            link(last)
            dve.sem_inc(z_done[s], 1)

        def state(self, v, p):
            s, dve, link = p % 2, self.eng, self.link
            wait(dve, s_mm[s], v + 1)
            for d in range(2):
                last = nc.vector.scalar_tensor_tensor(rm[s][:, d, :], bank[s][:, 1, d * P:(d + 1) * P], h[p][:, d:d + 1],
                                                      keep.head_ones[:], ALU.mult, ALU.mult)
            link(last)
            dve.sem_inc(s_done[s], 1)
            for d in range(2):
                last = nc.vector.scalar_tensor_tensor(keep.state[:, 2 * p + d, :], z[s][:, d, :], h[p][:, d:d + 1],
                                                      rm[s][:, d, :], ALU.mult, ALU.add)
            link(last)

    class Pool:
        def __init__(self, eng):
            self.eng = eng

        def operands(self, v, p, n):
            s, pool = p % 2, self.eng
            emit = not isinstance(n, int) or n >= 2
            wait(pool, exp_done[s], v + 1)
            at = tokens(n)
            for d in range(2):
                nc.gpsimd.tensor_tensor(ar[p][:, d, 0, :], seg(kk, p, at[d]), ar[p][:, d, 0, :], ALU.mult)
                if emit:
                    nc.gpsimd.tensor_tensor(ar[p][:, d, 1, :], seg(keep.r, p, at[d]), ar[p][:, d, 1, :], ALU.mult)
                last = nc.gpsimd.tensor_copy(v_st[s][:, d, :], seg(rk, T_V + p, at[d]))
            last.then_inc(ar_done[s], 1)

    class Sync:
        def __init__(self, eng):
            self.eng = eng

        def y(self, v, p, n):
            s, sp = p % 2, self.eng
            sp.wait_ge(y_done[s], v - 3)
            at = tokens(n)
            for d in range(2):
                sp.dma_start(io["y"][d, p, :, bass.ds(at[d], P)], y_st[s][:, d, :]).then_inc(y_sent[s], 16)

    def program(engine, eng, link=None):
        if engine == "tensor":
            t = Tensor(eng)
            front = [lambda v, p, n: t.up(v, p, n), lambda v, p, n: t.bk_turn(v, p), lambda v, p, n: t.v_turn(v, p)]
            places = [1, 3, 4]
        elif engine == "scalar":
            t = Scalar(eng)
            front = [lambda v, p, n: t.gates(v, p), lambda v, p, n: t.exps(v, p), lambda v, p, n: t.bk(v, p),
                     lambda v, p, n: t.v(v, p)]
            places = [1, 2, 3, 4]
        elif engine == "vector":
            t = Vector(eng, link)
            front = [lambda v, p, n: t.cumulate(v, p), lambda v, p, n: t.operands(v, p, n)]
            places = [1, 2]
        elif engine == "sync":
            t, front, places = Sync(eng), [], []
        else:
            t = Pool(eng)
            front = [lambda v, p, n: t.operands(v, p, n)]
            places = [2]

        def fronts(after, nxt):
            for place, step in zip(places, front):
                if place == after or after is None:
                    for v, p, n in nxt:
                        step(v, p, n)

        def half(n, sub, emit, nxt):
            v = 2 * n + sub
            pairs = (2 * sub, 2 * sub + 1)
            for p in pairs:
                if engine in ("tensor", "vector"):
                    t.scores(v, p, emit)
            for p in pairs:
                if engine == "tensor":
                    t.x1_turn(v, p)
                elif engine == "scalar":
                    t.x(v, p, 1)
            for j in LEVELS:
                for p in pairs:
                    if engine == "tensor":
                        t.level_w(v, p, j)
                    elif engine == "vector":
                        t.level(v, p, j)
                fronts(j, nxt)
                if j == 5:
                    for p in pairs:
                        if engine == "tensor":
                            t.rhs(v, p, int(bool(nxt)))
                        elif engine == "vector":
                            t.z(v, p)
                        elif engine == "scalar":
                            t.rhs(v, p)
                for p in pairs:
                    if engine == "tensor":
                        t.level_x(v, p, j)
                    elif engine == "scalar":
                        t.x(v, p, j + 1)
            for p in pairs:
                if engine in ("tensor", "scalar"):
                    t.solve(v, p)
            for p in pairs:
                if engine == "tensor":
                    t.ends(v, p, emit)
                elif engine == "vector":
                    t.state(v, p)
                elif engine == "scalar" and emit:
                    t.y(v, p)
                elif engine == "sync" and emit:
                    t.y(v, p, n)

        def chunk(n, emit, more):
            half(n, 0, emit, [(2 * n + 1, p, n) for p in (2, 3)])
            half(n, 1, emit, [(2 * n + 2, p, n + 1) for p in (0, 1)] if more else [])

        fronts(None, [(0, p, 0) for p in (0, 1)])
        chunk(0, False, True)
        chunk(1, False, True)
        with eng.Fori(0, NT - 3) as i:
            if link is not None:
                link.enter(i, chunk_links)
            chunk(i + 2, True, True)
        if link is not None:
            link.leave(NT - 3)
        chunk(NT - 1, True, False)

    chunk_links = PAIRS * 8
    with nc.Block() as block:
        @block.sync
        def _(sp):
            program("sync", sp)
            for s in range(2):
                sp.wait_ge(y_sent[s], 32 * 2 * SEQ // P)

        @block.tensor
        def _(pe):
            program("tensor", pe)

        @block.scalar
        def _(act):
            program("scalar", act)

        @block.vector
        def _(dve):
            program("vector", dve, Link(dve_link, dve))

        @block.gpsimd
        def _(pool):
            program("gpsimd", pool)


def finish_rwkv(nc, sem, io, keep, stack):
    sb, ps = memory(nc, stack)
    rk, cols = keep.rk, keep.cols
    y, bonus = sb("gn_y", [P, 2, 2, SEQ]), sb("gn_bonus", [P, 2, SEQ])
    th, work = sb("gn_th", [P, 2, SEQ]), sb("gn_work", [P, SEQ])
    sq, root = sb("gn_sq", [P, SEQ]), sb("gn_root", [P, SEQ])
    out = sb("gn_out", [P, 2, SEQ])
    a_ps, sum_ps, mean_ps = ps("gn_a", [P, 2, 1024]), ps("gn_sum", [P, 1024]), ps("gn_mean", [P, 1024])
    y_in = [sem(f"gn_in{b}") for b in range(2)]
    sent = [sem(f"gn_sent{b}") for b in range(2)]
    a_mm, th_done, work_done, bonus_mm, bonus_done = map(sem, ("gn_a_mm", "gn_th_done", "gn_work_done", "gn_bonus_mm", "gn_bonus_done"))
    y_sum, mean_mm, centred, sq_done, var_mm, root_done, out_done = map(
        sem, ("gn_y_sum", "gn_mean_mm", "gn_centred", "gn_sq_done", "gn_var_mm", "gn_root_done", "gn_out_done"))
    dve_link, act_link = sem("gn_dve"), sem("gn_act")
    col = lambda name, p: cols[:, COL[name] + p:COL[name] + p + 1]
    halves = ((0, 512), (512, SEQ))
    with nc.Block() as block:
        @block.sync
        def _(sp):
            for p in range(PAIRS):
                if p >= 2:
                    sp.wait_ge(out_done, p - 1)
                for d in range(2):
                    sp.dma_start(y[:, p % 2, d, :], io["y"][d, p]).then_inc(y_in[p % 2], 16)
            for p in range(PAIRS):
                sp.wait_ge(out_done, p + 1)
                sp.dma_start(io["branch"][1, p], out[:, p % 2, :]).then_inc(sent[p % 2], 16)
            for b in range(2):
                sp.wait_ge(sent[b], 32)

        @block.tensor
        def _(pe):
            def head_sums(dst, src):
                for a, e in halves:
                    last = nc.tensor.matmul(dst[:, a:e], keep.head_ones[:], src[:, a:e], start=True, stop=True)
                return last

            for p in range(PAIRS):
                if p:
                    pe.wait_ge(th_done, p)
                for d in range(2):
                    for a, e in halves:
                        c = (2 + d) * W + p * P
                        last = nc.tensor.matmul(a_ps[:, d, a:e], keep.up[:, c:c + P], rk[:, T_AD, a:e], start=True, stop=True)
                last.then_inc(a_mm, 1)
                pe.wait_ge(y_sum, p + 1)
                if p:
                    pe.wait_ge(root_done, p)
                head_sums(mean_ps, y[:, p % 2, 0, :]).then_inc(mean_mm, 1)
                pe.wait_ge(work_done, p + 1)
                if p:
                    pe.wait_ge(bonus_done, p)
                head_sums(sum_ps, work).then_inc(bonus_mm, 1)
                pe.wait_ge(sq_done, p + 1)
                head_sums(mean_ps, sq).then_inc(var_mm, 1)

        @block.scalar
        def _(act):
            for p in range(PAIRS):
                act.wait_ge(a_mm, p + 1)
                if p:
                    act.wait_ge(work_done, p)
                for d in range(2):
                    last = nc.scalar.activation(th[:, d, :], a_ps[:, d, :], ACT.Tanh, scale=0.5,
                                                bias=keep.half_a0[:, d * 4 + p:d * 4 + p + 1])
                last.then_inc(th_done, 1)
                act.wait_ge(centred, p + 1)
                if p:
                    act.wait_ge(var_mm, p)
                nc.scalar.activation(sq[:], y[:, p % 2, 1, :], ACT.Square).then_inc(sq_done, 1)
                act.wait_ge(var_mm, p + 1)
                if p:
                    act.wait_ge(out_done, p)
                nc.scalar.activation(root[:], mean_ps[:], ACT.Sqrt, scale=1.0 / HEAD, bias=keep.eps[:, 1:2]).then_inc(root_done, 1)

        @block.vector
        def _(dve):
            link = Link(dve_link, dve)
            for p in range(PAIRS):
                b = p % 2
                dve.wait_ge(y_in[b], 32 * (p // 2 + 1))
                link(nc.vector.tensor_tensor(y[:, b, 0, :], y[:, b, 0, :], y[:, b, 1, :], ALU.add))
                dve.sem_inc(y_sum, 1)
                if p:
                    dve.wait_ge(bonus_mm, p)
                link(nc.vector.scalar_tensor_tensor(work[:], rk[:, T_K + p, 0:SEQ], col("r_k", p), keep.r[:, p, :],
                                                    ALU.mult, ALU.mult))
                dve.wait_ge(th_done, p + 1)
                link(nc.vector.tensor_tensor(bonus[:, b, :], th[:, 0, :], th[:, 1, :], ALU.add))
                link(nc.vector.tensor_scalar(bonus[:, b, :], bonus[:, b, :], keep.half_ka[:, p:p + 1],
                                             keep.rest_ka2[:, p:p + 1], ALU.mult, ALU.add))
                nc.vector.tensor_tensor(work[:], work[:], bonus[:, b, :], ALU.mult).then_inc(work_done, 1)
                dve.wait_ge(mean_mm, p + 1)
                nc.vector.scalar_tensor_tensor(y[:, b, 1, :], mean_ps[:], -1.0 / HEAD, y[:, b, 0, :],
                                               ALU.mult, ALU.add).then_inc(centred, 1)
                dve.wait_ge(centred, p + 1)
                dve.wait_ge(bonus_mm, p + 1)
                nc.vector.tensor_tensor(bonus[:, b, :], sum_ps[:], rk[:, T_V + p, 0:SEQ], ALU.mult).then_inc(bonus_done, 1)
                dve.wait_ge(bonus_done, p + 1)
                dve.wait_ge(root_done, p + 1)
                link(nc.vector.reciprocal(root[:], root[:]))
                if p >= 2:
                    dve.wait_ge(sent[b], 16)
                link(nc.vector.scalar_tensor_tensor(out[:, b, :], y[:, b, 1, :], col("gn_g", p), root[:], ALU.mult, ALU.mult))
                nc.vector.scalar_tensor_tensor(out[:, b, :], out[:, b, :], col("gn_b", p), bonus[:, b, :],
                                               ALU.add, ALU.add).then_inc(out_done, 1)
                dve.wait_ge(out_done, p + 1)


def normalise_latents(nc, sem, io, keep, stack):
    sb, ps = memory(nc, stack)
    lat, ql = sb("lat", [P, 4, NTOK]), sb("ql", [P, 3, SEQ])
    rope = sb("rope_k", [P, 2, SEQ])
    ones, sq = sb("lat_ones", [P, P]), sb("lat_sq", [P, 3, NTOK])
    root = sb("lat_root", [P, NTOK])
    val = sb("lat_val", [P, 2, NTOK])
    kr = sb("kr_val", [P, NTOK])
    sum_ps = ps("lat_ps", [P, 3 * 512])
    land, sq_done, sum_mm, root_done, val_done, hi_done, lo_done = map(
        sem, ("lat_land", "lat_sq_done", "lat_sum_mm", "lat_root_done", "lat_val_done", "lat_hi_done", "lat_lo_done"))
    dve_link, ones_done, kr_done = sem("lat_dve"), sem("lat_ones_done"), sem("kr_done")
    parts = [(2, NTOK, KV_LORA, lat, "g_kv", keep.kvn_hi, keep.kvn_lo), (3, SEQ, Q_LORA, ql, "g_q", keep.qn_hi, keep.qn_lo)]
    items = [(i, k) for i, part in enumerate(parts) for k in range(part[0])]
    with nc.Block() as block:
        @block.sync
        def _(sp):
            for i in range(4):
                sp.dma_start(lat[:, i, :], io["lat"][i]).then_inc(land, 16)
            for i in range(3):
                sp.dma_start(ql[:, i, :], io["ql"][i]).then_inc(land, 16)
            for part, src in ((0, io["rope"][0:32, :]), (1, io["rope"][32:64, :])):
                for q in (64, 96):
                    sp.dma_start(rope[q:q + 32, part, :], src).then_inc(land, 16)
            sp.dma_start(keep.rope_q[64:P, :], io["rope"]).then_inc(land, 16)
            sp.wait_ge(land, 12 * 16)

        @block.gpsimd
        def _(pool):
            nc.gpsimd.memset(ones[:], 1.0).then_inc(ones_done, 1)
            for n, (i, k) in enumerate(items):
                _, e, _, _, _, hi, lo = parts[i]
                pool.wait_ge(hi_done, n + 1)
                nc.gpsimd.tensor_tensor(lo[:, k, 0:e], keep.kvn[:, k, :] if i == 0 else val[:, n % 2, 0:e],
                                        hi[:, k, 0:e].bitcast(F32), ALU.subtract).then_inc(lo_done, 1)

        @block.tensor
        def _(pe):
            pe.wait_ge(ones_done, 1)
            for i, (tiles, end, *_) in enumerate(parts):
                pe.wait_ge(sq_done, i + 1)
                if i:
                    pe.wait_ge(root_done, i)
                for a in range(0, end, 512):
                    e = min(a + 512, end)
                    for k in range(tiles):
                        last = nc.tensor.matmul(sum_ps[:, a:e], ones[:], sq[:, k, a:e], start=k == 0, stop=k == tiles - 1)
                last.then_inc(sum_mm, 1)

        @block.scalar
        def _(act):
            act.wait_ge(land, 12 * 16)
            for i, (tiles, end, width, src, *_) in enumerate(parts):
                if i:
                    act.wait_ge(sum_mm, i)
                last = nc.scalar.activation(sq[:, 0:tiles, 0:end], src[:, 0:tiles, 0:end], ACT.Square)
                last.then_inc(sq_done, 1)
                act.wait_ge(sum_mm, i + 1)
                if i:
                    act.wait_ge(val_done, parts[0][0])
                nc.scalar.activation(root[:, 0:end], sum_ps[:, 0:end], ACT.Sqrt, scale=1.0 / width,
                                     bias=keep.eps[:, 0:1]).then_inc(root_done, 1)
                for n, (j, k) in enumerate(items):
                    if j == i:
                        act.wait_ge(val_done, n + 1)
                        nc.scalar.activation(parts[i][5][:, k, 0:end], keep.kvn[:, k, :] if i == 0 else val[:, n % 2, 0:end],
                                             ACT.Copy).then_inc(hi_done, 1)
            act.wait_ge(kr_done, 1)
            for b in range(2):
                last = nc.scalar.activation(keep.k_hi[b][64:P, :], kr[64:P, :], ACT.Copy)
            last.then_inc(kr_done, 1)

        @block.vector
        def _(dve):
            link = Link(dve_link, dve)
            dve.wait_ge(land, 12 * 16)
            link(nc.vector.memset(keep.rope_q[0:64, :], 1.0))
            for i, (tiles, end, width, src, g, *_) in enumerate(parts):
                dve.wait_ge(root_done, i + 1)
                link(nc.vector.reciprocal(root[:, 0:end], root[:, 0:end]))
                for n, (j, k) in enumerate(items):
                    if j == i:
                        if i and n >= 4:
                            dve.wait_ge(lo_done, n - 1)
                        dst = keep.kvn[:, k, :] if i == 0 else val[:, n % 2, 0:end]
                        nc.vector.scalar_tensor_tensor(dst, src[:, k, 0:end], cols_of(keep, g, k), root[:, 0:end],
                                                       ALU.mult, ALU.mult).then_inc(val_done, 1)
                dve.wait_ge(val_done, sum(p[0] for p in parts[:i + 1]))
            low = slice(64, P)
            link(nc.vector.tensor_tensor(kr[low, 0:SEQ], lat[low, 2, 0:SEQ], rope[low, 0, :], ALU.mult))
            link(nc.vector.tensor_tensor(lat[low, 3, 0:SEQ], lat[low, 3, 0:SEQ], rope[low, 1, :], ALU.mult))
            nc.vector.tensor_copy(kr[low, SEQ:NTOK], lat[low, 2, SEQ:NTOK])
            nc.vector.tensor_tensor(kr[low, 0:SEQ], kr[low, 0:SEQ], lat[low, 3, 0:SEQ], ALU.add).then_inc(kr_done, 1)
            dve.wait_ge(kr_done, 2)
            for b in range(2):
                last = nc.vector.tensor_tensor(keep.k_lo[b][low, :], kr[low, :], keep.k_hi[b][low, :].bitcast(F32), ALU.subtract)
            link(last)


def cols_of(keep, name, i):
    return keep.cols[:, COL[name] + i:COL[name] + i + 1]


def attention(nc, sem, io, keep, stack):
    sb, ps = memory(nc, stack)
    NQ = SEQ // P
    raw = sb("at_raw", [P, 2, 3 * P + 2 * NOPE])
    w_hi, w_lo = sb("at_w_hi", [P, 2, 3 * P + 2 * NOPE], F32R), sb("at_w_lo", [P, 2, 3 * P + 2 * NOPE], F32R)
    uv = sb("at_uv", [P, 2 * P])
    kv_val, q_val = sb("at_k_val", [HEAD, NTOK]), sb("at_q_val", [P, SEQ])
    q_hi, q_lo = sb("q_hi", [P, SEQ], F32R), sb("q_lo", [P, SEQ], F32R)
    v_val = sb("v_val", [P, NT, P])
    v_hi, v_lo = sb("v_hi", [P, NT, P], F32R), sb("v_lo", [P, NT, P], F32R)
    probs = sb("probs", [P, 2, NTOK])
    pt_hi, pt_lo = sb("pt_hi", [P, NT, 4 * P], F32R), sb("pt_lo", [P, NT, 4 * P], F32R)
    top, total = sb("top", [P, 2, 1]), sb("total", [P, 2, 1])
    o_sb = sb("o_sb", [P, 2, 512])
    s_ps = ps("s_ps", [P, 2, 3 * 512])
    t_ps, o_ps = ps("t_ps", [P, 512]), ps("o_ps", [P, 512])
    names = ("w_land", "w_used", "w_hi_done", "w_lo_done", "uv_land", "uv_used", "k_mm", "k_val", "k_hi", "k_lo",
             "q_mm", "q_val", "q_hi", "q_lo", "v_mm", "v_val", "v_parts", "s_mm", "top_done", "exp_done", "probs_done",
             "t_mm", "t_hi", "t_lo", "o_mm", "o_done", "o_free")
    S = {n: sem(f"at_{n}") for n in names}
    o_sent = [sem(f"at_o_sent{b}") for b in range(2)]
    dve_link = sem("at_dve")
    TURNS = [(0, 4), (4, 8), (8, NT)]
    NW = 3 * P + 2 * NOPE

    def turn_hi(act, h, q):
        for n, (a, b) in enumerate(TURNS):
            act.wait_ge(S["t_mm"], (h * 8 + q) * 3 + n + 1)
            if n == 0 and q % 4 == 0:
                act.wait_ge(S["o_mm"], h * 2 + q // 4 + 1)
            nc.scalar.activation(pt_hi[:, a:b, (q % 4) * P:(q % 4 + 1) * P],
                                 t_ps[:, 0:(b - a) * P].rearrange("p (t c) -> p t c", c=P), ACT.Copy).then_inc(S["t_hi"], 1)

    def norm(dve, link, h, q):
        dve.wait_ge(S["exp_done"], h * 8 + q + 3)
        link(nc.vector.reciprocal(total[:, q % 2, :], total[:, q % 2, :]))
        nc.vector.tensor_scalar(probs[:, q % 2, :], probs[:, q % 2, :], total[:, q % 2, :], None, ALU.mult).then_inc(S["probs_done"], 1)

    def out(dve, h, p, e, half):
        dve.wait_ge(S["o_mm"], h * 2 + half + 2)
        dve.wait_ge(S["o_free"], h * 2 + half + 1)
        part = slice(e * HEAD, (e + 1) * HEAD)
        nc.vector.tensor_copy(o_sb[part, half, :], o_ps[part, :]).then_inc(S["o_done"], 1)

    with nc.Block() as block:
        @block.sync
        def _(sp):
            with sp.Fori(0, PAIRS) as p:
                sp.wait_ge(S["uv_used"], p + 1)
                sp.dma_start(uv[:], io["uv"][bass.ds(p, 1)].rearrange("a p n -> p (a n)")).then_inc(S["uv_land"], 16)
                for e in range(2):
                    h = p * 2 + e
                    sp.wait_ge(S["w_lo_done"], h + 1)
                    sp.dma_start(raw[:, e, 0:3 * P], io["uq"][bass.ds(h, 1)].rearrange("a p n -> p (a n)")).then_inc(S["w_land"], 16)
                    sp.dma_start(raw[:, e, 3 * P:NW], io["uk"][bass.ds(h, 1)].rearrange("a p n -> p (a n)")).then_inc(S["w_land"], 16)

        @block.gpsimd
        def _(pool):
            pool.sem_inc(S["w_lo_done"], 1)
            pool.sem_inc(S["v_parts"], 1)
            pool.sem_inc(S["o_free"], 2)
            with pool.Fori(0, PAIRS) as p:
                for e in range(2):
                    h = p * 2 + e
                    pool.wait_ge(S["w_hi_done"], h + 1)
                    nc.gpsimd.tensor_tensor(w_lo[:, e, :], raw[:, e, :], w_hi[:, e, :].bitcast(F32), ALU.subtract).then_inc(S["w_lo_done"], 1)
                    if e == 0:
                        pool.wait_ge(S["v_val"], p * 2 + 2)
                        nc.gpsimd.tensor_tensor(v_lo[:], v_val[:], v_hi[:].bitcast(F32), ALU.subtract).then_inc(S["v_parts"], 1)
                    pool.wait_ge(S["k_hi"], h + 1)
                    nc.gpsimd.tensor_tensor(keep.k_lo[e][0:HEAD, :], kv_val[:], keep.k_hi[e][0:HEAD, :].bitcast(F32),
                                            ALU.subtract).then_inc(S["k_lo"], 1)
                    pool.wait_ge(S["q_hi"], h + 1)
                    nc.gpsimd.tensor_tensor(q_lo[:], q_val[:], q_hi[:].bitcast(F32), ALU.subtract).then_inc(S["q_lo"], 1)
                    for q in range(2):
                        pool.wait_ge(S["o_done"], h * 2 + q + 2)
                        pool.dma_start(io["branch"][0, p, e * HEAD:(e + 1) * HEAD, q * 512:(q + 1) * 512],
                                       o_sb[e * HEAD:(e + 1) * HEAD, q, :]).then_inc(o_sent[q], 16)
                    for q in range(2):
                        pool.wait_ge(o_sent[q], h * 16 + 16)
                        pool.sem_inc(S["o_free"], 1)

        @block.tensor
        def _(pe):
            pe.sem_inc(S["uv_used"], 1)
            pe.sem_inc(S["o_mm"], 1)

            def passes(out, ws, hs, first, end):
                for n, (w, x) in enumerate(((ws[0], hs[0]), (ws[0], hs[1]), (ws[1], hs[0]))):
                    last = nc.tensor.matmul(out, w, x, start=first and n == 0, stop=end and n == 2)
                return last

            with pe.Fori(0, PAIRS) as p:
                pe.wait_ge(S["uv_land"], p * 16 + 16)
                for half in range(2):
                    pe.wait_ge(S["exp_done"], p * 16 + 2)
                    for t in range(5 * half, 5 * half + 5):
                        c = (t - 5 * half) * P
                        for k in range(2):
                            last = nc.tensor.matmul(s_ps[:, half, c:c + P], keep.kvn[:, k, t * P:(t + 1) * P],
                                                    uv[:, k * P:(k + 1) * P], start=k == 0, stop=k == 1)
                    last.then_inc(S["v_mm"], 1)
                pe.wait_ge(S["v_mm"], p * 2 + 2)
                pe.sem_inc(S["uv_used"], 1)
                for e in range(2):
                    h = p * 2 + e
                    pe.wait_ge(S["w_lo_done"], h + 2)
                    if e == 0:
                        pe.wait_ge(S["v_val"], p * 2 + 2)
                    pe.wait_ge(S["exp_done"], h * 8 + 2)
                    for a in range(0, NTOK, 512):
                        b = min(a + 512, NTOK)
                        for k in range(2):
                            c = 3 * P + k * NOPE
                            last = passes(s_ps[0:HEAD, 0, a:b], (w_hi[:, e, c:c + NOPE], w_lo[:, e, c:c + NOPE]),
                                          (keep.kvn_hi[:, k, a:b], keep.kvn_lo[:, k, a:b]), k == 0, k == 1)
                    last.then_inc(S["k_mm"], 1)
                    for a in (0, 512):
                        for k in range(3):
                            last = passes(s_ps[:, 1, a:a + 512], (w_hi[:, e, k * P:(k + 1) * P], w_lo[:, e, k * P:(k + 1) * P]),
                                          (keep.qn_hi[:, k, a:a + 512], keep.qn_lo[:, k, a:a + 512]), k == 0, k == 2)
                    last.then_inc(S["q_mm"], 1)
                    pe.wait_ge(S["k_lo"], h + 1)
                    pe.wait_ge(S["q_lo"], h + 1)

                    def scores(q):
                        if q < 2:
                            pe.wait_ge(S["k_val"] if q == 0 else S["q_val"], h + 1)
                        else:
                            pe.wait_ge(S["exp_done"], h * 8 + q + 1)
                        for a in range(0, NTOK, 512):
                            b = min(a + 512, NTOK)
                            c = q * P
                            last = passes(s_ps[:, q % 2, a:b], (q_hi[:, c:c + P], q_lo[:, c:c + P]),
                                          (keep.k_hi[e][:, a:b], keep.k_lo[e][:, a:b]), True, True)
                        last.then_inc(S["s_mm"], 1)

                    scores(0)
                    for q in range(NQ):
                        if q + 1 < NQ:
                            scores(q + 1)
                        pe.wait_ge(S["probs_done"], h * 8 + q + 1)
                        for n, (a, b) in enumerate(TURNS):
                            pe.wait_ge(S["t_lo"], (h * 8 + q) * 3 + n + 1)
                            for t in range(a, b):
                                last = nc.tensor.transpose(t_ps[:, (t - a) * P:(t - a + 1) * P],
                                                           probs[:, q % 2, t * P:(t + 1) * P], keep.ident[:])
                            last.then_inc(S["t_mm"], 1)
                        if q % 4 == 3:
                            pe.wait_ge(S["t_lo"], (h * 8 + q) * 3 + 4)
                            if e == 0:
                                pe.wait_ge(S["v_parts"], p + 2)
                            pe.wait_ge(S["o_done"], h * 2 + q // 4 + 1)
                            for t in range(NT):
                                last = passes(o_ps[:], (v_hi[:, t, :], v_lo[:, t, :]), (pt_hi[:, t, :], pt_lo[:, t, :]),
                                              t == 0, t == NT - 1)
                            last.then_inc(S["o_mm"], 1)

        @block.scalar
        def _(act):
            act.sem_inc(S["exp_done"], 2)
            with act.Fori(0, PAIRS) as p:
                for e in range(2):
                    h = p * 2 + e
                    act.wait_ge(S["w_land"], h * 32 + 32)
                    nc.scalar.activation(w_hi[:, e, :], raw[:, e, :], ACT.Copy).then_inc(S["w_hi_done"], 1)
                    if e == 0:
                        for half in range(2):
                            act.wait_ge(S["v_mm"], p * 2 + half + 1)
                            if half == 0:
                                act.wait_ge(S["v_parts"], p + 1)
                            src = s_ps[:, half, 0:5 * P].rearrange("p (t c) -> p t c", t=5)
                            nc.scalar.activation(v_hi[:, 5 * half:5 * half + 5, :], src, ACT.Copy)
                            nc.scalar.activation(v_val[:, 5 * half:5 * half + 5, :], src, ACT.Copy).then_inc(S["v_val"], 1)
                    act.wait_ge(S["k_mm"], h + 1)
                    nc.scalar.activation(kv_val[:], s_ps[0:HEAD, 0, 0:NTOK], ACT.Copy)
                    nc.scalar.activation(keep.k_hi[e][0:HEAD, :], s_ps[0:HEAD, 0, 0:NTOK], ACT.Copy).then_inc(S["k_hi"], 1)
                    act.wait_ge(S["k_hi"], h + 1)
                    act.sem_inc(S["k_val"], 1)
                    act.wait_ge(S["q_val"], h + 1)
                    nc.scalar.activation(q_hi[:], q_val[:], ACT.Copy).then_inc(S["q_hi"], 1)
                    for q in range(NQ):
                        n = h * 8 + q
                        act.wait_ge(S["top_done"], n + 1)
                        nc.scalar.activation(probs[:, q % 2, :], s_ps[:, q % 2, 0:NTOK], ACT.Exp, scale=SCALE,
                                             bias=top[:, q % 2, :], accum_out=total[:, q % 2, :]).then_inc(S["exp_done"], 1)
                        if q:
                            turn_hi(act, h, q - 1)
                    turn_hi(act, h, NQ - 1)

        @block.vector
        def _(dve):
            link = Link(dve_link, dve)
            dve.sem_inc(S["t_lo"], 1)
            dve.sem_inc(S["o_done"], 1)

            def turn_lo(h, q):
                for n, (a, b) in enumerate(TURNS):
                    dve.wait_ge(S["t_hi"], (h * 8 + q) * 3 + n + 1)
                    part = (slice(None), slice(a, b), slice((q % 4) * P, (q % 4 + 1) * P))
                    nc.vector.tensor_tensor(pt_lo[part], t_ps[:, 0:(b - a) * P].rearrange("p (t c) -> p t c", c=P),
                                            pt_hi[part].bitcast(F32), ALU.subtract).then_inc(S["t_lo"], 1)

            with dve.Fori(0, PAIRS) as p:
                link.enter(p, 2 * NQ * 2)
                for e in range(2):
                    h = p * 2 + e
                    dve.wait_ge(S["q_mm"], h + 1)
                    nc.vector.tensor_tensor(q_val[:], s_ps[:, 1, 0:SEQ], keep.rope_q[:], ALU.mult).then_inc(S["q_val"], 1)
                    for q in range(NQ):
                        n = h * 8 + q
                        dve.wait_ge(S["s_mm"], n + 1)
                        link(nc.vector.reduce_max(top[:, q % 2, :], s_ps[:, q % 2, 0:NTOK], AX.X))
                        nc.vector.tensor_scalar(top[:, q % 2, :], top[:, q % 2, :], -SCALE, None, ALU.mult).then_inc(S["top_done"], 1)
                        if q:
                            norm(dve, link, h, q - 1)
                            turn_lo(h, q - 1)
                            if q == 4:
                                out(dve, h, p, e, 0)
                    norm(dve, link, h, NQ - 1)
                    turn_lo(h, NQ - 1)
                    out(dve, h, p, e, 1)
            link.leave(PAIRS)


def gate_branches(nc, sem, io, keep, stack):
    sb, ps = memory(nc, stack)
    ring = WeightRing(nc, sem, stack, "gb")
    out_ps = ps("gb_ps", [P, 3, 1024])
    pad = sb("conv_u", [P, SEQ + 2])
    conv = sb("conv_sum", [P, SEQ])
    th, val = sb("gate_th", [P, SEQ]), sb("gate_val", [P, SEQ])
    y = sb("branch_y", [P, SEQ])
    cols = keep.cols
    S = {n: sem(f"gb_{n}") for n in ("h_in", "drained", "in_done", "th_done", "val_done", "hi_done", "lo_done",
                                     "link", "y_used", "y_in")}
    IN, C, B, GATES = 0, 1, 2, (3, 4, 5)
    ORDER = (1, 0, 2)
    def lo_part(pool, c, g):
        hi, lo = keep.branch[ORDER[g]]
        pool.wait_ge(S["hi_done"], c * 3 + g + 1)
        at = (slice(None), bass.ds(c, 1), slice(None))
        nc.gpsimd.tensor_tensor(lo[at].rearrange("p a t -> p (a t)"), val[:],
                                hi[at].rearrange("p a t -> p (a t)").bitcast(F32), ALU.subtract).then_inc(S["lo_done"], 1)

    def evacuate(act, c, t):
        if t == IN:
            act.wait_ge(ring.used, c * 6 + t + 3)
            act.wait_ge(S["val_done"], c * 3 + 1)
            nc.scalar.activation(th[:], out_ps[:, t % 3, :], ACT.Copy).then_inc(S["in_done"], 1)
        if t in GATES:
            g = t - 3
            act.wait_ge(ring.used, c * 6 + t + 3)
            if g:
                act.wait_ge(S["val_done"], c * 3 + g + 1)
            else:
                act.wait_ge(S["drained"], c * 6 + 5)
            nc.scalar.activation(th[:], out_ps[:, t % 3, :], ACT.Tanh, scale=0.5).then_inc(S["th_done"], 1)
            act.wait_ge(S["val_done"], c * 3 + g + 2)
            hi = keep.branch[ORDER[g]][0]
            nc.scalar.activation(hi[:, bass.ds(c, 1), :].rearrange("p a t -> p (a t)"), val[:],
                                 ACT.Copy).then_inc(S["hi_done"], 1)

    with nc.Block() as block:
        @block.sync
        def _(sp):
            for part, h in enumerate((keep.h_hi, keep.h_lo)):
                sp.dma_start(h[:].bitcast(F32), io["h"][part]).then_inc(S["h_in"], 16)
            with sp.Fori(0, PAIRS) as c:
                for t in range(6):
                    ring.load(sp, io["w_in"][c * 6 + (T_F + t), :, :], c * 6 + t, t % 2)
                    if t in (2, 5):
                        b = t // 3
                        sp.wait_ge(S["y_used"], c * 2 + b + 1)
                        sp.dma_start(y[:], io["branch"][b, bass.ds(c, 1)].rearrange("a p t -> p (a t)")).then_inc(S["y_in"], 16)

        @block.gpsimd
        def _(pool):
            pool.sem_inc(ring.lo_made, 2)
            pool.sem_inc(S["lo_done"], 1)
            with pool.Fori(0, PAIRS) as c:
                for t in range(6):
                    ring.split_lo(pool, c * 6 + t, t % 2)
                    if t in GATES:
                        lo_part(pool, c, t - 3)

        @block.tensor
        def _(pe):
            pe.sem_inc(ring.used, 2)
            pe.wait_ge(S["h_in"], 32)
            with pe.Fori(0, PAIRS) as c:
                for t in range(6):
                    ring.wait(pe, c * 6 + t)
                    pe.wait_ge(S["drained"], c * 6 + t + 1)
                    outs = [(out_ps[:, t % 3, a:a + 512], a, a + 512) for a in (0, 512)]
                    ring.products(t % 2, keep.h_hi, keep.h_lo, outs).then_inc(ring.used, 1)

        @block.scalar
        def _(act):
            with act.Fori(0, PAIRS) as c:
                for t in range(6):
                    ring.split_hi(act, c * 6 + t, t % 2, c * 3 + t // 2)
                    if t >= 1:
                        evacuate(act, c, t - 1)
                evacuate(act, c, 5)

        @block.vector
        def _(dve):
            link = Link(S["link"], dve)
            dve.sem_inc(S["drained"], 3)
            dve.sem_inc(S["val_done"], 1)
            dve.sem_inc(S["y_used"], 1)
            link(nc.vector.memset(pad[:], 0.0))
            with dve.Fori(0, PAIRS) as c:
                link.enter(c, 8)
                col = lambda name, i=0: cols[:, bass.ds(c + (COL[name] + i), 1)]
                dve.wait_ge(S["in_done"], c + 1)
                dve.sem_inc(S["drained"], 1)
                dve.wait_ge(ring.used, c * 6 + C + 3)
                link(nc.vector.tensor_tensor(pad[:, 1:SEQ + 1], out_ps[:, C % 3, :], th[:], ALU.mult))
                dve.sem_inc(S["drained"], 1)
                link(nc.vector.tensor_scalar(conv[:], pad[:, 0:SEQ], col("conv_w"), col("conv_b"), ALU.mult, ALU.add))
                link(nc.vector.scalar_tensor_tensor(conv[:], pad[:, 1:SEQ + 1], col("conv_w", 4), conv[:], ALU.mult, ALU.add))
                link(nc.vector.scalar_tensor_tensor(conv[:], pad[:, 2:SEQ + 2], col("conv_w", 8), conv[:], ALU.mult, ALU.add))
                dve.wait_ge(ring.used, c * 6 + B + 3)
                link(nc.vector.tensor_tensor(conv[:], out_ps[:, B % 3, :], conv[:], ALU.mult))
                dve.sem_inc(S["drained"], 1)
                for g in range(3):
                    t = 3 + g
                    dve.wait_ge(S["th_done"], c * 3 + g + 1)
                    link(nc.vector.scalar_tensor_tensor(th[:], th[:], 1.0, out_ps[:, t % 3, :], ALU.add, ALU.mult))
                    dve.sem_inc(S["drained"], 1)
                    dve.wait_ge(S["lo_done"], c * 3 + g + 1)
                    src = conv if g == 0 else y
                    if g:
                        dve.wait_ge(S["y_in"], c * 32 + g * 16)
                    nc.vector.scalar_tensor_tensor(val[:], src[:], 0.5, th[:], ALU.mult, ALU.mult).then_inc(S["val_done"], 1)
                    dve.wait_ge(S["val_done"], c * 3 + g + 2)
                    if g:
                        dve.sem_inc(S["y_used"], 1)
            link.leave(PAIRS)


def merge(nc, sem, io, keep, stack):
    sb, ps = memory(nc, stack)
    ring = WeightRing(nc, sem, stack, "mg", D + W, raws=1)
    out_ps = ps("mg_ps", [P, 2, 2, 1024])
    th, term = sb("mg_th", [P, 2, SEQ]), sb("mg_term", [P, SEQ])
    acc = sb("mg_acc", [P, SEQ])
    S = {n: sem(f"mg_{n}") for n in ("th_done", "drained", "link", "acc_done", "summed")}
    sent = sem("mg_sent")
    TILES = 6
    def gate(act, i, t):
        act.wait_ge(ring.used, i * TILES + t + 3)
        act.wait_ge(S["drained"], i * TILES + t + 1)
        nc.scalar.activation(th[:, t % 2, :], out_ps[:, t % 2, 0, :], ACT.Tanh, scale=0.5).then_inc(S["th_done"], 1)

    def store(act, i, b):
        act.wait_ge(S["acc_done"], i * 2 + b + 1)
        act.dma_start(io["merged"][bass.ds(i * 2 + b, 1)].rearrange("a p t -> p (a t)"), acc[:]).then_inc(sent, 16)

    with nc.Block() as block:
        @block.sync
        def _(sp):
            with sp.Fori(0, KD // 2) as i:
                for t in range(TILES):
                    ring.load(sp, io["w_merge"][i * TILES + t, :, :], i * TILES + t, t % 2)

        @block.gpsimd
        def _(pool):
            pool.sem_inc(ring.lo_made, 2)
            with pool.Fori(0, KD // 2) as i:
                for t in range(TILES):
                    ring.split_lo(pool, i * TILES + t, t % 2)

        @block.tensor
        def _(pe):
            pe.sem_inc(ring.used, 2)
            with pe.Fori(0, KD // 2) as i:
                for t in range(TILES):
                    ring.wait(pe, i * TILES + t)
                    pe.wait_ge(S["drained"], i * TILES + t + 1)
                    b = t % 2
                    outs = lambda j: [(out_ps[:, b, j, a:a + 512], a, a + 512) for a in (0, 512)]
                    ring.products(b, keep.h_hi, keep.h_lo, outs(0))
                    ring.products(b, *keep.branch[t % 3], outs(1), at=D, tiles=PAIRS).then_inc(ring.used, 1)

        @block.scalar
        def _(act):
            act.sem_inc(sent, 16)
            with act.Fori(0, KD // 2) as i:
                for t in range(TILES):
                    ring.split_hi(act, i * TILES + t, t % 2, i * 3 + t // 2)
                    if t:
                        gate(act, i, t - 1)
                    if t == 4:
                        store(act, i, 0)
                gate(act, i, TILES - 1)
                store(act, i, 1)
            act.wait_ge(sent, 16 + 16 * KD)

        @block.vector
        def _(dve):
            link = Link(S["link"], dve)
            dve.sem_inc(S["drained"], 2)
            with dve.Fori(0, KD // 2) as i:
                link.enter(i, 6)
                for t in range(TILES):
                    b = t // 3
                    dve.wait_ge(S["th_done"], i * TILES + t + 1)
                    if t % 3 == 0:
                        dve.wait_ge(sent, (i * 2 + b) * 16 + 16)
                    dst = term[:] if t % 3 else acc[:]
                    link(nc.vector.scalar_tensor_tensor(dst, th[:, t % 2, :], 1.0, out_ps[:, t % 2, 1, :],
                                                        ALU.add, ALU.mult))
                    dve.sem_inc(S["drained"], 1)
                    if t % 3:
                        last = nc.vector.tensor_tensor(acc[:], acc[:], term[:], ALU.add)
                        if t % 3 == 2:
                            last.then_inc(S["acc_done"], 1)
                            dve.wait_ge(S["acc_done"], i * 2 + b + 1)
                        else:
                            last.then_inc(S["summed"], 1)
                            dve.wait_ge(S["summed"], i * 2 + b + 1)
            link.leave(KD // 2)


def project_out(nc, sem, io, keep, stack):
    sb, ps = memory(nc, stack)
    raw = sb("po_raw", [P, 2, D])
    w_hi, w_lo = sb("po_w_hi", [P, KD, D], F32R), sb("po_w_lo", [P, KD, D], F32R)
    m_hi, m_lo = sb("po_m_hi", [P, KD, SEQ], F32R), sb("po_m_lo", [P, KD, SEQ], F32R)
    gate = sb("po_gate", [P, D])
    wide = sb("po_silu", [P, KD, P])
    res, x_in, junk = sb("po_res", [P, 2, D]), sb("po_x", [P, 2, D]), sb("po_junk", [P, D])
    rows = sb("po_rows", [P, 2, D])
    ss = sb("po_ss", [P, 2, 2])
    out_ps = ps("po_ps", [P, 3, 1024])
    gate_ps = ps("po_gate_ps", [P, 1024])
    S = {n: sem(f"po_{n}") for n in ("hi_done", "lo_done", "rows_in", "wide_done", "mm", "sq_done", "root_done",
                                     "res_done", "link", "gate_used")}
    land = [sem(f"po_land{b}") for b in range(2)]
    x_land = [sem(f"po_x_land{b}") for b in range(2)]
    sent = [sem(f"po_sent{b}") for b in range(2)]
    items = [(kind, k) for k in range(KD) for kind in ("w", "m")]
    NQ = SEQ // P
    with nc.Block() as block:
        @block.sync
        def _(sp):
            for part, row in enumerate((io["bm_gate"], io["g_post"])):
                sp.dma_start(rows[:, part, :], row[0:1, :].broadcast_to([P, D])).then_inc(S["rows_in"], 16)
            for n in range(KD + len(items)):
                if n >= 2:
                    if n - 2 < KD:
                        sp.wait_ge(S["gate_used"], n - 1)
                    else:
                        sp.wait_ge(S["lo_done"], n - 1 - KD)
                if n < KD:
                    src = io["wm_gate"][n * P:(n + 1) * P, :]
                else:
                    kind, k = items[n - KD]
                    src = io["w_out"][k * P:(k + 1) * P, :] if kind == "w" else io["merged"][k]
                sp.dma_start(raw[:, n % 2, :], src).then_inc(land[n % 2], 16)
            for t in range(NQ):
                if t >= 2:
                    sp.wait_ge(S["res_done"], t - 1)
                sp.dma_start(x_in[:, t % 2, :], io["x"][t * P:(t + 1) * P, :]).then_inc(x_land[t % 2], 16)
            for b in range(2):
                sp.wait_ge(sent[b], 16 * NQ // 2)

        @block.gpsimd
        def _(pool):
            for n, (kind, k) in enumerate(items):
                hi, lo = (w_hi, w_lo) if kind == "w" else (m_hi, m_lo)
                pool.wait_ge(S["hi_done"], n + 1)
                nc.gpsimd.tensor_tensor(lo[:, k, :], raw[:, n % 2, :], hi[:, k, :].bitcast(F32), ALU.subtract).then_inc(S["lo_done"], 1)

        @block.scalar
        def _(act):
            for n, (kind, k) in enumerate(items):
                act.wait_ge(land[n % 2], 16 * ((n + KD) // 2 + 1))
                nc.scalar.activation((w_hi if kind == "w" else m_hi)[:, k, :], raw[:, n % 2, :], ACT.Copy).then_inc(S["hi_done"], 1)
            for t in range(NQ):
                act.wait_ge(S["mm"], t + 1)
                if t >= 2:
                    act.wait_ge(S["res_done"], t - 1)
                nc.scalar.activation(junk[:], out_ps[:, t % 3, :], ACT.Square, scale=0.5,
                                     accum_out=ss[:, t % 2, 0:1]).then_inc(S["sq_done"], 1)
                act.wait_ge(S["sq_done"], t + 1)
                nc.scalar.activation(ss[:, t % 2, 1:2], ss[:, t % 2, 0:1], ACT.Sqrt, scale=1.0 / D,
                                     bias=keep.eps[:, 0:1]).then_inc(S["root_done"], 1)
                act.wait_ge(S["res_done"], t + 1)
                act.dma_start(io["out"][t * P:(t + 1) * P, :], res[:, t % 2, :]).then_inc(sent[t % 2], 16)

        @block.tensor
        def _(pe):
            pe.wait_ge(S["wide_done"], 1)
            for k in range(KD):
                pe.wait_ge(land[k % 2], 16 * (k // 2 + 1))
                for a in (0, 512):
                    last = nc.tensor.matmul(gate_ps[:, a:a + 512], wide[:, k, :], raw[:, k % 2, a:a + 512],
                                            start=k == 0, stop=k == KD - 1)
                last.then_inc(S["gate_used"], 1)
            for t in range(NQ):
                if t >= 3:
                    pe.wait_ge(S["res_done"], t - 2)
                for k in range(KD):
                    if t == 0:
                        pe.wait_ge(S["lo_done"], 2 * k + 2)
                    for m, w in ((m_hi, w_hi), (m_hi, w_lo), (m_lo, w_hi)):
                        for a in (0, 512):
                            last = nc.tensor.matmul(out_ps[:, t % 3, a:a + 512], m[:, k, t * P:(t + 1) * P], w[:, k, a:a + 512],
                                                    start=k == 0 and m is m_hi and w is w_hi, stop=k == KD - 1 and m is m_lo)
                last.then_inc(S["mm"], 1)

        @block.vector
        def _(dve):
            link = Link(S["link"], dve)
            link(nc.vector.memset(wide[:], 1.0))
            for k in range(KD):
                last = nc.vector.tensor_scalar(wide[:, k, :], wide[:, k, :], keep.silu_c[:, k, 0:1], None, ALU.mult)
            last.then_inc(S["wide_done"], 1)
            dve.wait_ge(S["rows_in"], 32)
            dve.wait_ge(S["gate_used"], KD)
            link(nc.vector.tensor_tensor(gate[:], gate_ps[:], rows[:, 0, :], ALU.add))
            link(nc.vector.scalar_tensor_tensor(gate[:], gate[:], 0.5, rows[:, 1, :], ALU.mult, ALU.mult))
            for t in range(NQ):
                dve.wait_ge(S["root_done"], t + 1)
                link(nc.vector.reciprocal(ss[:, t % 2, 1:2], ss[:, t % 2, 1:2]))
                if t >= 2:
                    dve.wait_ge(sent[t % 2], 16 * (t // 2))
                link(nc.vector.scalar_tensor_tensor(res[:, t % 2, :], out_ps[:, t % 3, :], ss[:, t % 2, 1:2], gate[:],
                                                    ALU.mult, ALU.mult))
                dve.wait_ge(x_land[t % 2], 16 * (t // 2 + 1))
                nc.vector.tensor_tensor(res[:, t % 2, :], res[:, t % 2, :], x_in[:, t % 2, :], ALU.add).then_inc(S["res_done"], 1)


def phases(nc, io, keep):
    def run(phase, stack):
        sems = []

        def sem(name):
            sems.append(nc.alloc_semaphore(name))
            return sems[-1]

        phase(nc, sem, io, keep, stack)
        nc.clear_and_free_semaphores(sems)
        nc.all_engine_barrier()

    with ExitStack() as first:
        sb, _ = memory(nc, first)
        keep.rk = sb("rk", [P, T_KV, NTOK])
        keep.r = sb("r", [P, PAIRS, SEQ])
        with ExitStack() as hbuf:
            sbh, _ = memory(nc, hbuf)
            keep.h_hi, keep.h_lo = sbh("h_hi", [P, KD, NTOK], F32R), sbh("h_lo", [P, KD, NTOK], F32R)
            with ExitStack() as own:
                run(start, own)
            with ExitStack() as own:
                run(project, own)
        keep.up = sb("up", [P, 4 * W])
        keep.head_ones, keep.ones = sb("head_ones", [P, P]), sb("ones", [P, P])
        keep.half_w0, keep.half_a0 = sb("half_w0", [P, 8]), sb("half_a0", [P, 8])
        keep.half_ka, keep.rest_ka, keep.rest_ka2 = (sb(n, [P, 4]) for n in ("half_ka", "rest_ka", "rest_ka2"))
        with ExitStack() as own:
            sb, _ = memory(nc, own)
            keep.kk = sb("kk", [P, PAIRS, NTOK])
            keep.state = sb("state", [P, 2 * PAIRS, P])
            keep.nt, keep.bt, keep.dt, keep.et, keep.x1t = (
                [sb(f"{name}{s}", [P, 4, P]) for s in range(2)] for name in ("nt", "bt", "dt", "et", "x1t"))
            keep.wp = [[sb(f"wp{s}{j}", [P, 4, P]) for j in range(6)] for s in range(2)]
            keep.bkz = [sb(f"bkz{s}", [P, 2, 2, 2, P]) for s in range(2)]
            keep.m_strict, keep.m_incl = sb("m_strict", [P, 4, P], U8), sb("m_incl", [P, 4, P], U8)
            keep.m_level = [sb(f"m_level{j}", [P, 4, P], U8) for j in range(7)]
            with ExitStack() as prep:
                run(prepare_rwkv, prep)
            with ExitStack() as prep:
                run(recurrence, prep)
        with ExitStack() as own:
            run(finish_rwkv, own)
    with ExitStack() as second:
        sb, _ = memory(nc, second)
        keep.kvn, keep.rope_q = sb("kvn", [P, 2, NTOK]), sb("rope_q", [P, SEQ])
        keep.kvn_hi, keep.kvn_lo = sb("kvn_hi", [P, 2, NTOK], F32R), sb("kvn_lo", [P, 2, NTOK], F32R)
        keep.qn_hi, keep.qn_lo = sb("qn_hi", [P, 3, SEQ], F32R), sb("qn_lo", [P, 3, SEQ], F32R)
        keep.k_hi = [sb(f"k_hi{b}", [P, NTOK], F32R) for b in range(2)]
        keep.k_lo = [sb(f"k_lo{b}", [P, NTOK], F32R) for b in range(2)]
        with ExitStack() as own:
            run(normalise_latents, own)
        with ExitStack() as own:
            run(attention, own)
    with ExitStack() as third:
        sb, _ = memory(nc, third)
        keep.h_hi, keep.h_lo = sb("hx_hi", [P, KD, SEQ], F32R), sb("hx_lo", [P, KD, SEQ], F32R)
        keep.branch = [(sb(f"b{b}_hi", [P, PAIRS, SEQ], F32R), sb(f"b{b}_lo", [P, PAIRS, SEQ], F32R)) for b in range(3)]
        with ExitStack() as own:
            run(gate_branches, own)
        with ExitStack() as own:
            run(merge, own)
    with ExitStack() as own:
        run(project_out, own)


def build(nc, io):
    with ExitStack() as always:
        sb, _ = memory(nc, always)
        keep = Kept()
        keep.cols, keep.ident = sb("cols", [P, NCOL]), sb("ident", [P, P])
        keep.silu_c, keep.eps = sb("silu_c", [P, KD, 2]), sb("eps", [P, len(EPS)])
        phases(nc, io, keep)


def scratch(nc, io):
    new = lambda name, shape, dt=F32: nc.dram_tensor(name, shape, dt).ap()
    io["y"] = new("y_scratch", (2, PAIRS, P, SEQ))
    io["h"] = new("h_scratch", (2, P, KD, SEQ))
    io["lat"] = new("lat_scratch", (4, P, NTOK))
    io["ql"] = new("ql_scratch", (3, P, SEQ))
    io["branch"] = new("branch_scratch", (2, PAIRS, P, SEQ))
    io["merged"] = new("merged_scratch", (KD, P, SEQ))


def vectors(a):
    import numpy as np
    rows = [a["c"], a["c_ctx"], a["b_mod"][0, :2 * D], a["g_pre"]] + [a[n] for n, _ in COLS[4:]]
    return np.ascontiguousarray(np.concatenate([np.reshape(r, (-1, P)) for r in rows]).T)


def feature_tiles(w, n=P):
    import numpy as np
    c, f = w.shape
    return np.ascontiguousarray(w.reshape(c // P, P, f // n, n).transpose(2, 1, 0, 3).reshape(f // n, P, -1))


def laid_out(a):
    import numpy as np
    w = a["w_in"][0]
    at = np.cumsum([0, 384, 256, 32, 512, 512, 512, 512, 512, 512, 512, 512, 64, 64, 64, 64, 512, 3072])
    (ql, kv, kr, gm, ci, cb, cc, gc, r, k, v, wdf, wdb, adf, adb, gr, gl) = [w[:, s:e] for s, e in zip(at, at[1:])]
    rot, swap = (np.concatenate([kr[:, a::2], kr[:, 1 - a::2]], 1) for a in (0, 1))
    quarters = np.concatenate([z[:, s:s + P] for s in range(0, W, P) for z in (ci, cc, cb, gc, gm, gr)], 1)
    w_in = np.concatenate([k, v, wdf, wdb, adf, adb, kv, rot, rot, rot, rot, swap, swap, swap, swap, r, ql, quarters], 1)
    branches = [feature_tiles(a[n][0]) for n in ("w_br_mla", "w_br_conv", "w_br_rwkv")]
    gates = [feature_tiles(gl[:, b * D:(b + 1) * D]) for b in range(3)]
    merge = np.concatenate([np.stack(gates, 1), np.stack(branches, 1)], 3).reshape(3 * KD, P, D + W)
    uq = a["w_uq"][0].reshape(Q_LORA, HEADS, QK_HEAD)
    e, o = uq[:, :, NOPE::2], uq[:, :, NOPE + 1::2]
    uq = np.concatenate([uq[:, :, :NOPE], e, o, o, e], 2).reshape(Q_LORA, HEADS * P)
    ukv = a["w_ukv"][0].reshape(KV_LORA, HEADS, 2, HEAD).transpose(0, 2, 1, 3).reshape(KV_LORA, 2 * W)
    zero = np.zeros((HEAD, W), np.float32)
    up = [np.concatenate([m[0, 0], zero, zero, m[0, 1]], 0) for m in (a["w_up"], a["a_up"])]
    up = np.concatenate([u.reshape(2, P, W).transpose(1, 0, 2).reshape(P, 2 * W) for u in up], 1)
    freq = THETA ** (-np.arange(ROPE // 4, dtype=np.float32) / (ROPE // 4))
    tok = np.arange(SEQ)
    ang = np.concatenate([(tok // GRID_W).astype(np.float32)[None] * freq[:, None],
                          (tok % GRID_W).astype(np.float32)[None] * freq[:, None]]).astype(np.float32)
    cos, sin = np.cos(ang), np.sin(ang)
    rope = np.concatenate([cos, cos, -sin, sin]).astype(np.float32)
    return {
        "x": a["x"][0], "ctx": a["ctx"][0], "cols": vectors(a), "w_in": feature_tiles(w_in),
        "wm": feature_tiles(a["w_mod"][0][:, :2 * D]), "wm_gate": a["w_mod"][0][:, 2 * D:],
        "bm_gate": a["b_mod"][:, 2 * D:], "g_post": a["g_post"], "up": up, "rope": rope,
        "uq": feature_tiles(uq), "uk": feature_tiles(ukv[:, :W], NOPE), "uv": feature_tiles(ukv[:, W:]),
        "w_merge": merge, "w_out": a["w_out"][0],
    }


def kernel(**inputs):
    import numpy as np
    import concourse.bacc as bacc
    from concourse.bass_utils import run_bass_kernel_spmd

    nc = bacc.Bacc("TRN2", target_bir_lowering=False, num_devices=1)
    arrays, io = {}, {}
    for name, v in laid_out({k: np.asarray(v) for k, v in inputs.items()}).items():
        arrays[f"{name}_dram"] = np.ascontiguousarray(v)
        io[name] = nc.dram_tensor(f"{name}_dram", v.shape, mybir.dt.from_np(v.dtype), kind="ExternalInput").ap()
    io["out"] = nc.dram_tensor("out_dram", (SEQ, D), F32, kind="ExternalOutput").ap()
    scratch(nc, io)
    build(nc, io)
    got = run_bass_kernel_spmd(nc, [arrays], core_ids=[0]).results[0]["out_dram"]
    return got.reshape(1, SEQ, D)
```

```python
import math
from contextlib import ExitStack

import concourse.bass as bass
from concourse import mybir

ALU = mybir.AluOpType
ACT = mybir.ActivationFunctionType
AX = mybir.AxisListType
F32 = mybir.dt.float32
F32R = mybir.dt.float32r
U8 = mybir.dt.uint8
P = 128

D, SEQ, CTX = 1024, 1024, 256
KD = D // P
NTOK = SEQ + CTX
NT = NTOK // P
HEADS, HEAD = 8, 64
W = HEADS * HEAD
PAIRS = HEADS // 2
Q_LORA, KV_LORA, ROPE, NOPE = 384, 256, 32, 64
QK_HEAD = NOPE + ROPE
GRID_W, THETA = 64, 10000.0
SCALE = QK_HEAD ** -0.5
RMS_EPS, GN_EPS, L2_EPS = 1e-6, 64e-5, 1e-12
EPS = (RMS_EPS, GN_EPS, L2_EPS)
DECAY = math.exp(-0.5)

COLS = [("c", KD), ("c_ctx", KD), ("b_mod", 3 * KD), ("g_pre", KD), ("w0", 8), ("a0", 8), ("k_k", 4), ("k_a", 4),
        ("r_k", 4), ("gn_g", 4), ("gn_b", 4), ("conv_w", 12), ("conv_b", 4), ("g_q", 3), ("g_kv", 2), ("g_post", KD)]
COL = {name: sum(n for _, n in COLS[:i]) for i, (name, _) in enumerate(COLS)}
NCOL = sum(n for _, n in COLS)
T_K, T_V, T_WD, T_AD, T_KV, T_KR, T_R, T_QL, T_F, T_GL = 0, 4, 8, 9, 10, 12, 14, 18, 21, 45


class Kept:
    pass


class Count:

    def __init__(self, sem):
        self.sem, self.n, self.before = sem, 0, 0

    def up(self, ins):
        ins.then_inc(self.sem, 1)
        self.n += 1
        return self.before + self.n

    def enter(self, i, per):
        self.start, self.per = self.n, per
        self.before, self.n = i * per + self.start, 0

    def leave(self, rounds):
        assert self.n == self.per, (self.n, self.per)
        self.before, self.n = 0, self.start + self.per * rounds


class Link(Count):

    def __init__(self, sem, eng):
        super().__init__(sem)
        self.eng = eng

    def __call__(self, ins):
        self.eng.wait_ge(self.sem, self.up(ins))


def memory(nc, stack):
    def sb(name, shape, dt=F32):
        return stack.enter_context(nc.sbuf_tensor(name, shape, dt))

    def ps(name, shape, dt=F32):
        return stack.enter_context(nc.psum_tensor(name, shape, dt))

    return sb, ps


def start(nc, sem, io, keep, stack):
    sb, ps = memory(nc, stack)
    space = keep.rk[:].rearrange("p f t -> p (f t)")
    x_in = space[:, 0:NT * D].rearrange("p (t c) -> p t c", c=D)
    wm = keep.r
    junk = space[:, NT * D:(NT + 1) * D]
    ss = sb("ss", [P, NT])
    rs = sb("rs", [P, NT])
    silu_t = sb("silu_t", [P, 2 * KD])
    silu_s = sb("silu_s", [P, 2 * KD])
    silu_c = keep.silu_c
    mod = sb("mod", [P, 2, 2 * KD])
    h_val = sb("h_val", [P, 2, 512])
    mod_ps = ps("mod_ps", [P, 512])
    tr_ps = ps("tr_ps", [P, 4, 512])
    cols, ident, hi, lo = keep.cols, keep.ident, keep.h_hi, keep.h_lo

    cols_in, x_land = sem("cols_in"), [sem(f"x_land{t}") for t in range(NT)]
    wm_land, wm_used = [sem(f"wm_land{b}") for b in range(4)], sem("wm_used")
    sq_done, rs_done, xn_done, id_done = sem("sq_done"), sem("rs_done"), sem("xn_done"), sem("id_done")
    silu_done, root_done, eps_done = sem("silu_done"), sem("root_done"), sem("eps_done")
    tr_done, val_done, hi_done, lo_done = sem("tr_done"), sem("val_done"), sem("hi_done"), sem("lo_done")
    pool_link, dve_link = sem("start_pool"), sem("start_dve")
    NF = 2 * KD
    groups = [(4 * g, min(4, NT - 4 * g)) for g in range((NT + 3) // 4)]
    order = [(g, k) for g in (2, 0, 1) for k in range(KD)]

    with nc.Block() as block:
        @block.sync
        def _(sp):
            sp.dma_start(cols[:], io["cols"]).then_inc(cols_in, 16)
            for f in range(4):
                sp.dma_start(wm[:, f, :], io["wm"][f]).then_inc(wm_land[f], 16)
            for t in (8, 9, 0, 1, 2, 3, 4, 5, 6, 7):
                src = io["ctx"][(t - 8) * P:(t - 7) * P, :] if t >= 8 else io["x"][t * P:(t + 1) * P, :]
                sp.dma_start(x_in[:, t, :], src).then_inc(x_land[t], 16)
                f = 4 + (t + 2) % 10
                if f < NF:
                    sp.wait_ge(wm_used, f - 3)
                    sp.dma_start(wm[:, f % 4, :], io["wm"][f]).then_inc(wm_land[f % 4], 16)
            for f in range(14, NF):
                sp.wait_ge(wm_used, f - 3)
                sp.dma_start(wm[:, f % 4, :], io["wm"][f]).then_inc(wm_land[f % 4], 16)

        @block.scalar
        def _(act):
            squares = Link(sq_done, act)
            act.wait_ge(cols_in, 16)
            act.wait_ge(eps_done, len(EPS))
            nc.scalar.activation(silu_t[:], cols[:, 0:2 * KD], ACT.Tanh, scale=0.5).then_inc(silu_done, 1)
            for t in (8, 9, 0, 1, 2, 3, 4, 5, 6, 7):
                act.wait_ge(x_land[t], 16)
                squares(nc.scalar.activation(junk, x_in[:, t, :], ACT.Square, accum_out=ss[:, t:t + 1]))
                nc.scalar.activation(ss[:, t:t + 1], ss[:, t:t + 1], ACT.Sqrt, scale=1.0 / D,
                                     bias=keep.eps[:, 0:1]).then_inc(root_done, 1)
            for n, (g, k) in enumerate(order):
                w = groups[g][1] * P
                act.wait_ge(val_done, n + 1)
                nc.scalar.activation(hi[:, k, g * 512:g * 512 + w], h_val[:, n % 2, 0:w], ACT.Copy).then_inc(hi_done, 1)

        @block.gpsimd
        def _(pool):
            link = Link(pool_link, pool)
            for e, value in enumerate(EPS):
                nc.gpsimd.memset(keep.eps[:, e:e + 1], value).then_inc(eps_done, 1)
            link(nc.gpsimd.memset(ident[:], 0.0))
            nc.gpsimd.affine_select(out=ident[:], in_=ident[:], compare_op=ALU.not_equal, fill=1.0, base=0,
                                    pattern=[[-1, P]], channel_multiplier=1).then_inc(id_done, 1)
            for n, t in enumerate((8, 9, 0, 1, 2, 3, 4, 5, 6, 7)):
                pool.wait_ge(rs_done, n + 1)
                nc.gpsimd.tensor_scalar(x_in[:, t, :], x_in[:, t, :], rs[:, t:t + 1], None, ALU.mult).then_inc(xn_done, 1)
            for n, (g, k) in enumerate(order):
                w = groups[g][1] * P
                pool.wait_ge(hi_done, n + 1)
                nc.gpsimd.tensor_tensor(lo[:, k, g * 512:g * 512 + w], h_val[:, n % 2, 0:w],
                                        hi[:, k, g * 512:g * 512 + w].bitcast(F32), ALU.subtract).then_inc(lo_done, 1)

        @block.vector
        def _(dve):
            link = Link(dve_link, dve)
            dve.wait_ge(silu_done, 1)
            link(nc.vector.tensor_scalar(silu_s[:], silu_t[:], 0.5, 0.5, ALU.mult, ALU.add))
            nc.vector.tensor_tensor(silu_c[:], silu_s[:].rearrange("p (s k) -> p k s", s=2),
                                    cols[:, 0:2 * KD].rearrange("p (s k) -> p k s", s=2), ALU.mult).then_inc(silu_done, 1)
            for n, t in enumerate((8, 9, 0, 1, 2, 3, 4, 5, 6, 7)):
                dve.wait_ge(root_done, n + 1)
                nc.vector.reciprocal(rs[:, t:t + 1], ss[:, t:t + 1]).then_inc(rs_done, 1)
            dve.wait_ge(wm_used, NF)
            bias = cols[:, COL["b_mod"]:COL["b_mod"] + NF]
            for s in range(2):
                link(nc.vector.tensor_tensor(mod[:, s, :], mod_ps[:, s:2 * NF:2], bias, ALU.add))
                link(nc.vector.scalar_tensor_tensor(mod[:, s, KD:NF], mod[:, s, KD:NF], 1.0,
                                                    cols[:, COL["g_pre"]:COL["g_pre"] + KD], ALU.add, ALU.mult))
            for n, (g, k) in enumerate(order):
                w, s = groups[g][1] * P, int(g == 2)
                dve.wait_ge(tr_done, n + 1)
                if n >= 2:
                    dve.wait_ge(lo_done, n - 1)
                nc.vector.tensor_scalar(h_val[:, n % 2, 0:w], tr_ps[:, n % 4, 0:w], mod[:, s, KD + k:KD + k + 1],
                                        mod[:, s, k:k + 1], ALU.mult, ALU.add).then_inc(val_done, 1)

        @block.tensor
        def _(pe):
            pe.wait_ge(silu_done, 2)
            for f in range(NF):
                pe.wait_ge(wm_land[f % 4], 16 * (f // 4 + 1))
                for k in range(KD):
                    last = nc.tensor.matmul(mod_ps[:, 2 * f:2 * f + 2], wm[:, f % 4, k * P:(k + 1) * P],
                                            silu_c[:, k, :], start=(k == 0), stop=(k == KD - 1))
                last.then_inc(wm_used, 1)
            pe.wait_ge(id_done, 1)
            for n, (g, k) in enumerate(order):
                pe.wait_ge(xn_done, 2 + groups[g][0] + groups[g][1] if g < 2 else 2)
                if n >= 4:
                    pe.wait_ge(val_done, n - 3)
                for j in range(groups[g][1]):
                    last = nc.tensor.transpose(tr_ps[:, n % 4, j * P:(j + 1) * P],
                                               x_in[:, groups[g][0] + j, k * P:(k + 1) * P], ident[:])
                last.then_inc(tr_done, 1)


class WeightRing:

    def __init__(self, nc, sem, stack, name, width=D, raws=2):
        sb, _ = memory(nc, stack)
        self.nc, self.raws = nc, raws
        self.raw = sb(f"{name}_raw", [P, raws, width])
        self.hi = sb(f"{name}_hi", [P, 2, width], F32R)
        self.lo = sb(f"{name}_lo", [P, 2, width], F32R)
        self.landed = [sem(f"{name}_landed{b}") for b in range(2)]
        self.hi_made, self.lo_made, self.used = sem(f"{name}_hi_made"), sem(f"{name}_lo_made"), sem(f"{name}_used")

    def load(self, sp, src, t, b):
        sp.wait_ge(self.lo_made, t + 3 - self.raws)
        sp.dma_start(self.raw[:, b % self.raws, :], src).then_inc(self.landed[b], 16)

    def split_hi(self, act, t, b, turn):
        act.wait_ge(self.landed[b], turn * 16 + 16)
        act.wait_ge(self.used, t + 1)
        self.nc.scalar.activation(self.hi[:, b, :], self.raw[:, b % self.raws, :], ACT.Copy).then_inc(self.hi_made, 1)

    def split_lo(self, pool, t, b):
        pool.wait_ge(self.hi_made, t + 1)
        self.nc.gpsimd.tensor_tensor(self.lo[:, b, :], self.raw[:, b % self.raws, :], self.hi[:, b, :].bitcast(F32),
                                     ALU.subtract).then_inc(self.lo_made, 1)

    def wait(self, pe, t):
        pe.wait_ge(self.lo_made, t + 3)

    def products(self, b, hi, lo, outs, at=0, tiles=KD, before=None):
        for k in range(tiles):
            if before:
                before(k)
            for w, h in ((self.hi, hi), (self.hi, lo), (self.lo, hi)):
                for out, a, e in outs:
                    first, end = k == 0 and w is self.hi and h is hi, k == tiles - 1 and w is self.lo
                    last = self.nc.tensor.matmul(out, w[:, b, at + k * P:at + (k + 1) * P], h[:, k, a:e],
                                                 start=first, stop=end)
        return last


def project(nc, sem, io, keep, stack):
    sb, ps = memory(nc, stack)
    ring = WeightRing(nc, sem, stack, "in")
    out_ps = ps("in_ps", [P, 2, 3 * 512])
    stage = sb("lat_stage", [P, 2, NTOK])
    drained, staged, h_out = sem("in_drained"), sem("lat_staged"), sem("h_out")
    sent = [sem(f"lat_sent{b}") for b in range(2)]
    gate_ps = ps("gate_ps", [P, 2 * KD])
    gate_w = [keep.r[:, n, :] for n in range(PAIRS)] + [keep.rk[:, T_WD - 2 + n, 0:D] for n in range(PAIRS)]
    PEELED = 4
    gate_land, gate_mm, gate_done = sem("gate_land"), sem("gate_mm"), sem("gate_done")

    def send(act, t, n):
        if T_R <= t < T_QL:
            return n
        act.wait_ge(staged, n + 1)
        dst, e = (io["lat"][t - T_KV], NTOK) if t < T_R else (io["ql"][t - T_QL], SEQ)
        act.dma_start(dst, stage[:, n % 2, 0:e]).then_inc(sent[n % 2], 16)
        return n + 1

    with nc.Block() as block:
        @block.sync
        def _(sp):
            with sp.Fori(0, T_F // 2) as i:
                for b in range(2):
                    ring.load(sp, io["w_in"][i * 2 + b, :, :], i * 2 + b, b)
            ring.load(sp, io["w_in"][T_F - 1, :, :], T_F - 1, 0)

        @block.scalar
        def _(act):
            for f in range(KD):
                act.dma_start(gate_w[f], io["wm"][2 * KD + f]).then_inc(gate_land, 16)
            for part, h in enumerate((keep.h_hi, keep.h_lo)):
                act.dma_start(io["h"][part], h[:, :, 0:SEQ].bitcast(F32)).then_inc(h_out, 16)
            with act.Fori(0, T_KV // 2) as i:
                for b in range(2):
                    ring.split_hi(act, i * 2 + b, b, i)
            n = 0
            for t in range(T_KV, T_F):
                ring.split_hi(act, t, t % 2, t // 2)
                if t >= T_KV + 2:
                    n = send(act, t - 2, n)
            for t in (T_F - 2, T_F - 1):
                n = send(act, t, n)
            for b in range(2):
                act.wait_ge(sent[b], 16 * ((n + 1 - b) // 2))
            act.wait_ge(h_out, 32)

        @block.gpsimd
        def _(pool):
            pool.sem_inc(ring.lo_made, 2)
            with pool.Fori(0, T_KV // 2) as i:
                for b in range(2):
                    ring.split_lo(pool, i * 2 + b, b)
            for t in range(T_KV, T_F):
                ring.split_lo(pool, t, t % 2)

        @block.tensor
        def _(pe):
            pe.sem_inc(ring.used, 2)

            def tile(t, b, end):
                ring.wait(pe, t)
                pe.wait_ge(drained, t + 1)
                outs = [(out_ps[:, b, a:min(a + 512, end)], a, min(a + 512, end)) for a in range(0, end, 512)]
                ring.products(b, keep.h_hi, keep.h_lo, outs).then_inc(ring.used, 1)

            for t in range(PEELED):
                tile(t, t % 2, NTOK)
            pe.wait_ge(gate_land, 16 * KD)
            for f in range(KD):
                for k in range(KD):
                    last = nc.tensor.matmul(gate_ps[:, 2 * f:2 * f + 2], gate_w[f][:, k * P:(k + 1) * P],
                                            keep.silu_c[:, k, :], start=k == 0, stop=k == KD - 1)
            last.then_inc(gate_mm, 1)
            for first, end, tokens in ((PEELED, T_R, NTOK), (T_R, T_F - 1, SEQ)):
                with pe.Fori(first // 2, end // 2) as i:
                    for b in range(2):
                        tile(i * 2 + b, b, tokens)
            tile(T_F - 1, 0, SEQ)

        @block.vector
        def _(dve):
            dve.sem_inc(drained, 2)

            def drain(t, b, end, dst):
                dve.wait_ge(ring.used, t + 3)
                nc.vector.tensor_copy(dst, out_ps[:, b, 0:end]).then_inc(drained, 1)

            def row(store, i):
                return store[:, bass.ds(i, 1), :].rearrange("p a t -> p (a t)")

            for t in range(PEELED):
                drain(t, t % 2, NTOK, keep.rk[:, t, :])
            dve.wait_ge(gate_mm, 1)
            half_post = keep.gate_cols
            nc.vector.tensor_tensor(half_post[:], gate_ps[:, 0:2 * KD:2], keep.cols[:, COL["b_mod"] + 2 * KD:COL["b_mod"] + 3 * KD],
                                    ALU.add).then_inc(gate_done, 1)
            dve.wait_ge(gate_done, 1)
            nc.vector.scalar_tensor_tensor(half_post[:], half_post[:], 0.5, keep.cols[:, COL["g_post"]:COL["g_post"] + KD],
                                           ALU.mult, ALU.mult)
            with dve.Fori(PEELED // 2, T_KV // 2) as i:
                for b in range(2):
                    drain(i * 2 + b, b, NTOK, row(keep.rk, i * 2 + b))
            n = 0
            for t in range(T_KV, T_F):
                if T_R <= t < T_QL:
                    drain(t, t % 2, SEQ, keep.r[:, t - T_R, :])
                    continue
                if n >= 2:
                    dve.wait_ge(sent[n % 2], 16 * (n // 2))
                end = NTOK if t < T_R else SEQ
                dve.wait_ge(ring.used, t + 3)
                nc.vector.tensor_copy(stage[:, n % 2, 0:end], out_ps[:, t % 2, 0:end]).then_inc(drained, 1)
                dve.wait_ge(drained, t + 3)
                dve.sem_inc(staged, 1)
                n += 1


def prepare_rwkv(nc, sem, io, keep, stack):
    sb, ps = memory(nc, stack)
    sq = sb("kk_sq", [P, NTOK])
    root = sb("kk_root", [P, NTOK])
    norm_ps = ps("kk_ps", [P, 3 * 512])
    work = sb("mask_work", [P, 2, P])
    rk, kk, cols = keep.rk, keep.kk, keep.cols
    sq_done, norm_mm, root_done, kk_done = sem("kk_sq_done"), sem("kk_mm"), sem("kk_root_done"), sem("kk_done")
    ones_done, up_in = sem("block_ones_done"), sem("up_in")
    pool_link, dve_link, act_link = sem("prep_pool"), sem("prep_dve"), sem("prep_act")
    with nc.Block() as block:
        @block.sync
        def _(sp):
            sp.dma_start(keep.up[:], io["up"]).then_inc(up_in, 16)
            sp.wait_ge(up_in, 16)

        @block.gpsimd
        def _(pool):
            link = Link(pool_link, pool)
            nc.gpsimd.memset(keep.ones[:], 1.0)
            nc.gpsimd.memset(keep.state[:], 0.0)
            for s in range(2):
                nc.gpsimd.memset(keep.bkz[s][:], 0.0)
                for buf in (keep.nt[s], keep.bt[s], keep.dt[s], keep.et[s], keep.x1t[s], *keep.wp[s]):
                    link(nc.gpsimd.memset(buf[:], 0.0))
                for buf in (keep.x1t[s], *keep.wp[s]):
                    nc.gpsimd.affine_select(out=buf[:], in_=buf[:], compare_op=ALU.not_equal, fill=1.0, base=0,
                                            pattern=[[0, 4], [-1, P]], channel_multiplier=1)

            def mask(dst, cuts, view):
                for d in range(2):
                    w = work[:, d, :]
                    link(nc.gpsimd.memset(w, 0.0))
                    part = view(w, d)
                    link(nc.gpsimd.memset(part, 1.0))
                    for base, pattern, mult in cuts[d]:
                        link(nc.gpsimd.affine_select(out=part, in_=part, compare_op=ALU.is_ge, fill=0.0, base=base,
                                                     pattern=pattern, channel_multiplier=mult))
                    for e in range(2):
                        link(nc.gpsimd.tensor_copy(dst[:, 2 * d + e, :], w))

            whole = lambda w, d: w
            mask(keep.m_strict, [[(-1, [[1, P]], -1)], [(-1, [[-1, P]], 1)]], whole)
            mask(keep.m_incl, [[(0, [[1, P]], -1)], [(0, [[-1, P]], 1)]], whole)
            for j in range(7):
                half = 1 << j
                n = P // (2 * half)

                def halves(w, d, second):
                    return w.rearrange("p (n two h) -> p n two h", two=2, h=half)[:, :, second, :]

                first_rows = [(0, [[-2 * half, n], [0, half]], 1), (half - 1, [[2 * half, n], [0, half]], -1)]
                second_rows = [(-half, [[-2 * half, n], [0, half]], 1), (2 * half - 1, [[2 * half, n], [0, half]], -1)]
                flip = j == 0
                rows = [first_rows, second_rows] if flip else [second_rows, first_rows]
                mask(keep.m_level[j], rows, lambda w, d: halves(w, d, (1 - d) if flip else d))

        @block.scalar
        def _(act):
            link = Link(act_link, act)
            link(nc.scalar.activation(rk[:, T_WD, :], rk[:, T_WD, :], ACT.Tanh))
            for p in range(PAIRS):
                if p:
                    act.wait_ge(norm_mm, p)
                nc.scalar.activation(sq[:], rk[:, T_K + p, :], ACT.Square,
                                     scale=cols[:, COL["k_k"] + p:COL["k_k"] + p + 1]).then_inc(sq_done, 1)
                act.wait_ge(norm_mm, p + 1)
                if p:
                    act.wait_ge(kk_done, p)
                nc.scalar.activation(root[:], norm_ps[:, 0:NTOK], ACT.Sqrt, bias=keep.eps[:, 2:3]).then_inc(root_done, 1)

        @block.tensor
        def _(pe):
            pe.wait_ge(ones_done, 1)
            for p in range(PAIRS):
                pe.wait_ge(sq_done, p + 1)
                if p:
                    pe.wait_ge(root_done, p)
                for a, e in ((0, 512), (512, 1024), (1024, NTOK)):
                    last = nc.tensor.matmul(norm_ps[:, a:e], keep.head_ones[:], sq[:, a:e], start=True, stop=True)
                last.then_inc(norm_mm, 1)

        @block.vector
        def _(dve):
            link = Link(dve_link, dve)
            link(nc.vector.memset(keep.head_ones[:], 0.0))
            nc.vector.memset(keep.head_ones[0:HEAD, 0:HEAD], 1.0)
            nc.vector.memset(keep.head_ones[HEAD:P, HEAD:P], 1.0).then_inc(ones_done, 1)
            nc.vector.tensor_scalar(keep.half_w0[:], cols[:, COL["w0"]:COL["w0"] + 8], 0.5, None, ALU.mult)
            nc.vector.tensor_scalar(keep.half_a0[:], cols[:, COL["a0"]:COL["a0"] + 8], 0.5, None, ALU.mult)
            ka = cols[:, COL["k_a"]:COL["k_a"] + 4]
            nc.vector.tensor_scalar(keep.half_ka[:], ka, 0.5, None, ALU.mult)
            nc.vector.tensor_scalar(keep.rest_ka[:], ka, -0.5, 1.0, ALU.mult, ALU.add)
            nc.vector.tensor_scalar(keep.rest_ka2[:], ka, -1.0, 2.0, ALU.mult, ALU.add)
            for p in range(PAIRS):
                dve.wait_ge(root_done, p + 1)
                link(nc.vector.reciprocal(root[:], root[:]))
                nc.vector.scalar_tensor_tensor(kk[:, p, :], rk[:, T_K + p, :],
                                               cols[:, COL["k_k"] + p:COL["k_k"] + p + 1], root[:],
                                               ALU.mult, ALU.mult).then_inc(kk_done, 1)


def recurrence(nc, sem, io, keep, stack):
    sb, ps = memory(nc, stack)
    rk, kk = keep.rk, keep.kk
    bank = [ps(f"bank{s}", [P, 4, 512]) for s in range(2)]
    th = [sb(f"th{s}", [P, 4, P]) for s in range(2)]
    ell = [sb(f"ell{s}", [P, 2, P]) for s in range(2)]
    cum = [sb(f"cum{s}", [P, 2, P]) for s in range(2)]
    exc = [sb(f"exc{s}", [P, 2, P]) for s in range(2)]
    mid = [sb(f"mid{s}", [P, 2, 2]) for s in range(2)]
    e_inv = [sb(f"e_inv{s}", [P, 2, P]) for s in range(2)]
    a_e, v_st = ell, cum
    g_e = [t[:, 0:2, :] for t in th]
    h = [sb(f"h{p}", [P, 2]) for p in range(PAIRS)]
    ar = [sb(f"ar{p}", [P, 2, 2, P]) for p in range(PAIRS)]
    tok = [sb(f"tok{p}", [P, 3, 2, P]) for p in range(PAIRS)]
    xm = [sb(f"xm{s}", [P, 4, P]) for s in range(2)]
    xt = [sb(f"xt{s}", [P, 4, P]) for s in range(2)]
    z = [sb(f"z{s}", [P, 2, P]) for s in range(2)]
    p1 = [sb(f"p1_{s}", [P, 2, P]) for s in range(2)]
    u = [sb(f"u{s}", [P, 2, P]) for s in range(2)]
    bk_both = [sb(f"bk_both{s}", [P, 2, 2, P]) for s in range(2)]
    rm, y_st = p1, u
    dve_link, passed = sem("rec_dve"), sem("rec_passed")
    two = lambda name: [sem(f"{name}{s}") for s in range(2)]
    up_mm, th_done, cum_done, exp_done, bk_done, ar_done = map(two, ("up_mm", "th_done", "cum_done", "exp_done", "bk_done", "ar_done"))
    bk_mm, bk_tok, v_mm, v_tok = map(two, ("bk_mm", "bk_tok", "v_mm", "v_tok"))
    score_mm, x1t_done, masked, x_mm, x_done = map(two, ("score_mm", "x1t_done", "masked", "x_mm", "x_done"))
    w_mm, w_done, xt_mm, xt_done = map(two, ("w_mm", "w_done", "xt_mm", "xt_done"))
    z_done, p_mm, p_done, u_mm, u_done, s_mm, s_done, y_mm, y_done, y_sent = map(
        two, ("z_done", "p_mm", "p_done", "u_mm", "u_done", "s_mm", "s_done", "y_mm", "y_done", "y_sent"))
    LEVELS = range(1, 7)
    UNITS = [(d, e) for d in range(2) for e in range(2)]

    def tokens(n):
        if isinstance(n, int) and n < 2:
            return SEQ + n * P, SEQ + CTX - P - n * P
        return (n - 2) * P, SEQ - P - (n - 2) * P

    def seg(buf, i, at):
        return buf[:, i, bass.ds(at, P)]

    def wait(eng, s, value):
        if not (isinstance(value, int) and value <= 0):
            eng.wait_ge(s, value)

    class Tensor:
        def __init__(self, eng):
            self.eng = eng

        def up(self, v, p, n):
            s, pe = p % 2, self.eng
            wait(pe, masked[s], v)
            at = tokens(n)
            for m, tile in ((0, T_WD), (1, T_AD)):
                for d in range(2):
                    last = nc.tensor.matmul(bank[s][:, 3, (2 * m + d) * P:(2 * m + d + 1) * P],
                                            keep.up[:, (2 * m + d) * W + p * P:(2 * m + d) * W + (p + 1) * P],
                                            seg(rk, tile, at[d]), start=True, stop=True)
            last.then_inc(up_mm[s], 1)

        def bk_turn(self, v, p):
            s, pe = p % 2, self.eng
            wait(pe, th_done[s], v + 1)
            wait(pe, bk_done[s], v + 1)
            for i in range(2):
                for d in range(2):
                    c = (2 * i + d) * P
                    last = nc.tensor.transpose(bank[s][:, 3, c:c + P], bk_both[s][:, i, d, :], keep.ident[:])
            last.then_inc(bk_mm[s], 1)

        def v_turn(self, v, p):
            s, pe = p % 2, self.eng
            wait(pe, bk_tok[s], v + 1)
            wait(pe, ar_done[s], v + 1)
            for d in range(2):
                last = nc.tensor.transpose(bank[s][:, 3, d * P:(d + 1) * P], v_st[s][:, d, :], keep.ident[:])
            last.then_inc(v_mm[s], 1)

        def scores(self, v, p, emit):
            s, pe = p % 2, self.eng
            wait(pe, bk_done[s], v + 1)
            wait(pe, ar_done[s], v + 1)
            wait(pe, v_tok[s], v + 1)
            wait(pe, p_done[s], v)
            wait(pe, u_done[s], v)
            wait(pe, s_done[s], v)
            wait(pe, y_done[s], v - 4)
            for i, (d, e) in enumerate(UNITS):
                for j in range(2):
                    m = 2 if emit else 1
                    last = nc.tensor.matmul(bank[s][:, i, 2 * j * P:(2 * j + m) * P], keep.bkz[s][:, j, d, e, :],
                                            ar[p][:, d, 0:m, :], start=True, stop=True)
            last.then_inc(score_mm[s], 1)

        def x1_turn(self, v, p):
            s, pe = p % 2, self.eng
            wait(pe, x1t_done[s], v + 1)
            wait(pe, masked[s], v + 1)
            for i in range(4):
                last = nc.tensor.transpose(bank[s][:, 1, i * P:(i + 1) * P], keep.x1t[s][:, i, :], keep.ident[:])
            last.then_inc(x_mm[s], 1)

        def level_w(self, v, p, j):
            s, pe = p % 2, self.eng
            wait(pe, x_done[s], v * 6 + j)
            for i in range(4):
                last = nc.tensor.matmul(bank[s][:, 0, i * P:(i + 1) * P], keep.nt[s][:, i, :], xm[s][:, i, :],
                                        start=True, stop=True)
            last.then_inc(w_mm[s], 1)

        def level_x(self, v, p, j):
            s, pe = p % 2, self.eng
            wait(pe, w_done[s], v * 6 + j)
            if j > 1:
                wait(pe, xt_done[s], v * 6 + j - 1)
            xt_now = keep.x1t[s] if j == 1 else xt[s]
            if j < 6:
                for i in range(4):
                    last = nc.tensor.matmul(bank[s][:, 1, i * P:(i + 1) * P], xt_now[:, i, :],
                                            keep.wp[s][j - 1][:, i, :], start=True, stop=True)
                last.then_inc(x_mm[s], 1)
            for i in range(4):
                last = nc.tensor.matmul(bank[s][:, 2, i * P:(i + 1) * P], keep.wp[s][j - 1][:, i, :],
                                        xt_now[:, i, :], start=True, stop=True)
            last.then_inc(xt_mm[s], 1)

        def rhs(self, v, p, fronted):
            s, pe = p % 2, self.eng
            wait(pe, z_done[s], v + 1)
            wait(pe, v_tok[s], v + 1 + fronted)
            for d in range(2):
                nc.tensor.matmul(bank[s][:, 3, d * P:(d + 1) * P], ar[p][:, d, 0, :], z[s][:, d, :],
                                 start=True, stop=False, skip_group_check=True)
                for e in range(2):
                    c = d * P + e * HEAD
                    last = nc.tensor.matmul(bank[s][:, 3, c:c + HEAD], keep.bt[s][:, 2 * d + e, :],
                                            tok[p][:, 2, d, e * HEAD:(e + 1) * HEAD], start=False, stop=True,
                                            skip_group_check=True)
            last.then_inc(p_mm[s], 1)

        def solve(self, v, p):
            s, pe = p % 2, self.eng
            wait(pe, p_done[s], v + 1)
            wait(pe, xt_done[s], v * 6 + 6)
            for i, (d, e) in enumerate(UNITS):
                c = d * P + e * HEAD
                last = nc.tensor.matmul(bank[s][:, 0, c:c + HEAD], xt[s][:, i, :],
                                        p1[s][:, d, e * HEAD:(e + 1) * HEAD], start=True, stop=True)
            last.then_inc(u_mm[s], 1)

        def ends(self, v, p, emit):
            s, pe = p % 2, self.eng
            wait(pe, u_done[s], v + 1)
            for d in range(2):
                for i, src in ((0, u[s][:, d, :]), (1, tok[p][:, 2, d, :])):
                    last = nc.tensor.matmul(bank[s][:, 1, d * P:(d + 1) * P], tok[p][:, i, d, :], src,
                                            start=(i == 0), stop=(i == 1))
            last.then_inc(s_mm[s], 1)
            if not emit:
                return
            for d in range(2):
                c = d * P
                nc.tensor.matmul(bank[s][:, 2, c:c + P], z[s][:, d, :], ar[p][:, d, 1, :], start=True, stop=False,
                                 skip_group_check=True)
                for e in range(2):
                    part = slice(e * HEAD, (e + 1) * HEAD)
                    nc.tensor.matmul(bank[s][part, 2, c:c + P], u[s][:, d, part], keep.dt[s][:, 2 * d + e, :],
                                     start=False, stop=False, skip_group_check=True)
                    last = nc.tensor.matmul(bank[s][part, 2, c:c + P], tok[p][:, 2, d, part],
                                            keep.et[s][:, 2 * d + e, :], start=False, stop=True, skip_group_check=True)
            last.then_inc(y_mm[s], 1)

    class Scalar:
        def __init__(self, eng):
            self.eng = eng

        def gates(self, v, p):
            s, act = p % 2, self.eng
            wait(act, up_mm[s], v + 1)
            wait(act, bk_done[s], v)
            for m, half in ((0, keep.half_w0), (1, keep.half_a0)):
                for d in range(2):
                    i = 2 * m + d
                    last = nc.scalar.activation(th[s][:, i, :], bank[s][:, 3, i * P:(i + 1) * P], ACT.Tanh,
                                                scale=0.5, bias=half[:, d * 4 + p:d * 4 + p + 1])
            last.then_inc(th_done[s], 1)

        def exps(self, v, p):
            s, act = p % 2, self.eng
            wait(act, cum_done[s], v + 1)
            wait(act, ar_done[s], v)
            wait(act, bk_done[s], v)
            minus, plus = mid[s][:, 0, :], mid[s][:, 1, :]
            now, before, inv = ar[p][:, :, 1, :], ar[p][:, :, 0, :], e_inv[s]
            for dst, d, src, up in ((inv, 0, cum, 0), (inv, 1, exc, 1), (before, 0, exc, 1), (before, 1, cum, 0),
                                    (now, 0, cum, 1), (now, 1, exc, 0)):
                nc.scalar.activation(dst[:, d, :], src[s][:, d, :], ACT.Exp, scale=1.0 if up else -1.0,
                                     bias=(minus if up else plus)[:, d:d + 1])
            nc.scalar.activation(h[p][:], plus, ACT.Exp).then_inc(exp_done[s], 1)

        def bk(self, v, p):
            s, act = p % 2, self.eng
            wait(act, bk_mm[s], v + 1)
            nc.scalar.activation(tok[p][:, 0:2, :, :], bank[s][:, 3, :].rearrange("p (i d t) -> p i d t", i=2, d=2),
                                 ACT.Copy).then_inc(bk_tok[s], 1)

        def v(self, v, p):
            s, act = p % 2, self.eng
            wait(act, v_mm[s], v + 1)
            nc.scalar.activation(tok[p][:, 2, :, :], bank[s][:, 3, 0:2 * P].rearrange("p (d t) -> p d t", d=2),
                                 ACT.Copy).then_inc(v_tok[s], 1)

        def x(self, v, p, j):
            s, act = p % 2, self.eng
            if j < 7:
                wait(act, x_mm[s], v * 6 + j)
                nc.scalar.activation(xm[s][:], bank[s][:, 1, :].rearrange("p (u t) -> p u t", u=4),
                                     ACT.Copy).then_inc(x_done[s], 1)
            if j > 1:
                wait(act, xt_mm[s], v * 6 + j - 1)
                nc.scalar.activation(xt[s][:], bank[s][:, 2, :].rearrange("p (u t) -> p u t", u=4),
                                     ACT.Copy).then_inc(xt_done[s], 1)

        def rhs(self, v, p):
            s, act = p % 2, self.eng
            wait(act, p_mm[s], v + 1)
            nc.scalar.activation(p1[s][:], bank[s][:, 3, 0:2 * P].rearrange("p (d t) -> p d t", d=2),
                                 ACT.Copy).then_inc(p_done[s], 1)

        def solve(self, v, p):
            s, act = p % 2, self.eng
            wait(act, u_mm[s], v + 1)
            wait(act, y_sent[s], (v - 4) * 32)
            nc.scalar.activation(u[s][:], bank[s][:, 0, 0:2 * P].rearrange("p (d t) -> p d t", d=2),
                                 ACT.Copy).then_inc(u_done[s], 1)

        def y(self, v, p):
            s, act = p % 2, self.eng
            wait(act, y_mm[s], v - 3)
            nc.scalar.activation(y_st[s][:], bank[s][:, 2, 0:2 * P].rearrange("p (d t) -> p d t", d=2),
                                 ACT.Copy).then_inc(y_done[s], 1)

    class Vector:
        def __init__(self, eng, link):
            self.eng, self.link = eng, link

        def cumulate(self, v, p):
            s, dve, link = p % 2, self.eng, self.link
            wait(dve, th_done[s], v + 1)
            link(nc.vector.tensor_scalar(ell[s][:], th[s][:, 0:2, :], -0.5 * DECAY, -0.5 * DECAY, ALU.mult, ALU.add))
            for d in range(2):
                last = nc.vector.tensor_tensor_scan(cum[s][:, d, :], keep.ones[:], ell[s][:, d, :], 0.0, ALU.mult, ALU.add)
            link(last)
            nc.vector.tensor_scalar(mid[s][:, 0, :], cum[s][:, :, P - 1], -0.5, None, ALU.mult)
            nc.vector.tensor_scalar(mid[s][:, 1, :], cum[s][:, :, P - 1], 0.5, None, ALU.mult)
            nc.vector.tensor_tensor(exc[s][:], cum[s][:], ell[s][:], ALU.subtract).then_inc(cum_done[s], 1)
            link(nc.vector.tensor_scalar(g_e[s], th[s][:, 2:4, :], keep.half_ka[:, p:p + 1], keep.rest_ka[:, p:p + 1],
                                         ALU.mult, ALU.add))

        def operands(self, v, p, n):
            s, dve, link = p % 2, self.eng, self.link
            wait(dve, exp_done[s], v + 1)
            nc.vector.scalar_tensor_tensor(a_e[s][:], th[s][:, 2:4, :], 1.0, e_inv[s][:], ALU.add, ALU.mult)
            link(nc.vector.tensor_tensor(g_e[s], g_e[s], e_inv[s][:], ALU.mult))
            at = tokens(n)
            for d in range(2):
                nc.vector.scalar_tensor_tensor(bk_both[s][:, 0, d, :], seg(kk, p, at[d]), -0.5, a_e[s][:, d, :],
                                               ALU.mult, ALU.mult)
                last = nc.vector.tensor_tensor(bk_both[s][:, 1, d, :], seg(rk, T_K + p, at[d]), g_e[s][:, d, :], ALU.mult)
            link(last)
            for e in range(2):
                part = slice(e * HEAD, (e + 1) * HEAD)
                last = nc.vector.tensor_copy(keep.bkz[s][part, :, :, e, :], bk_both[s][part, :, :, :])
            last.then_inc(bk_done[s], 1)

        def scores(self, v, p, emit):
            s, dve = p % 2, self.eng
            wait(dve, score_mm[s], v + 1)
            dve.sem_inc(passed, 1)
            part = lambda j: bank[s][:, :, j * P:(j + 1) * P]
            nc.vector.copy_predicated(keep.x1t[s][:], keep.m_level[0][:], part(0)).then_inc(x1t_done[s], 1)
            kept = [(keep.nt, keep.m_strict, 0), (keep.bt, keep.m_strict, 2)]
            if emit:
                kept += [(keep.dt, keep.m_incl, 1), (keep.et, keep.m_incl, 3)]
            for dst, m, j in kept:
                last = nc.vector.copy_predicated(dst[s][:], m[:], part(j))
            last.then_inc(masked[s], 1)

        def level(self, v, p, j):
            s, dve = p % 2, self.eng
            wait(dve, w_mm[s], v * 6 + j)
            dve.sem_inc(passed, 1)
            nc.vector.copy_predicated(keep.wp[s][j - 1][:], keep.m_level[j][:],
                                      bank[s][:, 0, :].rearrange("p (u t) -> p u t", u=4)).then_inc(w_done[s], 1)

        def z(self, v, p):
            s, dve, link = p % 2, self.eng, self.link
            for d in range(2):
                last = nc.vector.tensor_scalar(z[s][:, d, :], keep.state[:, 2 * p + d, :], h[p][:, d:d + 1], None, ALU.mult)
            link(last)
            dve.sem_inc(z_done[s], 1)

        def state(self, v, p):
            s, dve, link = p % 2, self.eng, self.link
            wait(dve, s_mm[s], v + 1)
            for d in range(2):
                last = nc.vector.scalar_tensor_tensor(rm[s][:, d, :], bank[s][:, 1, d * P:(d + 1) * P], h[p][:, d:d + 1],
                                                      keep.head_ones[:], ALU.mult, ALU.mult)
            link(last)
            dve.sem_inc(s_done[s], 1)
            for d in range(2):
                last = nc.vector.scalar_tensor_tensor(keep.state[:, 2 * p + d, :], z[s][:, d, :], h[p][:, d:d + 1],
                                                      rm[s][:, d, :], ALU.mult, ALU.add)
            link(last)

    class Pool:
        def __init__(self, eng):
            self.eng = eng

        def operands(self, v, p, n):
            s, pool = p % 2, self.eng
            emit = not isinstance(n, int) or n >= 2
            wait(pool, exp_done[s], v + 1)
            at = tokens(n)
            for d in range(2):
                nc.gpsimd.tensor_tensor(ar[p][:, d, 0, :], seg(kk, p, at[d]), ar[p][:, d, 0, :], ALU.mult)
                if emit:
                    nc.gpsimd.tensor_tensor(ar[p][:, d, 1, :], seg(keep.r, p, at[d]), ar[p][:, d, 1, :], ALU.mult)
                last = nc.gpsimd.tensor_copy(v_st[s][:, d, :], seg(rk, T_V + p, at[d]))
            last.then_inc(ar_done[s], 1)

    class Sync:
        def __init__(self, eng):
            self.eng = eng

        def y(self, v, p, n):
            s, sp = p % 2, self.eng
            sp.wait_ge(y_done[s], v - 3)
            at = tokens(n)
            for d in range(2):
                sp.dma_start(io["y"][d, p, :, bass.ds(at[d], P)], y_st[s][:, d, :]).then_inc(y_sent[s], 16)

    def program(engine, eng, link=None):
        if engine == "tensor":
            t = Tensor(eng)
            front = [lambda v, p, n: t.up(v, p, n), lambda v, p, n: t.bk_turn(v, p), lambda v, p, n: t.v_turn(v, p)]
            places = [1, 3, 4]
        elif engine == "scalar":
            t = Scalar(eng)
            front = [lambda v, p, n: t.gates(v, p), lambda v, p, n: t.exps(v, p), lambda v, p, n: t.bk(v, p),
                     lambda v, p, n: t.v(v, p)]
            places = [1, 2, 3, 4]
        elif engine == "vector":
            t = Vector(eng, link)
            front = [lambda v, p, n: t.cumulate(v, p), lambda v, p, n: t.operands(v, p, n)]
            places = [1, 2]
        elif engine == "sync":
            t, front, places = Sync(eng), [], []
        else:
            t = Pool(eng)
            front = [lambda v, p, n: t.operands(v, p, n)]
            places = [2]

        def fronts(after, nxt):
            for place, step in zip(places, front):
                if place == after or after is None:
                    for v, p, n in nxt:
                        step(v, p, n)

        def half(n, sub, emit, nxt):
            v = 2 * n + sub
            pairs = (2 * sub, 2 * sub + 1)
            for p in pairs:
                if engine in ("tensor", "vector"):
                    t.scores(v, p, emit)
            for p in pairs:
                if engine == "tensor":
                    t.x1_turn(v, p)
                elif engine == "scalar":
                    t.x(v, p, 1)
            for j in LEVELS:
                for p in pairs:
                    if engine == "tensor":
                        t.level_w(v, p, j)
                    elif engine == "vector":
                        t.level(v, p, j)
                fronts(j, nxt)
                if j == 5:
                    for p in pairs:
                        if engine == "tensor":
                            t.rhs(v, p, int(bool(nxt)))
                        elif engine == "vector":
                            t.z(v, p)
                        elif engine == "scalar":
                            t.rhs(v, p)
                for p in pairs:
                    if engine == "tensor":
                        t.level_x(v, p, j)
                    elif engine == "scalar":
                        t.x(v, p, j + 1)
            for p in pairs:
                if engine in ("tensor", "scalar"):
                    t.solve(v, p)
            for p in pairs:
                if engine == "tensor":
                    t.ends(v, p, emit)
                elif engine == "vector":
                    t.state(v, p)
                elif engine == "scalar" and emit:
                    t.y(v, p)
                elif engine == "sync" and emit:
                    t.y(v, p, n)

        def chunk(n, emit, more):
            half(n, 0, emit, [(2 * n + 1, p, n) for p in (2, 3)])
            half(n, 1, emit, [(2 * n + 2, p, n + 1) for p in (0, 1)] if more else [])

        fronts(None, [(0, p, 0) for p in (0, 1)])
        chunk(0, False, True)
        chunk(1, False, True)
        with eng.Fori(0, NT - 3) as i:
            if link is not None:
                link.enter(i, chunk_links)
            chunk(i + 2, True, True)
        if link is not None:
            link.leave(NT - 3)
        chunk(NT - 1, True, False)

    chunk_links = PAIRS * 8
    with nc.Block() as block:
        @block.sync
        def _(sp):
            program("sync", sp)
            for s in range(2):
                sp.wait_ge(y_sent[s], 32 * 2 * SEQ // P)

        @block.tensor
        def _(pe):
            program("tensor", pe)

        @block.scalar
        def _(act):
            program("scalar", act)

        @block.vector
        def _(dve):
            program("vector", dve, Link(dve_link, dve))

        @block.gpsimd
        def _(pool):
            program("gpsimd", pool)


def finish_rwkv(nc, sem, io, keep, stack):
    sb, ps = memory(nc, stack)
    rk, cols = keep.rk, keep.cols
    y, bonus = sb("gn_y", [P, 2, 2, SEQ]), sb("gn_bonus", [P, 2, SEQ])
    th, work = sb("gn_th", [P, 2, SEQ]), sb("gn_work", [P, SEQ])
    sq, root = sb("gn_sq", [P, SEQ]), sb("gn_root", [P, SEQ])
    out = sb("gn_out", [P, 2, SEQ])
    a_ps, sum_ps, mean_ps = ps("gn_a", [P, 2, 1024]), ps("gn_sum", [P, 1024]), ps("gn_mean", [P, 1024])
    y_in = [sem(f"gn_in{b}") for b in range(2)]
    sent = [sem(f"gn_sent{b}") for b in range(2)]
    a_mm, th_done, work_done, bonus_mm, bonus_done = map(sem, ("gn_a_mm", "gn_th_done", "gn_work_done", "gn_bonus_mm", "gn_bonus_done"))
    y_sum, mean_mm, centred, sq_done, var_mm, root_done, out_done = map(
        sem, ("gn_y_sum", "gn_mean_mm", "gn_centred", "gn_sq_done", "gn_var_mm", "gn_root_done", "gn_out_done"))
    dve_link, act_link = sem("gn_dve"), sem("gn_act")
    col = lambda name, p: cols[:, COL[name] + p:COL[name] + p + 1]
    halves = ((0, 512), (512, SEQ))
    with nc.Block() as block:
        @block.sync
        def _(sp):
            for p in range(PAIRS):
                if p >= 2:
                    sp.wait_ge(out_done, p - 1)
                for d in range(2):
                    sp.dma_start(y[:, p % 2, d, :], io["y"][d, p]).then_inc(y_in[p % 2], 16)
            for p in range(PAIRS):
                sp.wait_ge(out_done, p + 1)
                sp.dma_start(io["branch"][1, p], out[:, p % 2, :]).then_inc(sent[p % 2], 16)
            for b in range(2):
                sp.wait_ge(sent[b], 32)

        @block.tensor
        def _(pe):
            def head_sums(dst, src):
                for a, e in halves:
                    last = nc.tensor.matmul(dst[:, a:e], keep.head_ones[:], src[:, a:e], start=True, stop=True)
                return last

            for p in range(PAIRS):
                if p:
                    pe.wait_ge(th_done, p)
                for d in range(2):
                    for a, e in halves:
                        c = (2 + d) * W + p * P
                        last = nc.tensor.matmul(a_ps[:, d, a:e], keep.up[:, c:c + P], rk[:, T_AD, a:e], start=True, stop=True)
                last.then_inc(a_mm, 1)
                pe.wait_ge(y_sum, p + 1)
                if p:
                    pe.wait_ge(root_done, p)
                head_sums(mean_ps, y[:, p % 2, 0, :]).then_inc(mean_mm, 1)
                pe.wait_ge(work_done, p + 1)
                if p:
                    pe.wait_ge(bonus_done, p)
                head_sums(sum_ps, work).then_inc(bonus_mm, 1)
                pe.wait_ge(sq_done, p + 1)
                head_sums(mean_ps, sq).then_inc(var_mm, 1)

        @block.scalar
        def _(act):
            for p in range(PAIRS):
                act.wait_ge(a_mm, p + 1)
                if p:
                    act.wait_ge(work_done, p)
                for d in range(2):
                    last = nc.scalar.activation(th[:, d, :], a_ps[:, d, :], ACT.Tanh, scale=0.5,
                                                bias=keep.half_a0[:, d * 4 + p:d * 4 + p + 1])
                last.then_inc(th_done, 1)
                act.wait_ge(centred, p + 1)
                if p:
                    act.wait_ge(var_mm, p)
                nc.scalar.activation(sq[:], y[:, p % 2, 1, :], ACT.Square).then_inc(sq_done, 1)
                act.wait_ge(var_mm, p + 1)
                if p:
                    act.wait_ge(out_done, p)
                nc.scalar.activation(root[:], mean_ps[:], ACT.Sqrt, scale=1.0 / HEAD, bias=keep.eps[:, 1:2]).then_inc(root_done, 1)

        @block.vector
        def _(dve):
            link = Link(dve_link, dve)
            for p in range(PAIRS):
                b = p % 2
                dve.wait_ge(y_in[b], 32 * (p // 2 + 1))
                link(nc.vector.tensor_tensor(y[:, b, 0, :], y[:, b, 0, :], y[:, b, 1, :], ALU.add))
                dve.sem_inc(y_sum, 1)
                if p:
                    dve.wait_ge(bonus_mm, p)
                link(nc.vector.scalar_tensor_tensor(work[:], rk[:, T_K + p, 0:SEQ], col("r_k", p), keep.r[:, p, :],
                                                    ALU.mult, ALU.mult))
                dve.wait_ge(th_done, p + 1)
                link(nc.vector.tensor_tensor(bonus[:, b, :], th[:, 0, :], th[:, 1, :], ALU.add))
                link(nc.vector.tensor_scalar(bonus[:, b, :], bonus[:, b, :], keep.half_ka[:, p:p + 1],
                                             keep.rest_ka2[:, p:p + 1], ALU.mult, ALU.add))
                nc.vector.tensor_tensor(work[:], work[:], bonus[:, b, :], ALU.mult).then_inc(work_done, 1)
                dve.wait_ge(mean_mm, p + 1)
                nc.vector.scalar_tensor_tensor(y[:, b, 1, :], mean_ps[:], -1.0 / HEAD, y[:, b, 0, :],
                                               ALU.mult, ALU.add).then_inc(centred, 1)
                dve.wait_ge(centred, p + 1)
                dve.wait_ge(bonus_mm, p + 1)
                nc.vector.tensor_tensor(bonus[:, b, :], sum_ps[:], rk[:, T_V + p, 0:SEQ], ALU.mult).then_inc(bonus_done, 1)
                dve.wait_ge(bonus_done, p + 1)
                dve.wait_ge(root_done, p + 1)
                link(nc.vector.reciprocal(root[:], root[:]))
                if p >= 2:
                    dve.wait_ge(sent[b], 16)
                link(nc.vector.scalar_tensor_tensor(out[:, b, :], y[:, b, 1, :], col("gn_g", p), root[:], ALU.mult, ALU.mult))
                nc.vector.scalar_tensor_tensor(out[:, b, :], out[:, b, :], col("gn_b", p), bonus[:, b, :],
                                               ALU.add, ALU.add).then_inc(out_done, 1)
                dve.wait_ge(out_done, p + 1)


def normalise_latents(nc, sem, io, keep, stack):
    sb, ps = memory(nc, stack)
    lat, ql = sb("lat", [P, 4, NTOK]), sb("ql", [P, 3, SEQ])
    rope = sb("rope_k", [P, 2, SEQ])
    ones, sq = sb("lat_ones", [P, P]), sb("lat_sq", [P, 3, NTOK])
    root = sb("lat_root", [P, NTOK])
    val = sb("lat_val", [P, 2, NTOK])
    kr = sb("kr_val", [P, NTOK])
    sum_ps = ps("lat_ps", [P, 3 * 512])
    land, sq_done, sum_mm, root_done, val_done, hi_done, lo_done = map(
        sem, ("lat_land", "lat_sq_done", "lat_sum_mm", "lat_root_done", "lat_val_done", "lat_hi_done", "lat_lo_done"))
    dve_link, ones_done, kr_done = sem("lat_dve"), sem("lat_ones_done"), sem("kr_done")
    parts = [(2, NTOK, KV_LORA, lat, "g_kv", keep.kvn_hi, keep.kvn_lo), (3, SEQ, Q_LORA, ql, "g_q", keep.qn_hi, keep.qn_lo)]
    items = [(i, k) for i, part in enumerate(parts) for k in range(part[0])]
    with nc.Block() as block:
        @block.sync
        def _(sp):
            for i in range(4):
                sp.dma_start(lat[:, i, :], io["lat"][i]).then_inc(land, 16)
            for i in range(3):
                sp.dma_start(ql[:, i, :], io["ql"][i]).then_inc(land, 16)
            for part, src in ((0, io["rope"][0:32, :]), (1, io["rope"][32:64, :])):
                for q in (64, 96):
                    sp.dma_start(rope[q:q + 32, part, :], src).then_inc(land, 16)
            sp.dma_start(keep.rope_q[64:P, :], io["rope"]).then_inc(land, 16)
            sp.wait_ge(land, 12 * 16)

        @block.gpsimd
        def _(pool):
            nc.gpsimd.memset(ones[:], 1.0).then_inc(ones_done, 1)
            for n, (i, k) in enumerate(items):
                _, e, _, _, _, hi, lo = parts[i]
                pool.wait_ge(hi_done, n + 1)
                nc.gpsimd.tensor_tensor(lo[:, k, 0:e], keep.kvn[:, k, :] if i == 0 else val[:, n % 2, 0:e],
                                        hi[:, k, 0:e].bitcast(F32), ALU.subtract).then_inc(lo_done, 1)

        @block.tensor
        def _(pe):
            pe.wait_ge(ones_done, 1)
            for i, (tiles, end, *_) in enumerate(parts):
                pe.wait_ge(sq_done, i + 1)
                if i:
                    pe.wait_ge(root_done, i)
                for a in range(0, end, 512):
                    e = min(a + 512, end)
                    for k in range(tiles):
                        last = nc.tensor.matmul(sum_ps[:, a:e], ones[:], sq[:, k, a:e], start=k == 0, stop=k == tiles - 1)
                last.then_inc(sum_mm, 1)

        @block.scalar
        def _(act):
            act.wait_ge(land, 12 * 16)
            for i, (tiles, end, width, src, *_) in enumerate(parts):
                if i:
                    act.wait_ge(sum_mm, i)
                last = nc.scalar.activation(sq[:, 0:tiles, 0:end], src[:, 0:tiles, 0:end], ACT.Square)
                last.then_inc(sq_done, 1)
                act.wait_ge(sum_mm, i + 1)
                if i:
                    act.wait_ge(val_done, parts[0][0])
                nc.scalar.activation(root[:, 0:end], sum_ps[:, 0:end], ACT.Sqrt, scale=1.0 / width,
                                     bias=keep.eps[:, 0:1]).then_inc(root_done, 1)
                for n, (j, k) in enumerate(items):
                    if j == i:
                        act.wait_ge(val_done, n + 1)
                        nc.scalar.activation(parts[i][5][:, k, 0:end], keep.kvn[:, k, :] if i == 0 else val[:, n % 2, 0:end],
                                             ACT.Copy).then_inc(hi_done, 1)
            act.wait_ge(kr_done, 1)
            for b in range(2):
                last = nc.scalar.activation(keep.k_hi[b][64:P, :], kr[64:P, :], ACT.Copy)
            last.then_inc(kr_done, 1)

        @block.vector
        def _(dve):
            link = Link(dve_link, dve)
            dve.wait_ge(land, 12 * 16)
            link(nc.vector.memset(keep.rope_q[0:64, :], 1.0))
            for i, (tiles, end, width, src, g, *_) in enumerate(parts):
                dve.wait_ge(root_done, i + 1)
                link(nc.vector.reciprocal(root[:, 0:end], root[:, 0:end]))
                for n, (j, k) in enumerate(items):
                    if j == i:
                        if i and n >= 4:
                            dve.wait_ge(lo_done, n - 1)
                        dst = keep.kvn[:, k, :] if i == 0 else val[:, n % 2, 0:end]
                        nc.vector.scalar_tensor_tensor(dst, src[:, k, 0:end], cols_of(keep, g, k), root[:, 0:end],
                                                       ALU.mult, ALU.mult).then_inc(val_done, 1)
                dve.wait_ge(val_done, sum(p[0] for p in parts[:i + 1]))
            low = slice(64, P)
            link(nc.vector.tensor_tensor(kr[low, 0:SEQ], lat[low, 2, 0:SEQ], rope[low, 0, :], ALU.mult))
            link(nc.vector.tensor_tensor(lat[low, 3, 0:SEQ], lat[low, 3, 0:SEQ], rope[low, 1, :], ALU.mult))
            nc.vector.tensor_copy(kr[low, SEQ:NTOK], lat[low, 2, SEQ:NTOK])
            nc.vector.tensor_tensor(kr[low, 0:SEQ], kr[low, 0:SEQ], lat[low, 3, 0:SEQ], ALU.add).then_inc(kr_done, 1)
            dve.wait_ge(kr_done, 2)
            for b in range(2):
                last = nc.vector.tensor_tensor(keep.k_lo[b][low, :], kr[low, :], keep.k_hi[b][low, :].bitcast(F32), ALU.subtract)
            link(last)


def cols_of(keep, name, i):
    return keep.cols[:, COL[name] + i:COL[name] + i + 1]


def attention(nc, sem, io, keep, stack):
    sb, ps = memory(nc, stack)
    NQ = SEQ // P
    NW = 3 * P + 2 * NOPE
    AHEAD = 3
    PB = 4
    raw = sb("at_raw", [P, 2, NW])
    w_hi, w_lo = sb("at_w_hi", [P, 2, NW], F32R), sb("at_w_lo", [P, 2, NW], F32R)
    uv = sb("at_uv", [P, 2 * P])
    q_val = sb("at_q_val", [P, SEQ])
    q_hi, q_lo = sb("q_hi", [P, 2, SEQ], F32R), sb("q_lo", [P, 2, SEQ], F32R)
    v_hi, v_lo = sb("v_hi", [P, NT, P], F32R), sb("v_lo", [P, NT, P], F32R)
    probs = sb("probs", [P, PB, NTOK])
    pt_hi, pt_lo = sb("pt_hi", [P, NT, 4 * P], F32R), sb("pt_lo", [P, NT, 4 * P], F32R)
    top, total = sb("top", [P, PB, 1]), sb("total", [P, PB, 1])
    o_sb = sb("o_sb", [P, 2, 512])
    s_ps, ring = ps("s_ps", [P, 2, 3 * 512]), ps("ring_ps", [P, 2, 512])
    names = ("uv_land", "w_hi_done", "w_lo_done", "filled", "hi_done", "freed", "q_lo", "s_mm", "top_done",
             "exp_done", "total_done", "probs_done", "dve")
    S = {n: sem(f"at_{n}") for n in names}
    w_land = [sem(f"at_w_land{b}") for b in range(2)]
    o_sent = [sem(f"at_o_sent{b}") for b in range(2)]

    TURNS = [(0, 4), (4, 8), (8, NT)]
    VALUES = [("V", a, b) for a, b in ((0, 3), (3, 6), (6, 8), (8, NT))]

    def head_items(e):
        return ([("Q", e, 0, a, a + 512) for a in (0, 512)] +
                [("K", e, 0, a, min(a + 512, NTOK)) for a in range(0, NTOK, 512)])

    FIRST = head_items(-1)

    def extras(e, q, more):
        if e == 0:
            mine = head_items(0)
            return {0: VALUES[0:2], 1: VALUES[2:4], 2: mine[0:2], 3: mine[2:4], 4: mine[4:5]}.get(q, [])
        mine = head_items(1) if more else []
        return {1: mine[0:2], 2: mine[2:3], 3: mine[3:4], 4: mine[4:5]}.get(q, [])

    def step_items(e, q, more):
        made = extras(e, q, more)
        return ([("T", e, q, a, b) for a, b in TURNS] + made[:1] + ([("O", e, q // 4)] if q % 4 == 3 else []) + made[1:])

    def order(more):
        return [item for e in range(2) for q in range(NQ) for item in step_items(e, q, more)]

    ROUND = len(order(True))
    assert ROUND % 2 == 0

    def number(p, item, more=True):
        if item in FIRST:
            return FIRST.index(item), FIRST.index(item) % 2
        i = len(FIRST) + order(more).index(item)
        return i + p * ROUND, i % 2

    def steps(p, more):
        for e in range(2):
            for q in range(NQ):
                yield p * 2 + e, e, q

    def ahead(p, e, q, by, more):
        n = e * NQ + q + by
        if n >= 2 * NQ and not more:
            return None
        return p * 2 + n // NQ, (n // NQ) % 2, n % NQ

    def rounds(eng, link, body):
        with eng.Fori(0, PAIRS - 1) as p:
            if link is not None:
                link.enter(p, 2 * NQ)
            body(p, True)
        if link is not None:
            link.leave(PAIRS - 1)
        body(PAIRS - 1, False)

    with nc.Block() as block:
        @block.sync
        def _(sp):
            def load(h, e):
                sp.dma_start(raw[:, e, 0:3 * P], io["uq"][bass.ds(h, 1)].rearrange("a p n -> p (a n)")).then_inc(w_land[e], 16)
                sp.dma_start(raw[:, e, 3 * P:NW], io["uk"][bass.ds(h, 1)].rearrange("a p n -> p (a n)")).then_inc(w_land[e], 16)

            def load_uv(p):
                sp.dma_start(uv[:], io["uv"][bass.ds(p, 1)].rearrange("a p n -> p (a n)")).then_inc(S["uv_land"], 16)

            def body(p, more):
                for e in range(2):
                    h = p * 2 + e
                    if more:
                        sp.wait_ge(S["w_lo_done"], h + 1)
                        load(h + 2, e)
                    if more and e == 0:
                        sp.wait_ge(S["filled"], number(p, VALUES[-1])[0] + 1)
                        load_uv(p + 1)
                    for half in range(2):
                        sp.wait_ge(S["hi_done"], number(p, ("O", e, half), more)[0] + 1)
                        sp.dma_start(io["branch"][0, bass.ds(p, 1), e * HEAD:(e + 1) * HEAD, half * 512:(half + 1) * 512]
                                     .rearrange("a p t -> p (a t)"),
                                     o_sb[e * HEAD:(e + 1) * HEAD, half, :]).then_inc(o_sent[half], 16)

            load(0, 0)
            load_uv(0)
            load(1, 1)
            rounds(sp, None, body)
            for half in range(2):
                sp.wait_ge(o_sent[half], 16 + 16 * HEADS)

        @block.gpsimd
        def _(pool):
            def split_lo(h, e):
                pool.wait_ge(S["w_hi_done"], h + 1)
                nc.gpsimd.tensor_tensor(w_lo[:, e, :], raw[:, e, :], w_hi[:, e, :].bitcast(F32),
                                        ALU.subtract).then_inc(S["w_lo_done"], 1)

            def query_lo(p, item, h, e, more):
                _, _, _, a, b = item
                pool.wait_ge(S["hi_done"], number(p, item, more)[0] + 1)
                nc.gpsimd.tensor_tensor(q_lo[:, e, a:b], q_val[:, a:b], q_hi[:, e, a:b].bitcast(F32),
                                        ALU.subtract).then_inc(S["q_lo"], 1)

            def normalise(h, q):
                pool.wait_ge(S["total_done"], h * NQ + q + 1)
                b = q % PB
                nc.gpsimd.tensor_tensor(probs[:, b, :], probs[:, b, :], total[:, b, :].broadcast_to([P, NTOK]),
                                        ALU.mult).then_inc(S["probs_done"], 1)

            def body(p, more):
                for h, e, q in steps(p, more):
                    later = ahead(p, e, q, 1, more)
                    if later:
                        normalise(later[0], later[2])
                    if q == 0 and (more or e == 0):
                        split_lo(h + 1, 1 - e)
                    for item in extras(e, q, more):
                        if item[0] == "Q":
                            query_lo(p, item, h + 1, 1 - e, more)

            pool.sem_inc(S["q_lo"], 2)
            split_lo(0, 0)
            for item in FIRST[0:2]:
                query_lo(0, item, 0, 0, True)
            normalise(0, 0)
            rounds(pool, None, body)

        @block.tensor
        def _(pe):
            def passes(out, ws, hs, first, end):
                for n, (w, x) in enumerate(((ws[0], hs[0]), (ws[0], hs[1]), (ws[1], hs[0]))):
                    last = nc.tensor.matmul(out, w, x, start=first and n == 0, stop=end and n == 2)
                return last

            def fill(p, item, h, e, more):
                i, bank = number(p, item, more)
                pe.wait_ge(S["freed"], i + 1)
                if item[0] == "V":
                    for t in range(item[1], item[2]):
                        for k in range(2):
                            last = nc.tensor.matmul(ring[:, bank, (t - item[1]) * P:(t - item[1] + 1) * P],
                                                    keep.kvn[:, k, t * P:(t + 1) * P], uv[:, k * P:(k + 1) * P],
                                                    start=k == 0, stop=k == 1)
                    last.then_inc(S["filled"], 1)
                    return
                _, _, _, a, b = item
                if item[0] == "Q":
                    for k in range(3):
                        last = passes(ring[:, bank, :], (w_hi[:, e, k * P:(k + 1) * P], w_lo[:, e, k * P:(k + 1) * P]),
                                      (keep.qn_hi[:, k, a:b], keep.qn_lo[:, k, a:b]), k == 0, k == 2)
                else:
                    for k in range(2):
                        c = 3 * P + k * NOPE
                        last = passes(ring[0:HEAD, bank, 0:b - a], (w_hi[:, e, c:c + NOPE], w_lo[:, e, c:c + NOPE]),
                                      (keep.kvn_hi[:, k, a:b], keep.kvn_lo[:, k, a:b]), k == 0, k == 1)
                last.then_inc(S["filled"], 1)

            def scores(h, e, q, last_key, piece=None):
                if q == 0 and not piece:
                    pe.wait_ge(S["freed"], last_key + 3)
                    pe.wait_ge(S["q_lo"], h * 2 + 4)
                if not piece:
                    pe.wait_ge(S["exp_done"], h * NQ + q + 1)
                c = q * P
                for a in range(0, NTOK, 512) if piece is None else [piece * 512]:
                    b = min(a + 512, NTOK)
                    last = passes(s_ps[:, q % 2, a:b], (q_hi[:, e, c:c + P], q_lo[:, e, c:c + P]),
                                  (keep.k_hi[e][:, a:b], keep.k_lo[e][:, a:b]), True, True)
                if b == NTOK:
                    last.then_inc(S["s_mm"], 1)

            def turn(p, item, more):
                _, e, q, a, b = item
                i, bank = number(p, item, more)
                pe.wait_ge(S["freed"], i + 1)
                for t in range(a, b):
                    last = nc.tensor.transpose(ring[:, bank, (t - a) * P:(t - a + 1) * P],
                                               probs[:, q % PB, t * P:(t + 1) * P], keep.ident[:])
                last.then_inc(S["filled"], 1)

            def outputs(p, item, more, newest):
                i, bank = number(p, item, more)
                pe.wait_ge(S["freed"], i + 1 + newest)
                for t in range(NT):
                    last = passes(ring[:, bank, :], (v_hi[:, t, :], v_lo[:, t, :]), (pt_hi[:, t, :], pt_lo[:, t, :]),
                                  t == 0, t == NT - 1)
                last.then_inc(S["filled"], 1)

            def body(p, more):
                for h, e, q in steps(p, more):
                    later = ahead(p, e, q, AHEAD, more)
                    last_key = number(p, head_items(e)[-1], more)[0] if q >= NQ - AHEAD and later else None
                    items = step_items(e, q, more)
                    place = {0: 0, 1: 2, 2: 3} if q % 4 == 3 else {0: 0, 1: 1, 2: 3}
                    for n, item in enumerate(items + [None] * (4 - len(items))):
                        if item and item[0] == "T":
                            if n == 0:
                                pe.wait_ge(S["probs_done"], h * NQ + q + 1)
                            turn(p, item, more)
                        elif item and item[0] == "O":
                            outputs(p, item, more, 1 if n == 3 else 0)
                        elif item:
                            if item == VALUES[0]:
                                pe.wait_ge(S["uv_land"], p * 16 + 16)
                            if item[0] == "Q" and item[3] == 0:
                                pe.wait_ge(S["w_lo_done"], h + 2)
                            fill(p, item, h + 1, 1 - e, more)
                        for piece in place:
                            if place[piece] == n and later:
                                scores(*later, last_key, piece=piece)

            pe.wait_ge(S["w_lo_done"], 1)
            for item in FIRST:
                fill(0, item, 0, 0, True)
            for q in range(AHEAD):
                scores(0, 0, q, number(0, FIRST[-1])[0])
            rounds(pe, None, body)

        @block.scalar
        def _(act):
            def split_hi(h, p, e):
                act.wait_ge(w_land[e], p * 32 + 32)
                nc.scalar.activation(w_hi[:, e, :], raw[:, e, :], ACT.Copy).then_inc(S["w_hi_done"], 1)

            def hi(p, item, e, more):
                i, bank = number(p, item, more)
                if item[0] == "Q":
                    act.wait_ge(S["freed"], i + 3)
                    _, _, _, a, b = item
                    dst, src = q_hi[:, e, a:b], q_val[:, a:b]
                elif item[0] == "K":
                    act.wait_ge(S["filled"], i + 1)
                    _, _, _, a, b = item
                    dst, src = keep.k_hi[e][0:HEAD, a:b], ring[0:HEAD, bank, 0:b - a]
                else:
                    act.wait_ge(S["filled"], i + 1)
                    a, b = item[-2:]
                    src = ring[:, bank, 0:(b - a) * P].rearrange("p (t c) -> p t c", c=P)
                    dst = v_hi[:, a:b, :] if item[0] == "V" else pt_hi[:, a:b, (item[2] % 4) * P:(item[2] % 4 + 1) * P]
                nc.scalar.activation(dst, src, ACT.Copy).then_inc(S["hi_done"], 1)

            def exponentials(h, q):
                act.wait_ge(S["top_done"], h * NQ + q + 1)
                b = q % PB
                nc.scalar.activation(probs[:, b, :], s_ps[:, q % 2, 0:NTOK], ACT.Exp, scale=SCALE,
                                     bias=top[:, b, :], accum_out=total[:, b, :]).then_inc(S["exp_done"], 1)

            def body(p, more):
                for h, e, q in steps(p, more):
                    if q == 0 and (more or e == 0):
                        split_hi(h + 1, p + e, 1 - e)
                    for n, item in enumerate(step_items(e, q, more)):
                        if item[0] == "O":
                            out(p, h, e, q // 4, more)
                        else:
                            hi(p, item, e if item[0] == "T" else 1 - e, more)
                        later = ahead(p, e, q, AHEAD - 1, more)
                        if n == 2 and later:
                            exponentials(later[0], later[2])

            def out(p, h, e, half, more):
                i, bank = number(p, ("O", e, half), more)
                act.wait_ge(S["filled"], i + 1)
                act.wait_ge(o_sent[half], h * 16 + 16)
                part = slice(e * HEAD, (e + 1) * HEAD)
                nc.scalar.activation(o_sb[part, half, :], ring[part, bank, :], ACT.Copy).then_inc(S["hi_done"], 1)

            for half in range(2):
                act.sem_inc(o_sent[half], 16)
            act.sem_inc(S["exp_done"], 2)
            split_hi(0, 0, 0)
            for item in FIRST:
                hi(0, item, 0, True)
            for q in range(AHEAD - 1):
                exponentials(0, q)
            rounds(act, None, body)

        @block.vector
        def _(dve):
            link = Link(S["dve"], dve)

            def lo(p, item, h, e, more):
                i, bank = number(p, item, more)
                if item[0] == "Q":
                    _, _, _, a, b = item
                    dve.wait_ge(S["filled"], i + 1)
                    dve.wait_ge(S["q_lo"], h * 2 + a // 512 + 1)
                    nc.vector.tensor_tensor(q_val[:, a:b], ring[:, bank, :], keep.rope_q[:, a:b],
                                            ALU.mult).then_inc(S["freed"], 1)
                    return
                dve.wait_ge(S["hi_done"], i + 1)
                if item[0] == "K":
                    _, _, _, a, b = item
                    part = (slice(0, HEAD), slice(a, b))
                    dst, src, hi = keep.k_lo[e][part], ring[0:HEAD, bank, 0:b - a], keep.k_hi[e][part]
                else:
                    a, b = item[-2:]
                    src = ring[:, bank, 0:(b - a) * P].rearrange("p (t c) -> p t c", c=P)
                    if item[0] == "V":
                        dst, hi = v_lo[:, a:b, :], v_hi[:, a:b, :]
                    else:
                        part = (slice(None), slice(a, b), slice((item[2] % 4) * P, (item[2] % 4 + 1) * P))
                        dst, hi = pt_lo[part], pt_hi[part]
                nc.vector.tensor_tensor(dst, src, hi.bitcast(F32), ALU.subtract).then_inc(S["freed"], 1)

            def maximum(h, q):
                b = q % PB
                dve.wait_ge(S["s_mm"], h * NQ + q + 1)
                link(nc.vector.reduce_max(top[:, b, :], s_ps[:, q % 2, 0:NTOK], AX.X))
                nc.vector.tensor_scalar(top[:, b, :], top[:, b, :], -SCALE, None, ALU.mult).then_inc(S["top_done"], 1)

            def invert(h, q):
                dve.wait_ge(S["exp_done"], h * NQ + q + 3)
                nc.vector.reciprocal(total[:, q % PB, :], total[:, q % PB, :]).then_inc(S["total_done"], 1)

            def body(p, more):
                for h, e, q in steps(p, more):
                    items = step_items(e, q, more)
                    for n, item in enumerate(items):
                        if item[0] == "O":
                            dve.wait_ge(S["hi_done"], number(p, item, more)[0] + 1)
                            dve.sem_inc(S["freed"], 1)
                        elif item[0] == "T":
                            lo(p, item, h, e, more)
                        else:
                            lo(p, item, h + 1, 1 - e, more)
                        later = ahead(p, e, q, 1, more)
                        if n == 0 and later:
                            invert(later[0], later[2])
                        later = ahead(p, e, q, AHEAD, more)
                        if n == min(3, len(items) - 1) - (items[-1][0] == "O" and len(items) == 4) and later:
                            maximum(later[0], later[2])

            dve.sem_inc(S["freed"], 2)
            for item in FIRST:
                lo(0, item, 0, 0, True)
            for q in range(AHEAD):
                maximum(0, q)
            invert(0, 0)
            rounds(dve, link, body)


def gate_branches(nc, sem, io, keep, stack):
    sb, ps = memory(nc, stack)
    ring = WeightRing(nc, sem, stack, "gb", raws=1)
    out_ps = ps("gb_ps", [P, 3, 1024])
    pad = sb("conv_u", [P, SEQ + 2])
    conv = sb("conv_sum", [P, SEQ])
    th, val = sb("gate_th", [P, SEQ]), sb("gate_val", [P, SEQ])
    y = sb("branch_y", [P, 2, SEQ])
    cols = keep.cols
    S = {n: sem(f"gb_{n}") for n in ("h_in", "drained", "in_done", "th_done", "val_done", "hi_done", "lo_done",
                                     "link", "y_used", "y_in")}
    IN, C, B, GATES = 0, 1, 2, (3, 4, 5)
    ORDER = (1, 0, 2)
    def lo_part(pool, c, g):
        hi, lo = keep.branch[ORDER[g]]
        pool.wait_ge(S["hi_done"], c * 3 + g + 1)
        at = (slice(None), bass.ds(c, 1), slice(None))
        nc.gpsimd.tensor_tensor(lo[at].rearrange("p a t -> p (a t)"), val[:],
                                hi[at].rearrange("p a t -> p (a t)").bitcast(F32), ALU.subtract).then_inc(S["lo_done"], 1)

    def evacuate(act, c, t):
        if t == IN:
            act.wait_ge(ring.used, c * 6 + t + 3)
            act.wait_ge(S["val_done"], c * 3 + 1)
            nc.scalar.activation(th[:], out_ps[:, t % 3, :], ACT.Copy).then_inc(S["in_done"], 1)
        if t in GATES:
            g = t - 3
            act.wait_ge(ring.used, c * 6 + t + 3)
            if g:
                act.wait_ge(S["val_done"], c * 3 + g + 1)
            else:
                act.wait_ge(S["drained"], c * 6 + 5)
            nc.scalar.activation(th[:], out_ps[:, t % 3, :], ACT.Tanh, scale=0.5).then_inc(S["th_done"], 1)
            act.wait_ge(S["val_done"], c * 3 + g + 2)
            hi = keep.branch[ORDER[g]][0]
            nc.scalar.activation(hi[:, bass.ds(c, 1), :].rearrange("p a t -> p (a t)"), val[:],
                                 ACT.Copy).then_inc(S["hi_done"], 1)

    with nc.Block() as block:
        @block.sync
        def _(sp):
            for k in range(KD):
                for part, h in enumerate((keep.h_hi, keep.h_lo)):
                    sp.dma_start(h[:, k, :].bitcast(F32), io["h"][part, :, k, :]).then_inc(S["h_in"], 16)
            with sp.Fori(0, PAIRS) as c:
                for t in range(6):
                    ring.load(sp, io["w_in"][c * 6 + (T_F + t), :, :], c * 6 + t, t % 2)
                    if t == 2:
                        sp.wait_ge(S["y_used"], c + 1)
                        sp.dma_start(y[:], io["branch"][:, bass.ds(c, 1)].rearrange("b a p t -> p (a b) t")).then_inc(S["y_in"], 16)

        @block.gpsimd
        def _(pool):
            pool.sem_inc(ring.lo_made, 2)
            pool.sem_inc(S["lo_done"], 1)
            def body(c, more):
                for t in range(6):
                    if t < 5 or more:
                        ring.split_lo(pool, c * 6 + t + 1, (t + 1) % 2)
                    if t in GATES:
                        lo_part(pool, c, t - 3)

            ring.split_lo(pool, 0, 0)
            with pool.Fori(0, PAIRS - 1) as c:
                body(c, True)
            body(PAIRS - 1, False)

        @block.tensor
        def _(pe):
            pe.sem_inc(ring.used, 2)
            with pe.Fori(0, PAIRS) as c:
                for t in range(6):
                    ring.wait(pe, c * 6 + t)
                    pe.wait_ge(S["drained"], c * 6 + t + 1)
                    outs = [(out_ps[:, t % 3, a:a + 512], a, a + 512) for a in (0, 512)]
                    landed = (lambda k: pe.wait_ge(S["h_in"], 32 * (k + 1))) if t == 0 else None
                    ring.products(t % 2, keep.h_hi, keep.h_lo, outs, before=landed).then_inc(ring.used, 1)

        @block.scalar
        def _(act):
            def body(c, more):
                for t in range(6):
                    if t < 5 or more:
                        ring.split_hi(act, c * 6 + t + 1, (t + 1) % 2, c * 3 + (t + 1) // 2)
                    evacuate(act, c, t)

            ring.split_hi(act, 0, 0, 0)
            with act.Fori(0, PAIRS - 1) as c:
                body(c, True)
            body(PAIRS - 1, False)

        @block.vector
        def _(dve):
            link = Link(S["link"], dve)
            dve.sem_inc(S["drained"], 3)
            dve.sem_inc(S["val_done"], 1)
            dve.sem_inc(S["y_used"], 1)
            link(nc.vector.memset(pad[:], 0.0))
            with dve.Fori(0, PAIRS) as c:
                link.enter(c, 8)
                col = lambda name, i=0: cols[:, bass.ds(c + (COL[name] + i), 1)]
                dve.wait_ge(S["in_done"], c + 1)
                dve.sem_inc(S["drained"], 1)
                dve.wait_ge(ring.used, c * 6 + C + 3)
                link(nc.vector.tensor_tensor(pad[:, 1:SEQ + 1], out_ps[:, C % 3, :], th[:], ALU.mult))
                dve.sem_inc(S["drained"], 1)
                link(nc.vector.tensor_scalar(conv[:], pad[:, 0:SEQ], col("conv_w"), col("conv_b"), ALU.mult, ALU.add))
                link(nc.vector.scalar_tensor_tensor(conv[:], pad[:, 1:SEQ + 1], col("conv_w", 4), conv[:], ALU.mult, ALU.add))
                link(nc.vector.scalar_tensor_tensor(conv[:], pad[:, 2:SEQ + 2], col("conv_w", 8), conv[:], ALU.mult, ALU.add))
                dve.wait_ge(ring.used, c * 6 + B + 3)
                link(nc.vector.tensor_tensor(conv[:], out_ps[:, B % 3, :], conv[:], ALU.mult))
                dve.sem_inc(S["drained"], 1)
                for g in range(3):
                    t = 3 + g
                    dve.wait_ge(S["th_done"], c * 3 + g + 1)
                    link(nc.vector.scalar_tensor_tensor(th[:], th[:], 1.0, out_ps[:, t % 3, :], ALU.add, ALU.mult))
                    dve.sem_inc(S["drained"], 1)
                    dve.wait_ge(S["lo_done"], c * 3 + g + 1)
                    src = conv[:] if g == 0 else y[:, g - 1, :]
                    if g:
                        dve.wait_ge(S["y_in"], c * 16 + 16)
                    nc.vector.scalar_tensor_tensor(val[:], src, 0.5, th[:], ALU.mult, ALU.mult).then_inc(S["val_done"], 1)
                    dve.wait_ge(S["val_done"], c * 3 + g + 2)
                dve.sem_inc(S["y_used"], 1)
            link.leave(PAIRS)


def merge(nc, sem, io, keep, stack):
    sb, ps = memory(nc, stack)
    ring = WeightRing(nc, sem, stack, "mg", D + W, raws=1)
    out_ps = ps("mg_ps", [P, 2, 2, 1024])
    th, term = sb("mg_th", [P, 2, SEQ]), sb("mg_term", [P, SEQ])
    acc = sb("mg_acc", [P, SEQ])
    S = {n: sem(f"mg_{n}") for n in ("th_done", "drained", "link", "acc_done", "summed")}
    sent = sem("mg_sent")
    TILES = 6
    def gate(act, i, t):
        act.wait_ge(ring.used, i * TILES + t + 3)
        act.wait_ge(S["drained"], i * TILES + t + 1)
        nc.scalar.activation(th[:, t % 2, :], out_ps[:, t % 2, 0, :], ACT.Tanh, scale=0.5).then_inc(S["th_done"], 1)

    def store(act, i, b):
        act.wait_ge(S["acc_done"], i * 2 + b + 1)
        act.dma_start(io["merged"][bass.ds(i * 2 + b, 1)].rearrange("a p t -> p (a t)"), acc[:]).then_inc(sent, 16)

    with nc.Block() as block:
        @block.sync
        def _(sp):
            with sp.Fori(0, KD // 2) as i:
                for t in range(TILES):
                    ring.load(sp, io["w_merge"][i * TILES + t, :, :], i * TILES + t, t % 2)

        @block.gpsimd
        def _(pool):
            pool.sem_inc(ring.lo_made, 2)
            with pool.Fori(0, KD // 2) as i:
                for t in range(TILES):
                    ring.split_lo(pool, i * TILES + t, t % 2)

        @block.tensor
        def _(pe):
            pe.sem_inc(ring.used, 2)
            with pe.Fori(0, KD // 2) as i:
                for t in range(TILES):
                    ring.wait(pe, i * TILES + t)
                    pe.wait_ge(S["drained"], i * TILES + t + 1)
                    b = t % 2
                    outs = lambda j: [(out_ps[:, b, j, a:a + 512], a, a + 512) for a in (0, 512)]
                    ring.products(b, keep.h_hi, keep.h_lo, outs(0))
                    ring.products(b, *keep.branch[t % 3], outs(1), at=D, tiles=PAIRS).then_inc(ring.used, 1)

        @block.scalar
        def _(act):
            act.sem_inc(sent, 16)
            def body(i, more):
                for t in range(TILES):
                    if t < TILES - 1 or more:
                        ring.split_hi(act, i * TILES + t + 1, (t + 1) % 2, i * 3 + (t + 1) // 2)
                    gate(act, i, t)
                    if t % 3 == 2:
                        store(act, i, t // 3)

            ring.split_hi(act, 0, 0, 0)
            with act.Fori(0, KD // 2 - 1) as i:
                body(i, True)
            body(KD // 2 - 1, False)
            act.wait_ge(sent, 16 + 16 * KD)

        @block.vector
        def _(dve):
            link = Link(S["link"], dve)
            dve.sem_inc(S["drained"], 2)
            with dve.Fori(0, KD // 2) as i:
                link.enter(i, 6)
                for t in range(TILES):
                    b = t // 3
                    dve.wait_ge(S["th_done"], i * TILES + t + 1)
                    if t % 3 == 0:
                        dve.wait_ge(sent, (i * 2 + b) * 16 + 16)
                    dst = term[:] if t % 3 else acc[:]
                    link(nc.vector.scalar_tensor_tensor(dst, th[:, t % 2, :], 1.0, out_ps[:, t % 2, 1, :],
                                                        ALU.add, ALU.mult))
                    dve.sem_inc(S["drained"], 1)
                    if t % 3:
                        last = nc.vector.tensor_tensor(acc[:], acc[:], term[:], ALU.add)
                        if t % 3 == 2:
                            last.then_inc(S["acc_done"], 1)
                            dve.wait_ge(S["acc_done"], i * 2 + b + 1)
                        else:
                            last.then_inc(S["summed"], 1)
                            dve.wait_ge(S["summed"], i * 2 + b + 1)
            link.leave(KD // 2)


def project_out(nc, sem, io, keep, stack):
    sb, ps = memory(nc, stack)
    RAWS, FIRST = 4, 3
    raw = sb("po_raw", [P, RAWS, D])
    w_hi, w_lo = sb("po_w_hi", [P, KD, D], F32R), sb("po_w_lo", [P, KD, D], F32R)
    m_hi, m_lo = sb("po_m_hi", [P, KD, SEQ], F32R), sb("po_m_lo", [P, KD, SEQ], F32R)
    gate, wide = sb("po_gate", [P, D]), sb("po_wide", [P, KD, P])
    res, x_in, junk = sb("po_res", [P, 2, D]), sb("po_x", [P, 2, D]), sb("po_junk", [P, D])
    ss = sb("po_ss", [P, 2, 2])
    out_ps = ps("po_ps", [P, FIRST, 1024])
    gate_ps = ps("po_gate_ps", [P, 1024])
    S = {n: sem(f"po_{n}") for n in ("hi_done", "w_parts", "m_parts", "wide_done", "gate_mm", "mm", "sq_done",
                                     "root_done", "res_done", "link")}
    land = [sem(f"po_land{b}") for b in range(RAWS)]
    x_land = [sem(f"po_x_land{b}") for b in range(2)]
    sent = [sem(f"po_sent{b}") for b in range(2)]
    items = [(kind, k) for k in range(KD) for kind in ("w", "m")]
    NQ = SEQ // P
    with nc.Block() as block:
        @block.sync
        def _(sp):
            for n, (kind, k) in enumerate(items):
                if n >= RAWS:
                    sp.wait_ge(S["w_parts" if kind == "w" else "m_parts"], (n - RAWS) // 2 + 1)
                src = io["w_out"][k * P:(k + 1) * P, :] if kind == "w" else io["merged"][k]
                sp.dma_start(raw[:, n % RAWS, :], src).then_inc(land[n % RAWS], 16)
            for t in range(NQ):
                if t >= 2:
                    sp.wait_ge(S["res_done"], t - 1)
                sp.dma_start(x_in[:, t % 2, :], io["x"][t * P:(t + 1) * P, :]).then_inc(x_land[t % 2], 16)
            for b in range(2):
                sp.wait_ge(sent[b], 16 * NQ // 2)

        @block.gpsimd
        def _(pool):
            for n, (kind, k) in enumerate(items):
                if kind == "w":
                    pool.wait_ge(S["hi_done"], n + 1)
                    nc.gpsimd.tensor_tensor(w_lo[:, k, :], raw[:, n % RAWS, :], w_hi[:, k, :].bitcast(F32),
                                            ALU.subtract).then_inc(S["w_parts"], 1)

        @block.scalar
        def _(act):
            for n, (kind, k) in enumerate(items):
                act.wait_ge(land[n % RAWS], 16 * (n // RAWS + 1))
                nc.scalar.activation((w_hi if kind == "w" else m_hi)[:, k, :], raw[:, n % RAWS, :], ACT.Copy).then_inc(S["hi_done"], 1)
            for t in range(NQ):
                act.wait_ge(S["mm"], t + 1)
                if t >= 2:
                    act.wait_ge(S["res_done"], t - 1)
                nc.scalar.activation(junk[:], out_ps[:, t % FIRST, :], ACT.Square, scale=0.5,
                                     accum_out=ss[:, t % 2, 0:1]).then_inc(S["sq_done"], 1)
                act.wait_ge(S["sq_done"], t + 1)
                nc.scalar.activation(ss[:, t % 2, 1:2], ss[:, t % 2, 0:1], ACT.Sqrt, scale=1.0 / D,
                                     bias=keep.eps[:, 0:1]).then_inc(S["root_done"], 1)
                act.wait_ge(S["res_done"], t + 1)
                act.dma_start(io["out"][t * P:(t + 1) * P, :], res[:, t % 2, :]).then_inc(sent[t % 2], 16)

        @block.tensor
        def _(pe):
            pe.wait_ge(S["wide_done"], 1)
            for k in range(KD):
                last = nc.tensor.matmul(gate_ps[:, k * P:(k + 1) * P], wide[:, k, :], keep.ident[:], start=True, stop=True)
            last.then_inc(S["gate_mm"], 1)

            def products(t, k):
                for m, w in ((m_hi, w_hi), (m_hi, w_lo), (m_lo, w_hi)):
                    for a in (0, 512):
                        last = nc.tensor.matmul(out_ps[:, t % FIRST, a:a + 512], m[:, k, t * P:(t + 1) * P], w[:, k, a:a + 512],
                                                start=k == 0 and m is m_hi and w is w_hi, stop=k == KD - 1 and m is m_lo)
                if k == KD - 1:
                    last.then_inc(S["mm"], 1)

            for k in range(KD):
                pe.wait_ge(S["w_parts"], k + 1)
                pe.wait_ge(S["m_parts"], k + 1)
                for t in range(FIRST):
                    products(t, k)
            for t in range(FIRST, NQ):
                pe.wait_ge(S["res_done"], t - FIRST + 1)
                for k in range(KD):
                    products(t, k)

        @block.vector
        def _(dve):
            link = Link(S["link"], dve)
            link(nc.vector.memset(wide[:], 1.0))
            for k in range(KD):
                last = nc.vector.tensor_scalar(wide[:, k, :], wide[:, k, :], keep.gate_cols[:, k:k + 1], None, ALU.mult)
            last.then_inc(S["wide_done"], 1)
            for n, (kind, k) in enumerate(items):
                if kind == "m":
                    dve.wait_ge(S["hi_done"], n + 1)
                    nc.vector.tensor_tensor(m_lo[:, k, :], raw[:, n % RAWS, :], m_hi[:, k, :].bitcast(F32),
                                            ALU.subtract).then_inc(S["m_parts"], 1)
            dve.wait_ge(S["gate_mm"], 1)
            link(nc.vector.tensor_copy(gate[:], gate_ps[:]))
            for t in range(NQ):
                dve.wait_ge(S["root_done"], t + 1)
                link(nc.vector.reciprocal(ss[:, t % 2, 1:2], ss[:, t % 2, 1:2]))
                if t >= 2:
                    dve.wait_ge(sent[t % 2], 16 * (t // 2))
                link(nc.vector.scalar_tensor_tensor(res[:, t % 2, :], out_ps[:, t % FIRST, :], ss[:, t % 2, 1:2], gate[:],
                                                    ALU.mult, ALU.mult))
                dve.wait_ge(x_land[t % 2], 16 * (t // 2 + 1))
                nc.vector.tensor_tensor(res[:, t % 2, :], res[:, t % 2, :], x_in[:, t % 2, :], ALU.add).then_inc(S["res_done"], 1)


def phases(nc, io, keep):
    def run(phase, stack):
        sems = []

        def sem(name):
            sems.append(nc.alloc_semaphore(name))
            return sems[-1]

        phase(nc, sem, io, keep, stack)
        nc.clear_and_free_semaphores(sems)
        nc.all_engine_barrier()

    with ExitStack() as first:
        sb, _ = memory(nc, first)
        keep.rk = sb("rk", [P, T_KV, NTOK])
        keep.r = sb("r", [P, PAIRS, SEQ])
        with ExitStack() as hbuf:
            sbh, _ = memory(nc, hbuf)
            keep.h_hi, keep.h_lo = sbh("h_hi", [P, KD, NTOK], F32R), sbh("h_lo", [P, KD, NTOK], F32R)
            with ExitStack() as own:
                run(start, own)
            with ExitStack() as own:
                run(project, own)
        keep.up = sb("up", [P, 4 * W])
        keep.head_ones, keep.ones = sb("head_ones", [P, P]), sb("ones", [P, P])
        keep.half_w0, keep.half_a0 = sb("half_w0", [P, 8]), sb("half_a0", [P, 8])
        keep.half_ka, keep.rest_ka, keep.rest_ka2 = (sb(n, [P, 4]) for n in ("half_ka", "rest_ka", "rest_ka2"))
        with ExitStack() as own:
            sb, _ = memory(nc, own)
            keep.kk = sb("kk", [P, PAIRS, NTOK])
            keep.state = sb("state", [P, 2 * PAIRS, P])
            keep.nt, keep.bt, keep.dt, keep.et, keep.x1t = (
                [sb(f"{name}{s}", [P, 4, P]) for s in range(2)] for name in ("nt", "bt", "dt", "et", "x1t"))
            keep.wp = [[sb(f"wp{s}{j}", [P, 4, P]) for j in range(6)] for s in range(2)]
            keep.bkz = [sb(f"bkz{s}", [P, 2, 2, 2, P]) for s in range(2)]
            keep.m_strict, keep.m_incl = sb("m_strict", [P, 4, P], U8), sb("m_incl", [P, 4, P], U8)
            keep.m_level = [sb(f"m_level{j}", [P, 4, P], U8) for j in range(7)]
            with ExitStack() as prep:
                run(prepare_rwkv, prep)
            with ExitStack() as prep:
                run(recurrence, prep)
        with ExitStack() as own:
            run(finish_rwkv, own)
    with ExitStack() as second:
        sb, _ = memory(nc, second)
        keep.kvn, keep.rope_q = sb("kvn", [P, 2, NTOK]), sb("rope_q", [P, SEQ])
        keep.kvn_hi, keep.kvn_lo = sb("kvn_hi", [P, 2, NTOK], F32R), sb("kvn_lo", [P, 2, NTOK], F32R)
        keep.qn_hi, keep.qn_lo = sb("qn_hi", [P, 3, SEQ], F32R), sb("qn_lo", [P, 3, SEQ], F32R)
        keep.k_hi = [sb(f"k_hi{b}", [P, NTOK], F32R) for b in range(2)]
        keep.k_lo = [sb(f"k_lo{b}", [P, NTOK], F32R) for b in range(2)]
        with ExitStack() as own:
            run(normalise_latents, own)
        with ExitStack() as own:
            run(attention, own)
    with ExitStack() as third:
        sb, _ = memory(nc, third)
        keep.h_hi, keep.h_lo = sb("hx_hi", [P, KD, SEQ], F32R), sb("hx_lo", [P, KD, SEQ], F32R)
        keep.branch = [(sb(f"b{b}_hi", [P, PAIRS, SEQ], F32R), sb(f"b{b}_lo", [P, PAIRS, SEQ], F32R)) for b in range(3)]
        with ExitStack() as own:
            run(gate_branches, own)
        with ExitStack() as own:
            run(merge, own)
    with ExitStack() as own:
        run(project_out, own)


def build(nc, io):
    with ExitStack() as always:
        sb, _ = memory(nc, always)
        keep = Kept()
        keep.cols, keep.ident = sb("cols", [P, NCOL]), sb("ident", [P, P])
        keep.silu_c, keep.eps = sb("silu_c", [P, KD, 2]), sb("eps", [P, len(EPS)])
        keep.gate_cols = sb("gate_cols", [P, KD])
        phases(nc, io, keep)


def scratch(nc, io):
    new = lambda name, shape, dt=F32: nc.dram_tensor(name, shape, dt).ap()
    io["y"] = new("y_scratch", (2, PAIRS, P, SEQ))
    io["h"] = new("h_scratch", (2, P, KD, SEQ))
    io["lat"] = new("lat_scratch", (4, P, NTOK))
    io["ql"] = new("ql_scratch", (3, P, SEQ))
    io["branch"] = new("branch_scratch", (2, PAIRS, P, SEQ))
    io["merged"] = new("merged_scratch", (KD, P, SEQ))


def vectors(a):
    import numpy as np
    rows = [a["c"], a["c_ctx"], a["b_mod"], a["g_pre"]] + [a[n] for n, _ in COLS[4:]]
    return np.ascontiguousarray(np.concatenate([np.reshape(r, (-1, P)) for r in rows]).T)


def feature_tiles(w, n=P):
    import numpy as np
    c, f = w.shape
    return np.ascontiguousarray(w.reshape(c // P, P, f // n, n).transpose(2, 1, 0, 3).reshape(f // n, P, -1))


def laid_out(a):
    import numpy as np
    w = a["w_in"][0]
    at = np.cumsum([0, 384, 256, 32, 512, 512, 512, 512, 512, 512, 512, 512, 64, 64, 64, 64, 512, 3072])
    (ql, kv, kr, gm, ci, cb, cc, gc, r, k, v, wdf, wdb, adf, adb, gr, gl) = [w[:, s:e] for s, e in zip(at, at[1:])]
    rot, swap = (np.concatenate([kr[:, a::2], kr[:, 1 - a::2]], 1) for a in (0, 1))
    quarters = np.concatenate([z[:, s:s + P] for s in range(0, W, P) for z in (ci, cc, cb, gc, gm, gr)], 1)
    w_in = np.concatenate([k, v, wdf, wdb, adf, adb, kv, rot, rot, rot, rot, swap, swap, swap, swap, r, ql, quarters], 1)
    branches = [feature_tiles(a[n][0]) for n in ("w_br_mla", "w_br_conv", "w_br_rwkv")]
    gates = [feature_tiles(gl[:, b * D:(b + 1) * D]) for b in range(3)]
    merge = np.concatenate([np.stack(gates, 1), np.stack(branches, 1)], 3).reshape(3 * KD, P, D + W)
    uq = a["w_uq"][0].reshape(Q_LORA, HEADS, QK_HEAD)
    e, o = uq[:, :, NOPE::2], uq[:, :, NOPE + 1::2]
    uq = np.concatenate([uq[:, :, :NOPE], e, o, o, e], 2).reshape(Q_LORA, HEADS * P)
    ukv = a["w_ukv"][0].reshape(KV_LORA, HEADS, 2, HEAD).transpose(0, 2, 1, 3).reshape(KV_LORA, 2 * W)
    zero = np.zeros((HEAD, W), np.float32)
    up = [np.concatenate([m[0, 0], zero, zero, m[0, 1]], 0) for m in (a["w_up"], a["a_up"])]
    up = np.concatenate([u.reshape(2, P, W).transpose(1, 0, 2).reshape(P, 2 * W) for u in up], 1)
    freq = THETA ** (-np.arange(ROPE // 4, dtype=np.float32) / (ROPE // 4))
    tok = np.arange(SEQ)
    ang = np.concatenate([(tok // GRID_W).astype(np.float32)[None] * freq[:, None],
                          (tok % GRID_W).astype(np.float32)[None] * freq[:, None]]).astype(np.float32)
    cos, sin = np.cos(ang), np.sin(ang)
    rope = np.concatenate([cos, cos, -sin, sin]).astype(np.float32)
    return {
        "x": a["x"][0], "ctx": a["ctx"][0], "cols": vectors(a), "w_in": feature_tiles(w_in),
        "wm": feature_tiles(a["w_mod"][0]),
        "up": up, "rope": rope,
        "uq": feature_tiles(uq), "uk": feature_tiles(ukv[:, :W], NOPE), "uv": feature_tiles(ukv[:, W:]),
        "w_merge": merge, "w_out": a["w_out"][0],
    }


def kernel(**inputs):
    import numpy as np
    import concourse.bacc as bacc
    from concourse.bass_utils import run_bass_kernel_spmd

    nc = bacc.Bacc("TRN2", target_bir_lowering=False, num_devices=1)
    arrays, io = {}, {}
    for name, v in laid_out({k: np.asarray(v) for k, v in inputs.items()}).items():
        arrays[f"{name}_dram"] = np.ascontiguousarray(v)
        io[name] = nc.dram_tensor(f"{name}_dram", v.shape, mybir.dt.from_np(v.dtype), kind="ExternalInput").ap()
    io["out"] = nc.dram_tensor("out_dram", (SEQ, D), F32, kind="ExternalOutput").ap()
    scratch(nc, io)
    build(nc, io)
    got = run_bass_kernel_spmd(nc, [arrays], core_ids=[0]).results[0]["out_dram"]
    return got.reshape(1, SEQ, D)
```

```python
import math
from contextlib import ExitStack

import concourse.bass as bass
from concourse import mybir

ALU = mybir.AluOpType
ACT = mybir.ActivationFunctionType
AX = mybir.AxisListType
F32 = mybir.dt.float32
F32R = mybir.dt.float32r
U8 = mybir.dt.uint8
P = 128

D, SEQ, CTX = 1024, 1024, 256
KD = D // P
NTOK = SEQ + CTX
NT = NTOK // P
HEADS, HEAD = 8, 64
W = HEADS * HEAD
PAIRS = HEADS // 2
Q_LORA, KV_LORA, ROPE, NOPE = 384, 256, 32, 64
QK_HEAD = NOPE + ROPE
GRID_W, THETA = 64, 10000.0
SCALE = QK_HEAD ** -0.5
RMS_EPS, GN_EPS, L2_EPS = 1e-6, 64e-5, 1e-12
EPS = (RMS_EPS, GN_EPS, L2_EPS)
DECAY = math.exp(-0.5)

COLS = [("c", KD), ("c_ctx", KD), ("b_mod", 3 * KD), ("g_pre", KD), ("w0", 8), ("a0", 8), ("k_k", 4), ("k_a", 4),
        ("r_k", 4), ("gn_g", 4), ("gn_b", 4), ("conv_w", 12), ("conv_b", 4), ("g_q", 3), ("g_kv", 2), ("g_post", KD)]
COL = {name: sum(n for _, n in COLS[:i]) for i, (name, _) in enumerate(COLS)}
NCOL = sum(n for _, n in COLS)
T_K, T_V, T_WD, T_AD, T_KV, T_KR, T_R, T_QL, T_F = 0, 4, 8, 9, 10, 12, 13, 17, 20


class Kept:
    pass


class Count:

    def __init__(self, sem):
        self.sem, self.n, self.before = sem, 0, 0

    def up(self, ins):
        ins.then_inc(self.sem, 1)
        self.n += 1
        return self.before + self.n

    def enter(self, i, per):
        self.start, self.per = self.n, per
        self.before, self.n = i * per + self.start, 0

    def leave(self, rounds):
        assert self.n == self.per, (self.n, self.per)
        self.before, self.n = 0, self.start + self.per * rounds


class Link(Count):

    def __init__(self, sem, eng):
        super().__init__(sem)
        self.eng = eng

    def __call__(self, ins):
        self.eng.wait_ge(self.sem, self.up(ins))


def memory(nc, stack):
    def sb(name, shape, dt=F32):
        return stack.enter_context(nc.sbuf_tensor(name, shape, dt))

    def ps(name, shape, dt=F32):
        return stack.enter_context(nc.psum_tensor(name, shape, dt))

    return sb, ps


def start(nc, sem, io, keep, stack):
    sb, ps = memory(nc, stack)
    space = keep.rk[:].rearrange("p f t -> p (f t)")
    x_in = space[:, 0:NT * D].rearrange("p (t c) -> p t c", c=D)
    wm = keep.r
    junk = space[:, NT * D:(NT + 1) * D]
    ss = sb("ss", [P, NT])
    rs = sb("rs", [P, NT])
    silu_t = sb("silu_t", [P, 2 * KD])
    silu_s = sb("silu_s", [P, 2 * KD])
    silu_c = keep.silu_c
    mod = sb("mod", [P, 2, 2 * KD])
    HV = 4
    h_val = sb("h_val", [P, HV, 512])
    mod_row = sb("mod_row", [2, 2 * D])
    mod_ps = ps("mod_ps", [P, 2 * D])
    tr_ps = ps("tr_ps", [P, 4, 512])
    cols, ident, hi, lo = keep.cols, keep.ident, keep.h_hi, keep.h_lo

    cols_in, x_land = sem("cols_in"), [sem(f"x_land{t}") for t in range(NT)]
    wm_land, wm_used = [sem(f"wm_land{b}") for b in range(4)], sem("wm_used")
    sq_done, xn_done, id_done = sem("sq_done"), sem("xn_done"), sem("id_done")
    silu_done, root_done, eps_done = sem("silu_done"), sem("root_done"), sem("eps_done")
    tr_done, val_done, hi_done = sem("tr_done"), sem("val_done"), sem("hi_done")
    lo_done = [sem(f"lo_done{b}") for b in range(2)]
    pool_link, dve_link = sem("start_pool"), sem("start_dve")
    NF = 2 * KD
    pieces = [(k, half) for k in range(KD) for half in range(2)]
    row_done, col_mm = sem("mod_row_done"), sem("mod_col_mm")
    groups = [(4 * g, min(4, NT - 4 * g)) for g in range((NT + 3) // 4)]
    order = [(g, k) for g in (2, 0, 1) for k in range(KD)]

    def lower(engine, n):
        g, k = order[n]
        w = groups[g][1] * P
        return engine.tensor_tensor(lo[:, k, g * 512:g * 512 + w], h_val[:, n % HV, 0:w],
                                    hi[:, k, g * 512:g * 512 + w].bitcast(F32), ALU.subtract)

    with nc.Block() as block:
        @block.sync
        def _(sp):
            sp.dma_start(cols[:], io["cols"]).then_inc(cols_in, 16)
            tiles = [8, 9, 0, 1, 2, 3, 4, 5, 6, 7]
            for n, (k, half) in enumerate(pieces):
                if n >= 4:
                    sp.wait_ge(wm_used, n - 3)
                sp.dma_start(wm[:, n % 4, :], io["wm"][k * P:(k + 1) * P, half * D:(half + 1) * D]).then_inc(wm_land[n % 4], 16)
                for t in tiles[n * 10 // 16:(n + 1) * 10 // 16]:
                    src = io["ctx"][(t - 8) * P:(t - 7) * P, :] if t >= 8 else io["x"][t * P:(t + 1) * P, :]
                    sp.dma_start(x_in[:, t, :], src).then_inc(x_land[t], 16)

        @block.scalar
        def _(act):
            squares = Link(sq_done, act)
            act.wait_ge(cols_in, 16)
            act.wait_ge(eps_done, len(EPS))
            nc.scalar.activation(silu_t[:], cols[:, 0:2 * KD], ACT.Tanh, scale=0.5).then_inc(silu_done, 1)
            for t in (8, 9, 0, 1, 2, 3, 4, 5, 6, 7):
                act.wait_ge(x_land[t], 16)
                squares(nc.scalar.activation(junk, x_in[:, t, :], ACT.Square, accum_out=ss[:, t:t + 1]))
                nc.scalar.activation(ss[:, t:t + 1], ss[:, t:t + 1], ACT.Sqrt, scale=1.0 / D,
                                     bias=keep.eps[:, 0:1]).then_inc(root_done, 1)
            for n, (g, k) in enumerate(order):
                w = groups[g][1] * P
                act.wait_ge(val_done, n + 1)
                nc.scalar.activation(hi[:, k, g * 512:g * 512 + w], h_val[:, n % HV, 0:w], ACT.Copy).then_inc(hi_done, 1)

        @block.gpsimd
        def _(pool):
            link = Link(pool_link, pool)
            for e, value in enumerate(EPS):
                nc.gpsimd.memset(keep.eps[:, e:e + 1], value).then_inc(eps_done, 1)
            link(nc.gpsimd.memset(ident[:], 0.0))
            nc.gpsimd.affine_select(out=ident[:], in_=ident[:], compare_op=ALU.not_equal, fill=1.0, base=0,
                                    pattern=[[-1, P]], channel_multiplier=1).then_inc(id_done, 1)
            for n in range(0, len(order), 2):
                pool.wait_ge(hi_done, n + 1)
                lower(nc.gpsimd, n).then_inc(lo_done[0], 1)

        @block.vector
        def _(dve):
            link = Link(dve_link, dve)
            dve.wait_ge(silu_done, 1)
            link(nc.vector.tensor_scalar(silu_s[:], silu_t[:], 0.5, 0.5, ALU.mult, ALU.add))
            nc.vector.tensor_tensor(silu_c[:], silu_s[:].rearrange("p (s k) -> p k s", s=2),
                                    cols[:, 0:2 * KD].rearrange("p (s k) -> p k s", s=2), ALU.mult).then_inc(silu_done, 1)
            for n, t in enumerate((8, 9, 0, 1, 2, 3, 4, 5, 6, 7)):
                dve.wait_ge(root_done, n + 1)
                link(nc.vector.reciprocal(rs[:, t:t + 1], ss[:, t:t + 1]))
                nc.vector.tensor_scalar(x_in[:, t, :], x_in[:, t, :], rs[:, t:t + 1], None, ALU.mult).then_inc(xn_done, 1)
                if n == 7:
                    dve.wait_ge(wm_used, len(pieces))
                    nc.vector.tensor_copy(mod_row[:], mod_ps[0:2, :]).then_inc(row_done, 1)
            dve.wait_ge(col_mm, 1)
            bias = cols[:, COL["b_mod"]:COL["b_mod"] + NF]
            for s in range(2):
                link(nc.vector.tensor_tensor(mod[:, s, :], mod_ps[:, s:2 * NF:2], bias, ALU.add))
                link(nc.vector.scalar_tensor_tensor(mod[:, s, KD:NF], mod[:, s, KD:NF], 1.0,
                                                    cols[:, COL["g_pre"]:COL["g_pre"] + KD], ALU.add, ALU.mult))
            for n, (g, k) in enumerate(order):
                w, s = groups[g][1] * P, int(g == 2)
                dve.wait_ge(tr_done, n + 1)
                if n >= HV:
                    dve.wait_ge(lo_done[n % 2], (n - HV) // 2 + 1)
                nc.vector.tensor_scalar(h_val[:, n % HV, 0:w], tr_ps[:, n % 4, 0:w], mod[:, s, KD + k:KD + k + 1],
                                        mod[:, s, k:k + 1], ALU.mult, ALU.add).then_inc(val_done, 1)
                if n % 2 == 0 and n:
                    dve.wait_ge(hi_done, n)
                    lower(nc.vector, n - 1).then_inc(lo_done[1], 1)
            dve.wait_ge(hi_done, len(order))
            lower(nc.vector, len(order) - 1).then_inc(lo_done[1], 1)

        @block.tensor
        def _(pe):
            pe.wait_ge(silu_done, 2)
            for n, (k, half) in enumerate(pieces):
                pe.wait_ge(wm_land[n % 4], 16 * (n // 4 + 1))
                for a in range(0, D, 512):
                    last = nc.tensor.matmul(mod_ps[0:2, half * D + a:half * D + a + 512], silu_c[:, k, :],
                                            wm[:, n % 4, a:a + 512], start=k == 0, stop=k == KD - 1)
                last.then_inc(wm_used, 1)
            pe.wait_ge(id_done, 1)
            pe.wait_ge(row_done, 1)
            for f in range(NF):
                last = nc.tensor.transpose(mod_ps[:, 2 * f:2 * f + 2], mod_row[:, f * P:(f + 1) * P], ident[0:2, 0:2])
            last.then_inc(col_mm, 1)
            for n, (g, k) in enumerate(order):
                pe.wait_ge(xn_done, 2 + groups[g][0] + groups[g][1] if g < 2 else 2)
                if n >= 4:
                    pe.wait_ge(val_done, n - 3)
                for j in range(groups[g][1]):
                    last = nc.tensor.transpose(tr_ps[:, n % 4, j * P:(j + 1) * P],
                                               x_in[:, groups[g][0] + j, k * P:(k + 1) * P], ident[:])
                last.then_inc(tr_done, 1)


class WeightRing:

    def __init__(self, nc, sem, stack, name, width=D, raws=2):
        sb, _ = memory(nc, stack)
        self.nc, self.raws = nc, raws
        self.raw = sb(f"{name}_raw", [P, raws, width])
        self.hi = sb(f"{name}_hi", [P, 2, width], F32R)
        self.lo = sb(f"{name}_lo", [P, 2, width], F32R)
        self.landed = [sem(f"{name}_landed{b}") for b in range(2)]
        self.hi_made, self.lo_made, self.used = sem(f"{name}_hi_made"), sem(f"{name}_lo_made"), sem(f"{name}_used")

    def load(self, sp, src, t, b):
        sp.wait_ge(self.lo_made, t + 3 - self.raws)
        sp.dma_start(self.raw[:, b % self.raws, :], src).then_inc(self.landed[b], 16)

    def split_hi(self, act, t, b, turn):
        act.wait_ge(self.landed[b], turn * 16 + 16)
        act.wait_ge(self.used, t + 1)
        self.nc.scalar.activation(self.hi[:, b, :], self.raw[:, b % self.raws, :], ACT.Copy).then_inc(self.hi_made, 1)

    def split_lo(self, pool, t, b):
        pool.wait_ge(self.hi_made, t + 1)
        self.nc.gpsimd.tensor_tensor(self.lo[:, b, :], self.raw[:, b % self.raws, :], self.hi[:, b, :].bitcast(F32),
                                     ALU.subtract).then_inc(self.lo_made, 1)

    def wait(self, pe, t):
        pe.wait_ge(self.lo_made, t + 3)

    def products(self, b, hi, lo, outs, at=0, tiles=KD, before=None):
        for k in range(tiles):
            if before:
                before(k)
            for w, h in ((self.hi, hi), (self.hi, lo), (self.lo, hi)):
                for out, a, e in outs:
                    first, end = k == 0 and w is self.hi and h is hi, k == tiles - 1 and w is self.lo
                    last = self.nc.tensor.matmul(out, w[:, b, at + k * P:at + (k + 1) * P], h[:, k, a:e],
                                                 start=first, stop=end)
        return last


MASKS = 8


def make_mask(nc, keep, work, link, n):
    def mask(dst, cuts, view):
        for d in range(2):
            w = work[:, d, :]
            link(nc.gpsimd.memset(w, 0.0))
            part = view(w, d)
            link(nc.gpsimd.memset(part, 1.0))
            for base, pattern, mult in cuts[d]:
                link(nc.gpsimd.affine_select(out=part, in_=part, compare_op=ALU.is_ge, fill=0.0, base=base,
                                             pattern=pattern, channel_multiplier=mult))
            for e in range(2):
                link(nc.gpsimd.tensor_copy(dst[:, 2 * d + e, :], w))

    if n == 0:
        mask(keep.m_strict, [[(-1, [[1, P]], -1)], [(-1, [[-1, P]], 1)]], lambda w, d: w)
    else:
        j = n - 1
        half = 1 << j
        blocks = P // (2 * half)

        def halves(w, second):
            return w.rearrange("p (n two h) -> p n two h", two=2, h=half)[:, :, second, :]

        first_rows = [(0, [[-2 * half, blocks], [0, half]], 1), (half - 1, [[2 * half, blocks], [0, half]], -1)]
        second_rows = [(-half, [[-2 * half, blocks], [0, half]], 1),
                       (2 * half - 1, [[2 * half, blocks], [0, half]], -1)]
        flip = j == 0
        rows = [first_rows, second_rows] if flip else [second_rows, first_rows]
        mask(keep.m_level[j], rows, lambda w, d: halves(w, (1 - d) if flip else d))


def project(nc, sem, io, keep, stack):
    sb, ps = memory(nc, stack)
    ring = WeightRing(nc, sem, stack, "in")
    out_ps = ps("in_ps", [P, 2, 3 * 512])
    stage = sb("lat_stage", [P, 2, NTOK])
    drained, staged, h_out = sem("in_drained"), sem("lat_staged"), sem("h_out")
    sent = [sem(f"lat_sent{b}") for b in range(2)]
    gate_ps, gate_row = ps("gate_ps", [P, D]), sb("gate_row", [2, D])
    gate_w = [keep.r[:, n, :] for n in range(PAIRS)] + [keep.rk[:, T_WD - 2 + n, 0:D] for n in range(PAIRS)]
    work, mask_link = sb("mask_work", [P, 2, P]), sem("mask_link")
    PEELED = 4
    gate_land, gate_mm, gate_done = sem("gate_land"), sem("gate_mm"), sem("gate_done")
    row_done, col_mm = sem("gate_row_done"), sem("gate_col_mm")

    def send(act, t, n):
        if T_R <= t < T_QL:
            return n
        act.wait_ge(staged, n + 1)
        dst, e = (io["lat"][t - T_KV], NTOK) if t < T_R else (io["ql"][t - T_QL], SEQ)
        act.dma_start(dst, stage[:, n % 2, 0:e]).then_inc(sent[n % 2], 16)
        return n + 1

    with nc.Block() as block:
        @block.sync
        def _(sp):
            with sp.Fori(0, T_F // 2) as i:
                for b in range(2):
                    ring.load(sp, io["w_in"][i * 2 + b, :, :], i * 2 + b, b)

        @block.scalar
        def _(act):
            for f in range(KD):
                act.dma_start(gate_w[f], io["wm"][f * P:(f + 1) * P, 2 * D:3 * D]).then_inc(gate_land, 16)
            for t in range(PEELED + 2):
                ring.split_hi(act, t, t % 2, t // 2)
            act.wait_ge(gate_land, 16 * KD)
            for part, h in enumerate((keep.h_hi, keep.h_lo)):
                act.dma_start(io["h"][part], h[:, :, 0:SEQ].bitcast(F32)).then_inc(h_out, 16)
            with act.Fori(PEELED // 2 + 1, T_KV // 2) as i:
                for b in range(2):
                    ring.split_hi(act, i * 2 + b, b, i)
            n = 0
            for t in range(T_KV, T_F):
                ring.split_hi(act, t, t % 2, t // 2)
                if t >= T_KV + 2:
                    n = send(act, t - 2, n)
            for t in (T_F - 2, T_F - 1):
                n = send(act, t, n)
            for b in range(2):
                act.wait_ge(sent[b], 16 * ((n + 1 - b) // 2))
            act.wait_ge(h_out, 32)

        @block.gpsimd
        def _(pool):
            pool.sem_inc(ring.lo_made, 2)
            with pool.Fori(0, T_KV // 2) as i:
                for b in range(2):
                    ring.split_lo(pool, i * 2 + b, b)
            link = Link(mask_link, pool)
            for t in range(T_KV, T_F):
                ring.split_lo(pool, t, t % 2)
                if t - T_KV < MASKS:
                    make_mask(nc, keep, work, link, t - T_KV)

        @block.tensor
        def _(pe):
            pe.sem_inc(ring.used, 2)

            def tile(t, b, end):
                ring.wait(pe, t)
                pe.wait_ge(drained, t + 1)
                outs = [(out_ps[:, b, a:min(a + 512, end)], a, min(a + 512, end)) for a in range(0, end, 512)]
                ring.products(b, keep.h_hi, keep.h_lo, outs).then_inc(ring.used, 1)

            for t in range(PEELED):
                tile(t, t % 2, NTOK)
            pe.wait_ge(gate_land, 16 * KD)
            for k in range(KD):
                for a in (0, 512):
                    last = nc.tensor.matmul(gate_ps[0:2, a:a + 512], keep.silu_c[:, k, :], gate_w[k][:, a:a + 512],
                                            start=k == 0, stop=k == KD - 1)
            last.then_inc(gate_mm, 1)
            tile(PEELED, PEELED % 2, NTOK)
            pe.wait_ge(row_done, 1)
            for f in range(KD):
                last = nc.tensor.transpose(gate_ps[:, 2 * f:2 * f + 2], gate_row[:, f * P:(f + 1) * P], keep.ident[0:2, 0:2])
            last.then_inc(col_mm, 1)
            tile(PEELED + 1, (PEELED + 1) % 2, NTOK)
            with pe.Fori(PEELED // 2 + 1, T_R // 2) as i:
                for b in range(2):
                    tile(i * 2 + b, b, NTOK)
            tile(T_R - 1, 0, NTOK)
            tile(T_R, 1, SEQ)
            with pe.Fori(T_R // 2 + 1, T_F // 2) as i:
                for b in range(2):
                    tile(i * 2 + b, b, SEQ)

        @block.vector
        def _(dve):
            dve.sem_inc(drained, 2)

            def drain(t, b, end, dst):
                dve.wait_ge(ring.used, t + 3)
                nc.vector.tensor_copy(dst, out_ps[:, b, 0:end]).then_inc(drained, 1)

            def row(store, i):
                return store[:, bass.ds(i, 1), :].rearrange("p a t -> p (a t)")

            for t in range(PEELED):
                drain(t, t % 2, NTOK, keep.rk[:, t, :])
            dve.wait_ge(gate_mm, 1)
            nc.vector.tensor_copy(gate_row[:], gate_ps[0:2, :]).then_inc(row_done, 1)
            drain(PEELED, PEELED % 2, NTOK, keep.rk[:, PEELED, :])
            dve.wait_ge(col_mm, 1)
            half_post = keep.gate_cols
            nc.vector.tensor_tensor(half_post[:], gate_ps[:, 0:2 * KD:2], keep.cols[:, COL["b_mod"] + 2 * KD:COL["b_mod"] + 3 * KD],
                                    ALU.add).then_inc(gate_done, 1)
            dve.wait_ge(gate_done, 1)
            nc.vector.scalar_tensor_tensor(half_post[:], half_post[:], 0.5, keep.cols[:, COL["g_post"]:COL["g_post"] + KD],
                                           ALU.mult, ALU.mult)
            drain(PEELED + 1, (PEELED + 1) % 2, NTOK, keep.rk[:, PEELED + 1, :])
            with dve.Fori(PEELED // 2 + 1, T_KV // 2) as i:
                for b in range(2):
                    drain(i * 2 + b, b, NTOK, row(keep.rk, i * 2 + b))
            n = 0
            for t in range(T_KV, T_F):
                if T_R <= t < T_QL:
                    drain(t, t % 2, SEQ, keep.r[:, t - T_R, :])
                    continue
                if n >= 2:
                    dve.wait_ge(sent[n % 2], 16 * (n // 2))
                end = NTOK if t < T_R else SEQ
                dve.wait_ge(ring.used, t + 3)
                nc.vector.tensor_copy(stage[:, n % 2, 0:end], out_ps[:, t % 2, 0:end]).then_inc(drained, 1)
                dve.wait_ge(drained, t + 3)
                dve.sem_inc(staged, 1)
                n += 1


def head_patterns(nc, link, pick, spread):
    link(nc.gpsimd.memset(pick[:], 1.0))
    link(nc.gpsimd.memset(spread[:], 1.0))
    for sign, base in ((1, 0), (-1, HEAD - 1)):
        link(nc.gpsimd.affine_select(out=pick[:], in_=pick[:], compare_op=ALU.is_ge, fill=0.0, base=base,
                                     pattern=[[sign * P, PAIRS], [-sign * HEAD, HEADS]], channel_multiplier=sign))
        link(nc.gpsimd.affine_select(out=spread[:], in_=spread[:], compare_op=ALU.is_ge, fill=0.0, base=base,
                                     pattern=[[sign * P, PAIRS], [sign, P]], channel_multiplier=-sign * HEAD))


def prepare_rwkv(nc, sem, io, keep, stack):
    sb, ps = memory(nc, stack)
    sq = sb("kk_sq", [P, 2, NTOK])
    root = sb("kk_root", [HEADS, NTOK])
    pick, spread = sb("kk_pick", [P, PAIRS, HEADS]), sb("kk_spread", [HEADS, PAIRS, P])
    norm_ps = ps("kk_ps", [P, 2, 3 * 512])
    rk, kk, cols = keep.rk, keep.kk, keep.cols
    sq_done, norm_mm, root_done, kk_done = sem("kk_sq_done"), sem("kk_mm"), sem("kk_root_done"), sem("kk_done")
    ones_done, up_in, factor_mm = sem("block_ones_done"), sem("up_in"), sem("kk_factor_mm")
    pool_link, dve_link, act_link = sem("prep_pool"), sem("prep_dve"), sem("prep_act")
    with nc.Block() as block:
        @block.sync
        def _(sp):
            sp.dma_start(keep.up[:], io["up"]).then_inc(up_in, 16)
            sp.wait_ge(up_in, 16)

        @block.gpsimd
        def _(pool):
            link = Link(pool_link, pool)
            head_patterns(nc, link, pick, spread)
            pool.sem_inc(ones_done, 1)
            nc.gpsimd.memset(keep.ones[:], 1.0)
            nc.gpsimd.memset(keep.state[:], 0.0)
            for s in range(2):
                nc.gpsimd.memset(keep.bkz[s][:], 0.0)
                for buf in (keep.nt[s], keep.x1t[s], *keep.wp[s]):
                    link(nc.gpsimd.memset(buf[:], 0.0))
                for buf in (keep.x1t[s], *keep.wp[s]):
                    nc.gpsimd.affine_select(out=buf[:], in_=buf[:], compare_op=ALU.not_equal, fill=1.0, base=0,
                                            pattern=[[0, 4], [-1, P]], channel_multiplier=1)

        @block.scalar
        def _(act):
            link = Link(act_link, act)
            link(nc.scalar.activation(rk[:, T_WD, :], rk[:, T_WD, :], ACT.Tanh))
            for p in range(PAIRS):
                if p >= 2:
                    act.wait_ge(norm_mm, p - 1)
                nc.scalar.activation(sq[:, p % 2, :], rk[:, T_K + p, :], ACT.Square,
                                     scale=cols[:, COL["k_k"] + p:COL["k_k"] + p + 1]).then_inc(sq_done, 1)
            act.wait_ge(norm_mm, PAIRS)
            nc.scalar.activation(root[:], norm_ps[0:HEADS, 0, 0:NTOK], ACT.Sqrt,
                                 bias=keep.eps[0:HEADS, 2:3]).then_inc(root_done, 1)

        @block.tensor
        def _(pe):
            pe.wait_ge(ones_done, 1)
            for p in range(PAIRS):
                pe.wait_ge(sq_done, p + 1)
                for a, e in ((0, 512), (512, 1024), (1024, NTOK)):
                    last = nc.tensor.matmul(norm_ps[0:HEADS, 0, a:e], pick[:, p, :], sq[:, p % 2, a:e],
                                            start=p == 0, stop=p == PAIRS - 1)
                last.then_inc(norm_mm, 1)
            pe.wait_ge(root_done, 2)
            for p in range(PAIRS):
                if p >= 2:
                    pe.wait_ge(kk_done, p - 1)
                for a, e in ((0, 512), (512, 1024), (1024, NTOK)):
                    last = nc.tensor.matmul(norm_ps[:, p % 2, a:e], spread[:, p, :], root[:, a:e], start=True, stop=True)
                last.then_inc(factor_mm, 1)

        @block.vector
        def _(dve):
            link = Link(dve_link, dve)
            link(nc.vector.memset(keep.head_ones[:], 0.0))
            nc.vector.memset(keep.head_ones[0:HEAD, 0:HEAD], 1.0)
            nc.vector.memset(keep.head_ones[HEAD:P, HEAD:P], 1.0)
            nc.vector.tensor_scalar(keep.half_w0[:], cols[:, COL["w0"]:COL["w0"] + 8], 0.5, None, ALU.mult)
            nc.vector.tensor_scalar(keep.half_a0[:], cols[:, COL["a0"]:COL["a0"] + 8], 0.5, None, ALU.mult)
            ka = cols[:, COL["k_a"]:COL["k_a"] + 4]
            nc.vector.tensor_scalar(keep.half_ka[:], ka, 0.5, None, ALU.mult)
            nc.vector.tensor_scalar(keep.rest_ka[:], ka, -0.5, 1.0, ALU.mult, ALU.add)
            nc.vector.tensor_scalar(keep.rest_ka2[:], ka, -1.0, 2.0, ALU.mult, ALU.add)
            dve.wait_ge(root_done, 1)
            nc.vector.reciprocal(root[:], root[:]).then_inc(root_done, 1)
            for p in range(PAIRS):
                dve.wait_ge(factor_mm, p + 1)
                nc.vector.scalar_tensor_tensor(kk[:, p, :], rk[:, T_K + p, :],
                                               cols[:, COL["k_k"] + p:COL["k_k"] + p + 1], norm_ps[:, p % 2, 0:NTOK],
                                               ALU.mult, ALU.mult).then_inc(kk_done, 1)


def recurrence(nc, sem, io, keep, stack):
    sb, ps = memory(nc, stack)
    rk, kk = keep.rk, keep.kk
    bank = [ps(f"bank{s}", [P, 4, 512]) for s in range(2)]
    th = [sb(f"th{s}", [P, 4, P]) for s in range(2)]
    ell = [sb(f"ell{s}", [P, 2, P]) for s in range(2)]
    cum = [sb(f"cum{s}", [P, 2, P]) for s in range(2)]
    exc = [sb(f"exc{s}", [P, 2, P]) for s in range(2)]
    mid = [sb(f"mid{s}", [P, 2, 2]) for s in range(2)]
    e_inv = [sb(f"e_inv{s}", [P, 2, P]) for s in range(2)]
    a_e, v_st = ell, cum
    g_e = [t[:, 0:2, :] for t in th]
    h = [sb(f"h{p}", [P, 2]) for p in range(PAIRS)]
    ar = [sb(f"ar{p}", [P, 2, 2, P]) for p in range(PAIRS)]
    tok = [sb(f"tok{p}", [P, 3, 2, P]) for p in range(PAIRS)]
    xm = [sb(f"xm{s}", [P, 4, P]) for s in range(2)]
    xt = [sb(f"xt{s}", [P, 4, P]) for s in range(2)]
    z = [sb(f"z{s}", [P, 2, P]) for s in range(2)]
    p1 = [sb(f"p1_{s}", [P, 2, P]) for s in range(2)]
    u = [sb(f"u{s}", [P, 2, P]) for s in range(2)]
    bk_both = [sb(f"bk_both{s}", [P, 2, 2, P]) for s in range(2)]
    rm, y_st = p1, u
    kept = [sb(f"kept{s}", [P, 4, 3, P]) for s in range(2)]
    raw_done, kept_done = ([sem(f"{name}{s}") for s in range(2)] for name in ("rec_raw_done", "rec_kept_done"))
    dve_link, passed = sem("rec_dve"), sem("rec_passed")
    two = lambda name: [sem(f"{name}{s}") for s in range(2)]
    up_mm, th_done, cum_done, exp_done, bk_done, ar_done = map(two, ("up_mm", "th_done", "cum_done", "exp_done", "bk_done", "ar_done"))
    bk_mm, bk_tok, v_mm, v_tok = map(two, ("bk_mm", "bk_tok", "v_mm", "v_tok"))
    score_mm, x1t_done, masked, x_mm, x_done = map(two, ("score_mm", "x1t_done", "masked", "x_mm", "x_done"))
    w_mm, w_done, xt_mm, xt_done = map(two, ("w_mm", "w_done", "xt_mm", "xt_done"))
    z_done, p_mm, p_done, u_mm, u_done, s_mm, s_done, y_mm, y_done, y_sent = map(
        two, ("z_done", "p_mm", "p_done", "u_mm", "u_done", "s_mm", "s_done", "y_mm", "y_done", "y_sent"))
    LEVELS = range(1, 7)
    UNITS = [(d, e) for d in range(2) for e in range(2)]

    def tokens(n):
        if isinstance(n, int) and n < 2:
            return SEQ + n * P, SEQ + CTX - P - n * P
        return (n - 2) * P, SEQ - P - (n - 2) * P

    def seg(buf, i, at):
        return buf[:, i, bass.ds(at, P)]

    def wait(eng, s, value):
        if not (isinstance(value, int) and value <= 0):
            eng.wait_ge(s, value)

    class Tensor:
        def __init__(self, eng):
            self.eng = eng

        def up(self, v, p, n):
            s, pe = p % 2, self.eng
            wait(pe, masked[s], v)
            wait(pe, raw_done[s], v * 3)
            at = tokens(n)
            for m, tile in ((0, T_WD), (1, T_AD)):
                for d in range(2):
                    last = nc.tensor.matmul(bank[s][:, 3, (2 * m + d) * P:(2 * m + d + 1) * P],
                                            keep.up[:, (2 * m + d) * W + p * P:(2 * m + d) * W + (p + 1) * P],
                                            seg(rk, tile, at[d]), start=True, stop=True)
            last.then_inc(up_mm[s], 1)

        def bk_turn(self, v, p):
            s, pe = p % 2, self.eng
            wait(pe, th_done[s], v + 1)
            wait(pe, bk_done[s], v + 1)
            for i in range(2):
                for d in range(2):
                    c = (2 * i + d) * P
                    last = nc.tensor.transpose(bank[s][:, 3, c:c + P], bk_both[s][:, i, d, :], keep.ident[:])
            last.then_inc(bk_mm[s], 1)

        def v_turn(self, v, p):
            s, pe = p % 2, self.eng
            wait(pe, bk_tok[s], v + 1)
            wait(pe, ar_done[s], v + 1)
            for d in range(2):
                last = nc.tensor.transpose(bank[s][:, 3, d * P:(d + 1) * P], v_st[s][:, d, :], keep.ident[:])
            last.then_inc(v_mm[s], 1)

        def scores(self, v, p, emit):
            s, pe = p % 2, self.eng
            wait(pe, bk_done[s], v + 1)
            wait(pe, ar_done[s], v + 1)
            for part in range(4) if emit else (0, 2):
                if part == 0:
                    wait(pe, u_done[s], v)
                elif part == 1:
                    wait(pe, s_done[s], v)
                elif part == 2:
                    wait(pe, y_done[s], v - 4)
                else:
                    wait(pe, p_done[s], v)
                    wait(pe, v_tok[s], v + 1)
                for i, (d, e) in enumerate(UNITS):
                    last = nc.tensor.matmul(bank[s][:, part, i * P:(i + 1) * P], keep.bkz[s][:, part // 2, d, e, :],
                                            ar[p][:, d, part % 2, :], start=True, stop=True)
                last.then_inc(score_mm[s], 1 if emit else 2)

        def x1_turn(self, v, p):
            s, pe = p % 2, self.eng
            wait(pe, x1t_done[s], v + 1)
            wait(pe, masked[s], v + 1)
            wait(pe, raw_done[s], v * 3 + 1)
            for i in range(4):
                last = nc.tensor.transpose(bank[s][:, 1, i * P:(i + 1) * P], keep.x1t[s][:, i, :], keep.ident[:])
            last.then_inc(x_mm[s], 1)

        def level_w(self, v, p, j):
            s, pe = p % 2, self.eng
            wait(pe, x_done[s], v * 6 + j)
            for i in range(4):
                last = nc.tensor.matmul(bank[s][:, 0, i * P:(i + 1) * P], keep.nt[s][:, i, :], xm[s][:, i, :],
                                        start=True, stop=True)
            last.then_inc(w_mm[s], 1)

        def level_x(self, v, p, j):
            s, pe = p % 2, self.eng
            wait(pe, w_done[s], v * 6 + j)
            if j > 1:
                wait(pe, xt_done[s], v * 6 + j - 1)
            else:
                wait(pe, raw_done[s], v * 3 + 2)
            xt_now = keep.x1t[s] if j == 1 else xt[s]
            if j < 6:
                for i in range(4):
                    last = nc.tensor.matmul(bank[s][:, 1, i * P:(i + 1) * P], xt_now[:, i, :],
                                            keep.wp[s][j - 1][:, i, :], start=True, stop=True)
                last.then_inc(x_mm[s], 1)
            for i in range(4):
                last = nc.tensor.matmul(bank[s][:, 2, i * P:(i + 1) * P], keep.wp[s][j - 1][:, i, :],
                                        xt_now[:, i, :], start=True, stop=True)
            last.then_inc(xt_mm[s], 1)

        def rhs(self, v, p, fronted):
            s, pe = p % 2, self.eng
            wait(pe, z_done[s], v + 1)
            wait(pe, kept_done[s], v + 1)
            wait(pe, v_tok[s], v + 1 + fronted)
            for d in range(2):
                nc.tensor.matmul(bank[s][:, 3, d * P:(d + 1) * P], ar[p][:, d, 0, :], z[s][:, d, :],
                                 start=True, stop=False, skip_group_check=True)
                for e in range(2):
                    c = d * P + e * HEAD
                    last = nc.tensor.matmul(bank[s][:, 3, c:c + HEAD], kept[s][:, 2 * d + e, 1, :],
                                            tok[p][:, 2, d, e * HEAD:(e + 1) * HEAD], start=False, stop=True,
                                            skip_group_check=True)
            last.then_inc(p_mm[s], 1)

        def solve(self, v, p):
            s, pe = p % 2, self.eng
            wait(pe, p_done[s], v + 1)
            wait(pe, xt_done[s], v * 6 + 6)
            for i, (d, e) in enumerate(UNITS):
                c = d * P + e * HEAD
                last = nc.tensor.matmul(bank[s][:, 0, c:c + HEAD], xt[s][:, i, :],
                                        p1[s][:, d, e * HEAD:(e + 1) * HEAD], start=True, stop=True)
            last.then_inc(u_mm[s], 1)

        def ends(self, v, p, emit):
            s, pe = p % 2, self.eng
            wait(pe, u_done[s], v + 1)
            for d in range(2):
                for i, src in ((0, u[s][:, d, :]), (1, tok[p][:, 2, d, :])):
                    last = nc.tensor.matmul(bank[s][:, 1, d * P:(d + 1) * P], tok[p][:, i, d, :], src,
                                            start=(i == 0), stop=(i == 1))
            last.then_inc(s_mm[s], 1)
            if not emit:
                return
            for d in range(2):
                c = d * P
                nc.tensor.matmul(bank[s][:, 2, c:c + P], z[s][:, d, :], ar[p][:, d, 1, :], start=True, stop=False,
                                 skip_group_check=True)
                for e in range(2):
                    part = slice(e * HEAD, (e + 1) * HEAD)
                    nc.tensor.matmul(bank[s][part, 2, c:c + P], u[s][:, d, part], kept[s][:, 2 * d + e, 0, :],
                                     start=False, stop=False, skip_group_check=True)
                    last = nc.tensor.matmul(bank[s][part, 2, c:c + P], tok[p][:, 2, d, part],
                                            kept[s][:, 2 * d + e, 2, :], start=False, stop=True, skip_group_check=True)
            last.then_inc(y_mm[s], 1)

    class Scalar:
        def __init__(self, eng):
            self.eng = eng

        def gates(self, v, p):
            s, act = p % 2, self.eng
            wait(act, up_mm[s], v + 1)
            wait(act, bk_done[s], v)
            for m, half in ((0, keep.half_w0), (1, keep.half_a0)):
                for d in range(2):
                    i = 2 * m + d
                    last = nc.scalar.activation(th[s][:, i, :], bank[s][:, 3, i * P:(i + 1) * P], ACT.Tanh,
                                                scale=0.5, bias=half[:, d * 4 + p:d * 4 + p + 1])
            last.then_inc(th_done[s], 1)

        def exps(self, v, p):
            s, act = p % 2, self.eng
            wait(act, cum_done[s], v + 1)
            wait(act, ar_done[s], v)
            wait(act, bk_done[s], v)
            minus, plus = mid[s][:, 0, :], mid[s][:, 1, :]
            now, before, inv = ar[p][:, :, 1, :], ar[p][:, :, 0, :], e_inv[s]
            for dst, d, src, up in ((inv, 0, cum, 0), (inv, 1, exc, 1), (before, 0, exc, 1), (before, 1, cum, 0),
                                    (now, 0, cum, 1), (now, 1, exc, 0)):
                nc.scalar.activation(dst[:, d, :], src[s][:, d, :], ACT.Exp, scale=1.0 if up else -1.0,
                                     bias=(minus if up else plus)[:, d:d + 1])
            nc.scalar.activation(h[p][:], plus, ACT.Exp).then_inc(exp_done[s], 1)

        def bk(self, v, p):
            s, act = p % 2, self.eng
            wait(act, bk_mm[s], v + 1)
            nc.scalar.activation(tok[p][:, 0:2, :, :], bank[s][:, 3, :].rearrange("p (i d t) -> p i d t", i=2, d=2),
                                 ACT.Copy).then_inc(bk_tok[s], 1)

        def v(self, v, p):
            s, act = p % 2, self.eng
            wait(act, v_mm[s], v + 1)
            nc.scalar.activation(tok[p][:, 2, :, :], bank[s][:, 3, 0:2 * P].rearrange("p (d t) -> p d t", d=2),
                                 ACT.Copy).then_inc(v_tok[s], 1)

        def scores(self, v, p, emit):
            s, act = p % 2, self.eng
            for part in (1, 2, 3) if emit else (2,):
                wait(act, score_mm[s], v * 4 + part + 1)
                nc.scalar.activation(kept[s][:, :, part - 1, :], bank[s][:, part, :].rearrange("p (u t) -> p u t", u=4),
                                     ACT.Copy).then_inc(raw_done[s], 1 if emit else 3)

        def x(self, v, p, j):
            s, act = p % 2, self.eng
            if j < 7:
                wait(act, x_mm[s], v * 6 + j)
                nc.scalar.activation(xm[s][:], bank[s][:, 1, :].rearrange("p (u t) -> p u t", u=4),
                                     ACT.Copy).then_inc(x_done[s], 1)
            if j > 1:
                wait(act, xt_mm[s], v * 6 + j - 1)
                nc.scalar.activation(xt[s][:], bank[s][:, 2, :].rearrange("p (u t) -> p u t", u=4),
                                     ACT.Copy).then_inc(xt_done[s], 1)

        def rhs(self, v, p):
            s, act = p % 2, self.eng
            wait(act, p_mm[s], v + 1)
            nc.scalar.activation(p1[s][:], bank[s][:, 3, 0:2 * P].rearrange("p (d t) -> p d t", d=2),
                                 ACT.Copy).then_inc(p_done[s], 1)

        def solve(self, v, p):
            s, act = p % 2, self.eng
            wait(act, u_mm[s], v + 1)
            wait(act, y_sent[s], (v - 4) * 32)
            nc.scalar.activation(u[s][:], bank[s][:, 0, 0:2 * P].rearrange("p (d t) -> p d t", d=2),
                                 ACT.Copy).then_inc(u_done[s], 1)

        def y(self, v, p):
            s, act = p % 2, self.eng
            wait(act, y_mm[s], v - 3)
            nc.scalar.activation(y_st[s][:], bank[s][:, 2, 0:2 * P].rearrange("p (d t) -> p d t", d=2),
                                 ACT.Copy).then_inc(y_done[s], 1)

    class Vector:
        def __init__(self, eng, link):
            self.eng, self.link = eng, link

        def cumulate(self, v, p):
            s, dve, link = p % 2, self.eng, self.link
            wait(dve, th_done[s], v + 1)
            link(nc.vector.tensor_scalar(ell[s][:], th[s][:, 0:2, :], -0.5 * DECAY, -0.5 * DECAY, ALU.mult, ALU.add))
            for d in range(2):
                last = nc.vector.tensor_tensor_scan(cum[s][:, d, :], keep.ones[:], ell[s][:, d, :], 0.0, ALU.mult, ALU.add)
            link(last)
            nc.vector.tensor_scalar(mid[s][:, 0, :], cum[s][:, :, P - 1], -0.5, None, ALU.mult)
            nc.vector.tensor_scalar(mid[s][:, 1, :], cum[s][:, :, P - 1], 0.5, None, ALU.mult)
            nc.vector.tensor_tensor(exc[s][:], cum[s][:], ell[s][:], ALU.subtract).then_inc(cum_done[s], 1)
            link(nc.vector.tensor_scalar(g_e[s], th[s][:, 2:4, :], keep.half_ka[:, p:p + 1], keep.rest_ka[:, p:p + 1],
                                         ALU.mult, ALU.add))

        def operands(self, v, p, n):
            s, dve, link = p % 2, self.eng, self.link
            wait(dve, exp_done[s], v + 1)
            nc.vector.scalar_tensor_tensor(a_e[s][:], th[s][:, 2:4, :], 1.0, e_inv[s][:], ALU.add, ALU.mult)
            link(nc.vector.tensor_tensor(g_e[s], g_e[s], e_inv[s][:], ALU.mult))
            at = tokens(n)
            for d in range(2):
                nc.vector.scalar_tensor_tensor(bk_both[s][:, 0, d, :], seg(kk, p, at[d]), -0.5, a_e[s][:, d, :],
                                               ALU.mult, ALU.mult)
                last = nc.vector.tensor_tensor(bk_both[s][:, 1, d, :], seg(rk, T_K + p, at[d]), g_e[s][:, d, :], ALU.mult)
            link(last)
            for e in range(2):
                part = slice(e * HEAD, (e + 1) * HEAD)
                last = nc.vector.tensor_copy(keep.bkz[s][part, :, :, e, :], bk_both[s][part, :, :, :])
            last.then_inc(bk_done[s], 1)

        def scores(self, v, p, emit):
            s, dve = p % 2, self.eng
            wait(dve, score_mm[s], v * 4 + 1)
            dve.sem_inc(passed, 1)
            src = bank[s][:, 0, :].rearrange("p (u t) -> p u t", u=4)
            nc.vector.copy_predicated(keep.x1t[s][:], keep.m_level[0][:], src).then_inc(x1t_done[s], 1)
            nc.vector.copy_predicated(keep.nt[s][:], keep.m_strict[:], src).then_inc(masked[s], 1)

        def level(self, v, p, j):
            s, dve = p % 2, self.eng
            wait(dve, w_mm[s], v * 6 + j)
            dve.sem_inc(passed, 1)
            nc.vector.copy_predicated(keep.wp[s][j - 1][:], keep.m_level[j][:],
                                      bank[s][:, 0, :].rearrange("p (u t) -> p u t", u=4)).then_inc(w_done[s], 1)

        def z(self, v, p):
            s, dve, link = p % 2, self.eng, self.link
            for d in range(2):
                last = nc.vector.tensor_scalar(z[s][:, d, :], keep.state[:, 2 * p + d, :], h[p][:, d:d + 1], None, ALU.mult)
            link(last)
            dve.sem_inc(z_done[s], 1)

        def state(self, v, p):
            s, dve, link = p % 2, self.eng, self.link
            wait(dve, s_mm[s], v + 1)
            for d in range(2):
                last = nc.vector.scalar_tensor_tensor(rm[s][:, d, :], bank[s][:, 1, d * P:(d + 1) * P], h[p][:, d:d + 1],
                                                      keep.head_ones[:], ALU.mult, ALU.mult)
            link(last)
            dve.sem_inc(s_done[s], 1)
            for d in range(2):
                last = nc.vector.scalar_tensor_tensor(keep.state[:, 2 * p + d, :], z[s][:, d, :], h[p][:, d:d + 1],
                                                      rm[s][:, d, :], ALU.mult, ALU.add)
            link(last)

    class Pool:
        def __init__(self, eng):
            self.eng = eng

        def scores(self, v, p, emit):
            s, pool = p % 2, self.eng
            wait(pool, raw_done[s], v * 3 + 3)
            pool.sem_inc(passed, 1)
            for d, sign in ((0, 1), (1, -1)):
                units = slice(2 * d, 2 * d + 2)
                for part, base in ((0, 0), (1, -1), (2, 0)) if emit else ((1, -1),):
                    view = kept[s][:, units, part, :]
                    last = nc.gpsimd.affine_select(out=view, in_=view, compare_op=ALU.is_ge, fill=0.0, base=base,
                                                   pattern=[[0, 2], [sign, P]], channel_multiplier=-sign)
            last.then_inc(kept_done[s], 1)

        def operands(self, v, p, n):
            s, pool = p % 2, self.eng
            emit = not isinstance(n, int) or n >= 2
            wait(pool, exp_done[s], v + 1)
            at = tokens(n)
            for d in range(2):
                nc.gpsimd.tensor_tensor(ar[p][:, d, 0, :], seg(kk, p, at[d]), ar[p][:, d, 0, :], ALU.mult)
                if emit:
                    nc.gpsimd.tensor_tensor(ar[p][:, d, 1, :], seg(keep.r, p, at[d]), ar[p][:, d, 1, :], ALU.mult)
                last = nc.gpsimd.tensor_copy(v_st[s][:, d, :], seg(rk, T_V + p, at[d]))
            last.then_inc(ar_done[s], 1)

    class Sync:
        def __init__(self, eng):
            self.eng = eng

        def y(self, v, p, n):
            s, sp = p % 2, self.eng
            sp.wait_ge(y_done[s], v - 3)
            at = tokens(n)
            for d in range(2):
                sp.dma_start(io["y"][d, p, :, bass.ds(at[d], P)], y_st[s][:, d, :]).then_inc(y_sent[s], 16)

    def program(engine, eng, link=None):
        if engine == "tensor":
            t = Tensor(eng)
            front = [lambda v, p, n: t.up(v, p, n), lambda v, p, n: t.bk_turn(v, p), lambda v, p, n: t.v_turn(v, p)]
            places = [1, 3, 4]
        elif engine == "scalar":
            t = Scalar(eng)
            front = [lambda v, p, n: t.gates(v, p), lambda v, p, n: t.exps(v, p), lambda v, p, n: t.bk(v, p),
                     lambda v, p, n: t.v(v, p)]
            places = [1, 2, 3, 4]
        elif engine == "vector":
            t = Vector(eng, link)
            front = [lambda v, p, n: t.cumulate(v, p), lambda v, p, n: t.operands(v, p, n)]
            places = [1, 2]
        elif engine == "sync":
            t, front, places = Sync(eng), [], []
        else:
            t = Pool(eng)
            front = [lambda v, p, n: t.operands(v, p, n)]
            places = [2]

        def fronts(after, nxt):
            for place, step in zip(places, front):
                if place == after or after is None:
                    for v, p, n in nxt:
                        step(v, p, n)

        def half(n, sub, emit, nxt):
            v = 2 * n + sub
            pairs = (2 * sub, 2 * sub + 1)
            for p in pairs:
                if engine != "sync":
                    t.scores(v, p, emit)
                if engine == "tensor":
                    t.x1_turn(v, p)
                elif engine == "scalar":
                    t.x(v, p, 1)
            for j in LEVELS:
                for p in pairs:
                    if engine == "tensor":
                        t.level_w(v, p, j)
                    elif engine == "vector":
                        t.level(v, p, j)
                if j == 3 and engine == "vector":
                    for p in pairs:
                        t.z(v, p)
                fronts(j, nxt)
                if j == 5:
                    for p in pairs:
                        if engine == "tensor":
                            t.rhs(v, p, int(bool(nxt)))
                        elif engine == "scalar":
                            t.rhs(v, p)
                for p in pairs:
                    if engine == "tensor":
                        t.level_x(v, p, j)
                    elif engine == "scalar":
                        t.x(v, p, j + 1)
            for p in pairs:
                if engine in ("tensor", "scalar"):
                    t.solve(v, p)
            for p in pairs:
                if engine == "tensor":
                    t.ends(v, p, emit)
                elif engine == "vector":
                    t.state(v, p)
                elif engine == "scalar" and emit:
                    t.y(v, p)
                elif engine == "sync" and emit:
                    t.y(v, p, n)

        def chunk(n, emit, more):
            half(n, 0, emit, [(2 * n + 1, p, n) for p in (2, 3)])
            half(n, 1, emit, [(2 * n + 2, p, n + 1) for p in (0, 1)] if more else [])

        fronts(None, [(0, p, 0) for p in (0, 1)])
        chunk(0, False, True)
        chunk(1, False, True)
        with eng.Fori(0, NT - 3) as i:
            if link is not None:
                link.enter(i, chunk_links)
            chunk(i + 2, True, True)
        if link is not None:
            link.leave(NT - 3)
        chunk(NT - 1, True, False)

    chunk_links = PAIRS * 8
    with nc.Block() as block:
        @block.sync
        def _(sp):
            program("sync", sp)
            for s in range(2):
                sp.wait_ge(y_sent[s], 32 * 2 * SEQ // P)

        @block.tensor
        def _(pe):
            program("tensor", pe)

        @block.scalar
        def _(act):
            program("scalar", act)

        @block.vector
        def _(dve):
            program("vector", dve, Link(dve_link, dve))

        @block.gpsimd
        def _(pool):
            program("gpsimd", pool)


def finish_rwkv(nc, sem, io, keep, stack):
    sb, ps = memory(nc, stack)
    rk, cols = keep.rk, keep.cols
    y, centred, bonus = sb("gn_y", [P, 2, 2, SEQ]), sb("gn_centred", [P, PAIRS, SEQ]), sb("gn_bonus", [P, PAIRS, SEQ])
    th, gain = sb("gn_th", [P, 2, 2, SEQ]), sb("gn_gain", [P, SEQ])
    prod, work, sq = sb("gn_prod", [P, SEQ]), sb("gn_work", [P, SEQ]), sb("gn_sq", [P, SEQ])
    root, out = sb("gn_root", [HEADS, SEQ]), sb("gn_out", [P, 2, SEQ])
    slope, offset = sb("gn_slope", [P, PAIRS]), sb("gn_offset", [P, PAIRS])
    pick, spread = sb("gn_pick", [P, PAIRS, HEADS]), sb("gn_spread", [HEADS, PAIRS, P])
    picked, pool_link = sem("gn_picked"), sem("gn_pool")
    a_ps, sum_ps, mean_ps, var_ps = (ps(f"gn_{n}", [P, 1024]) for n in ("a", "sum", "mean", "var"))
    y_in = [sem(f"gn_in{b}") for b in range(2)]
    sent = [sem(f"gn_sent{b}") for b in range(2)]
    cols_done, a_mm, th_done, th_sum, gain_done, prod_done, work_done, bonus_mm, bonus_done = map(sem, (
        "gn_cols_done", "gn_a_mm", "gn_th_done", "gn_th_sum", "gn_gain_done", "gn_prod_done", "gn_work_done",
        "gn_bonus_mm", "gn_bonus_done"))
    y_sum, mean_mm, centred_done, sq_done, var_mm, root_done, factor_mm, out_done, dve_link = map(sem, (
        "gn_y_sum", "gn_mean_mm", "gn_centred", "gn_sq_done", "gn_var_mm", "gn_root_done", "gn_factor_mm",
        "gn_out_done", "gn_dve"))
    col = lambda name, p: cols[:, COL[name] + p:COL[name] + p + 1]
    halves = ((0, 512), (512, SEQ))
    factor_ps = (a_ps, sum_ps)
    with nc.Block() as block:
        @block.sync
        def _(sp):
            for p in range(PAIRS):
                if p >= 2:
                    sp.wait_ge(centred_done, p - 1)
                for d in range(2):
                    sp.dma_start(y[:, p % 2, d, :], io["y"][d, p]).then_inc(y_in[p % 2], 16)
            for p in range(PAIRS):
                sp.wait_ge(out_done, p + 1)
                sp.dma_start(io["branch"][1, p], out[:, p % 2, :]).then_inc(sent[p % 2], 16)
            for b in range(2):
                sp.wait_ge(sent[b], 32)

        @block.gpsimd
        def _(pool):
            head_patterns(nc, Link(pool_link, pool), pick, spread)
            pool.sem_inc(picked, 1)
            for p in range(PAIRS):
                if p:
                    pool.wait_ge(work_done, p)
                nc.gpsimd.tensor_tensor(prod[:], rk[:, T_K + p, 0:SEQ], keep.r[:, p, :], ALU.mult).then_inc(prod_done, 1)
                pool.wait_ge(th_done, 2 * p + 2)
                nc.gpsimd.tensor_tensor(th[:, p % 2, 0, :], th[:, p % 2, 0, :], th[:, p % 2, 1, :], ALU.add).then_inc(th_sum, 1)

        @block.tensor
        def _(pe):
            def head_sums(dst, src):
                for a, e in halves:
                    last = nc.tensor.matmul(dst[:, a:e], keep.head_ones[:], src[:, a:e], start=True, stop=True)
                return last

            pe.wait_ge(picked, 1)
            for p in range(PAIRS + 1):
                if p < PAIRS:
                    pe.wait_ge(y_sum, p + 1)
                    if p:
                        pe.wait_ge(centred_done, p)
                    head_sums(mean_ps, y[:, p % 2, 0, :]).then_inc(mean_mm, 1)
                    for d in range(2):
                        if p or d:
                            pe.wait_ge(th_done, 2 * p + d)
                        for a, e in halves:
                            c = (2 + d) * W + p * P
                            last = nc.tensor.matmul(a_ps[:, a:e], keep.up[:, c:c + P], rk[:, T_AD, a:e], start=True, stop=True)
                        last.then_inc(a_mm, 1)
                if p:
                    pe.wait_ge(work_done, p)
                    if p > 1:
                        pe.wait_ge(bonus_done, p - 1)
                    head_sums(sum_ps, work).then_inc(bonus_mm, 1)
                if p < PAIRS:
                    pe.wait_ge(sq_done, p + 1)
                    for a, e in halves:
                        last = nc.tensor.matmul(var_ps[0:HEADS, a:e], pick[:, p, :], sq[:, a:e],
                                                start=p == 0, stop=p == PAIRS - 1)
                    last.then_inc(var_mm, 1)
            pe.wait_ge(root_done, 2)
            pe.wait_ge(bonus_done, PAIRS)
            for p in range(PAIRS):
                if p >= 2:
                    pe.wait_ge(out_done, p - 1)
                for a, e in halves:
                    last = nc.tensor.matmul(factor_ps[p % 2][:, a:e], spread[:, p, :], root[:, a:e], start=True, stop=True)
                last.then_inc(factor_mm, 1)

        @block.scalar
        def _(act):
            act.wait_ge(cols_done, 1)
            for p in range(PAIRS):
                for d in range(2):
                    act.wait_ge(a_mm, 2 * p + d + 1)
                    if p >= 2:
                        act.wait_ge(gain_done, p - 1)
                    nc.scalar.activation(th[:, p % 2, d, :], a_ps[:], ACT.Tanh, scale=0.5,
                                         bias=keep.half_a0[:, d * 4 + p:d * 4 + p + 1]).then_inc(th_done, 1)
                act.wait_ge(centred_done, p + 1)
                if p:
                    act.wait_ge(var_mm, p)
                nc.scalar.activation(sq[:], centred[:, p, :], ACT.Square).then_inc(sq_done, 1)
                act.wait_ge(th_sum, p + 1)
                if p:
                    act.wait_ge(work_done, p)
                nc.scalar.activation(gain[:], th[:, p % 2, 0, :], ACT.Identity, scale=slope[:, p:p + 1],
                                     bias=offset[:, p:p + 1]).then_inc(gain_done, 1)
            act.wait_ge(var_mm, PAIRS)
            nc.scalar.activation(root[:], var_ps[0:HEADS, :], ACT.Sqrt, scale=1.0 / HEAD,
                                 bias=keep.eps[0:HEADS, 1:2]).then_inc(root_done, 1)

        @block.vector
        def _(dve):
            link = Link(dve_link, dve)
            r_k = cols[:, COL["r_k"]:COL["r_k"] + PAIRS]
            nc.vector.tensor_tensor(slope[:], keep.half_ka[:], r_k, ALU.mult)
            nc.vector.tensor_tensor(offset[:], keep.rest_ka2[:], r_k, ALU.mult).then_inc(cols_done, 1)

            def add_directions(p):
                dve.wait_ge(y_in[p % 2], 32 * (p // 2 + 1))
                nc.vector.tensor_tensor(y[:, p % 2, 0, :], y[:, p % 2, 0, :], y[:, p % 2, 1, :], ALU.add).then_inc(y_sum, 1)

            def add_bonus(p):
                dve.wait_ge(bonus_mm, p + 1)
                nc.vector.tensor_tensor(bonus[:, p, :], sum_ps[:], rk[:, T_V + p, 0:SEQ], ALU.mult).then_inc(bonus_done, 1)

            add_directions(0)
            for p in range(PAIRS):
                dve.wait_ge(mean_mm, p + 1)
                nc.vector.scalar_tensor_tensor(centred[:, p, :], mean_ps[:], -1.0 / HEAD, y[:, p % 2, 0, :],
                                               ALU.mult, ALU.add).then_inc(centred_done, 1)
                if p + 1 < PAIRS:
                    add_directions(p + 1)
                if p:
                    add_bonus(p - 1)
                dve.wait_ge(prod_done, p + 1)
                dve.wait_ge(gain_done, p + 1)
                nc.vector.tensor_tensor(work[:], prod[:], gain[:], ALU.mult).then_inc(work_done, 1)
            add_bonus(PAIRS - 1)
            dve.wait_ge(root_done, 1)
            nc.vector.reciprocal(root[:], root[:]).then_inc(root_done, 1)
            dve.wait_ge(bonus_done, PAIRS)
            for p in range(PAIRS):
                b = p % 2
                dve.wait_ge(factor_mm, p + 1)
                if p >= 2:
                    dve.wait_ge(sent[b], 16)
                link(nc.vector.scalar_tensor_tensor(out[:, b, :], centred[:, p, :], col("gn_g", p), factor_ps[b][:], ALU.mult, ALU.mult))
                nc.vector.scalar_tensor_tensor(out[:, b, :], out[:, b, :], col("gn_b", p), bonus[:, p, :],
                                               ALU.add, ALU.add).then_inc(out_done, 1)


def normalise_latents(nc, sem, io, keep, stack):
    sb, ps = memory(nc, stack)
    lat, ql = sb("lat", [P, 4, NTOK]), sb("ql", [P, 3, SEQ])
    rope = sb("rope_k", [P, 2, SEQ])
    sq = sb("lat_sq", [P, 5, NTOK])
    pick, spread = sb("lat_pick", [P, 2, 2]), sb("lat_spread", [2, 2, P])
    root = sb("lat_root", [2, NTOK])
    val = sb("lat_val", [P, 2, NTOK])
    kr = sb("kr_val", [P, NTOK])
    mean_ps, factor_ps = ps("lat_mean", [P, 3 * 512]), [ps(f"lat_factor{i}", [P, (3 - i) * 512]) for i in range(2)]
    lat_land = [sem(f"lat_land{n}") for n in range(5)]
    kr_land, sq_done, ones_done, mean_mm, root_done, factor_mm = map(sem, (
        "kr_land", "lat_sq_done", "lat_ones_done", "lat_mean_mm", "lat_root_done", "lat_factor_mm"))
    val_done, hi_done, lo_done, dve_link, kr_done = map(sem, ("lat_val_done", "lat_hi_done", "lat_lo_done", "lat_dve", "kr_done"))
    pool_link = sem("lat_pool")
    parts = [(2, NTOK, KV_LORA, lat, "g_kv", keep.kvn_hi, keep.kvn_lo), (3, SEQ, Q_LORA, ql, "g_q", keep.qn_hi, keep.qn_lo)]
    items = [(i, k) for i, part in enumerate(parts) for k in range(part[0])]
    with nc.Block() as block:
        @block.sync
        def _(sp):
            for n, (i, k) in enumerate(items):
                dst, src = (lat, io["lat"]) if i == 0 else (ql, io["ql"])
                sp.dma_start(dst[:, k, :], src[k]).then_inc(lat_land[n], 16)
            for i in range(2):
                sp.dma_start(lat[64:P, 2 + i, :], io["lat"][2, 64 * i:64 * (i + 1)]).then_inc(kr_land, 16)
            for part, src in ((0, io["rope"][0:32, :]), (1, io["rope"][32:64, :])):
                for q in (64, 96):
                    sp.dma_start(rope[q:q + 32, part, :], src).then_inc(kr_land, 16)
            sp.dma_start(keep.rope_q[64:P, :], io["rope"]).then_inc(kr_land, 16)
            sp.wait_ge(kr_land, 7 * 16)

        @block.gpsimd
        def _(pool):
            link = Link(pool_link, pool)
            link(nc.gpsimd.memset(pick[:], 0.0))
            link(nc.gpsimd.memset(spread[:], 0.0))
            for i, part in enumerate(parts):
                link(nc.gpsimd.memset(pick[:, i, i:i + 1], 1.0 / part[2]))
            nc.gpsimd.affine_select(out=spread[:], in_=spread[:], compare_op=ALU.not_equal, fill=1.0, base=0,
                                    pattern=[[1, 2], [0, P]], channel_multiplier=-1).then_inc(ones_done, 1)
            for n, (i, k) in enumerate(items):
                _, e, _, _, _, hi, lo = parts[i]
                pool.wait_ge(hi_done, n + 1)
                nc.gpsimd.tensor_tensor(lo[:, k, 0:e], keep.kvn[:, k, :] if i == 0 else val[:, n % 2, 0:e],
                                        hi[:, k, 0:e].bitcast(F32), ALU.subtract).then_inc(lo_done, 1)

        @block.tensor
        def _(pe):
            pe.wait_ge(ones_done, 1)
            for n, (i, k) in enumerate(items):
                end = parts[i][1]
                pe.wait_ge(sq_done, n + 1)
                for a in range(0, end, 512):
                    last = nc.tensor.matmul(mean_ps[0:2, a:min(a + 512, end)], pick[:, i, :], sq[:, n, a:min(a + 512, end)],
                                            start=n == 0, stop=n == len(items) - 1 or (n == 1 and a >= SEQ))
            last.then_inc(mean_mm, 1)
            pe.wait_ge(root_done, 2)
            for i, part in enumerate(parts):
                for a in range(0, part[1], 512):
                    e = min(a + 512, part[1])
                    last = nc.tensor.matmul(factor_ps[i][:, a:e], spread[:, i, :], root[:, a:e], start=True, stop=True)
                last.then_inc(factor_mm, 1)

        @block.scalar
        def _(act):
            for n, (i, k) in enumerate(items):
                _, end, _, src, *_ = parts[i]
                act.wait_ge(lat_land[n], 16)
                nc.scalar.activation(sq[:, n, 0:end], src[:, k, 0:end], ACT.Square).then_inc(sq_done, 1)
            act.wait_ge(mean_mm, 1)
            nc.scalar.activation(root[:], mean_ps[0:2, 0:NTOK], ACT.Sqrt, bias=keep.eps[0:2, 0:1]).then_inc(root_done, 1)
            act.wait_ge(kr_done, 1)
            for b in range(2):
                last = nc.scalar.activation(keep.k_hi[b][64:P, :], kr[64:P, :], ACT.Copy)
            last.then_inc(kr_done, 1)
            for n, (i, k) in enumerate(items):
                end = parts[i][1]
                act.wait_ge(val_done, n + 1)
                nc.scalar.activation(parts[i][5][:, k, 0:end], keep.kvn[:, k, :] if i == 0 else val[:, n % 2, 0:end],
                                     ACT.Copy).then_inc(hi_done, 1)

        @block.vector
        def _(dve):
            link = Link(dve_link, dve)
            link(nc.vector.memset(keep.rope_q[0:64, :], 1.0))
            dve.wait_ge(kr_land, 7 * 16)
            low = slice(64, P)
            link(nc.vector.tensor_tensor(kr[low, 0:SEQ], lat[low, 2, 0:SEQ], rope[low, 0, :], ALU.mult))
            link(nc.vector.tensor_tensor(lat[low, 3, 0:SEQ], lat[low, 3, 0:SEQ], rope[low, 1, :], ALU.mult))
            nc.vector.tensor_copy(kr[low, SEQ:NTOK], lat[low, 2, SEQ:NTOK])
            nc.vector.tensor_tensor(kr[low, 0:SEQ], kr[low, 0:SEQ], lat[low, 3, 0:SEQ], ALU.add).then_inc(kr_done, 1)
            dve.wait_ge(root_done, 1)
            nc.vector.reciprocal(root[:], root[:]).then_inc(root_done, 1)
            dve.wait_ge(kr_done, 2)
            for b in range(2):
                last = nc.vector.tensor_tensor(keep.k_lo[b][low, :], kr[low, :], keep.k_hi[b][low, :].bitcast(F32), ALU.subtract)
            link(last)
            for n, (i, k) in enumerate(items):
                _, end, _, src, g, *_ = parts[i]
                dve.wait_ge(factor_mm, i + 1)
                if i and n >= 4:
                    dve.wait_ge(lo_done, n - 1)
                dst = keep.kvn[:, k, :] if i == 0 else val[:, n % 2, 0:end]
                nc.vector.scalar_tensor_tensor(dst, src[:, k, 0:end], cols_of(keep, g, k), factor_ps[i][:, 0:end],
                                               ALU.mult, ALU.mult).then_inc(val_done, 1)


def cols_of(keep, name, i):
    return keep.cols[:, COL[name] + i:COL[name] + i + 1]


def attention(nc, sem, io, keep, stack):
    sb, ps = memory(nc, stack)
    NQ = SEQ // P
    NW = 3 * P + 2 * NOPE
    AHEAD = 3
    GROUPS = NQ // 2
    PB = 4
    raw = sb("at_raw", [P, 2, NW])
    w_hi, w_lo = sb("at_w_hi", [P, 2, NW], F32R), sb("at_w_lo", [P, 2, NW], F32R)
    uv = sb("at_uv", [P, 2 * P])
    q_val = sb("at_q_val", [P, SEQ])
    q_hi, q_lo = sb("q_hi", [P, 2, SEQ], F32R), sb("q_lo", [P, 2, SEQ], F32R)
    v_hi, v_lo = sb("v_hi", [P, NT, P], F32R), sb("v_lo", [P, NT, P], F32R)
    probs = sb("probs", [P, PB, NTOK])
    pt_hi, pt_lo = sb("pt_hi", [P, NT, 4 * P], F32R), sb("pt_lo", [P, NT, 4 * P], F32R)
    top, total = sb("top", [P, PB, 1]), sb("total", [P, PB, 1])
    o_sb = sb("o_sb", [P, GROUPS, 2 * P])
    s_ps, ring = ps("s_ps", [P, 2, 3 * 512]), ps("ring_ps", [P, 2, 512])
    names = ("uv_land", "w_hi_done", "w_lo_done", "filled", "hi_done", "freed", "q_lo", "s_mm", "top_done",
             "exp_done", "total_done", "probs_done", "dve")
    S = {n: sem(f"at_{n}") for n in names}
    w_land = [sem(f"at_w_land{b}") for b in range(2)]
    o_sent = [sem(f"at_o_sent{g}") for g in range(GROUPS)]

    TURNS = [(0, 4), (4, 8), (8, NT)]
    VALUES = [("V", a, b) for a, b in ((0, 3), (3, 6), (6, 8), (8, NT))]

    def head_items(e):
        return ([("Q", e, 0, a, a + 512) for a in (0, 512)] +
                [("K", e, 0, a, min(a + 512, NTOK)) for a in range(0, NTOK, 512)])

    FIRST = head_items(-1)

    def extras(e, q, more):
        if e == 0:
            mine = head_items(0)
            return {0: VALUES[0:2], 1: VALUES[2:4], 2: mine[0:2], 3: mine[2:4], 4: mine[4:5]}.get(q, [])
        mine = head_items(1) if more else []
        return {1: mine[0:2], 2: mine[2:3], 3: mine[3:4], 4: mine[4:5]}.get(q, [])

    def step_items(e, q, more):
        made = extras(e, q, more)
        turns = [("T", e, q, a, b) for a, b in TURNS]
        if q == NQ - 1:
            return turns + [("O", e, GROUPS - 1)]
        before = [("O", e, q // 2 - 1)] if q % 2 == 0 and q else []
        return turns[:2] + before + turns[2:] + made

    def order(more):
        return [item for e in range(2) for q in range(NQ) for item in step_items(e, q, more)]

    ROUND = len(order(True))
    assert ROUND % 2 == 0

    def number(p, item, more=True):
        if item in FIRST:
            return FIRST.index(item), FIRST.index(item) % 2
        i = len(FIRST) + order(more).index(item)
        return i + p * ROUND, i % 2

    def steps(p, more):
        for e in range(2):
            for q in range(NQ):
                yield p * 2 + e, e, q

    def ahead(p, e, q, by, more):
        n = e * NQ + q + by
        if n >= 2 * NQ and not more:
            return None
        return p * 2 + n // NQ, (n // NQ) % 2, n % NQ

    def rounds(eng, link, body):
        with eng.Fori(0, PAIRS - 1) as p:
            if link is not None:
                link.enter(p, 2 * NQ)
            body(p, True)
        if link is not None:
            link.leave(PAIRS - 1)
        body(PAIRS - 1, False)

    with nc.Block() as block:
        @block.sync
        def _(sp):
            def load(h, e):
                sp.dma_start(raw[:, e, 0:3 * P], io["uq"][bass.ds(h, 1)].rearrange("a p n -> p (a n)")).then_inc(w_land[e], 16)
                sp.dma_start(raw[:, e, 3 * P:NW], io["uk"][bass.ds(h, 1)].rearrange("a p n -> p (a n)")).then_inc(w_land[e], 16)

            def load_uv(p):
                sp.dma_start(uv[:], io["uv"][bass.ds(p, 1)].rearrange("a p n -> p (a n)")).then_inc(S["uv_land"], 16)

            def body(p, more):
                for e in range(2):
                    h = p * 2 + e
                    if more:
                        sp.wait_ge(S["w_lo_done"], h + 1)
                        load(h + 2, e)
                    if more and e == 0:
                        sp.wait_ge(S["filled"], number(p, VALUES[-1])[0] + 1)
                        load_uv(p + 1)
                    for g in range(GROUPS):
                        sp.wait_ge(S["hi_done"], number(p, ("O", e, g), more)[0] + 1)
                        sp.dma_start(io["branch"][0, bass.ds(p, 1), e * HEAD:(e + 1) * HEAD, g * 2 * P:(g + 1) * 2 * P]
                                     .rearrange("a p t -> p (a t)"),
                                     o_sb[e * HEAD:(e + 1) * HEAD, g, :]).then_inc(o_sent[g], 16)

            load(0, 0)
            load_uv(0)
            load(1, 1)
            rounds(sp, None, body)
            for g in range(GROUPS):
                sp.wait_ge(o_sent[g], 16 + 16 * HEADS)

        @block.gpsimd
        def _(pool):
            def split_lo(h, e):
                pool.wait_ge(S["w_hi_done"], h + 1)
                nc.gpsimd.tensor_tensor(w_lo[:, e, :], raw[:, e, :], w_hi[:, e, :].bitcast(F32),
                                        ALU.subtract).then_inc(S["w_lo_done"], 1)

            def query_lo(p, item, h, e, more):
                _, _, _, a, b = item
                pool.wait_ge(S["hi_done"], number(p, item, more)[0] + 1)
                nc.gpsimd.tensor_tensor(q_lo[:, e, a:b], q_val[:, a:b], q_hi[:, e, a:b].bitcast(F32),
                                        ALU.subtract).then_inc(S["q_lo"], 1)

            def normalise(h, q):
                pool.wait_ge(S["total_done"], h * NQ + q + 1)
                b = q % PB
                nc.gpsimd.tensor_tensor(probs[:, b, :], probs[:, b, :], total[:, b, :].broadcast_to([P, NTOK]),
                                        ALU.mult).then_inc(S["probs_done"], 1)

            def body(p, more):
                for h, e, q in steps(p, more):
                    later = ahead(p, e, q, 1, more)
                    if later:
                        normalise(later[0], later[2])
                    if q == 0 and (more or e == 0):
                        split_lo(h + 1, 1 - e)
                    for item in extras(e, q, more):
                        if item[0] == "Q":
                            query_lo(p, item, h + 1, 1 - e, more)

            pool.sem_inc(S["q_lo"], 2)
            split_lo(0, 0)
            for item in FIRST[0:2]:
                query_lo(0, item, 0, 0, True)
            normalise(0, 0)
            rounds(pool, None, body)

        @block.tensor
        def _(pe):
            def passes(out, ws, hs, first, end):
                for n, (w, x) in enumerate(((ws[0], hs[0]), (ws[0], hs[1]), (ws[1], hs[0]))):
                    last = nc.tensor.matmul(out, w, x, start=first and n == 0, stop=end and n == 2)
                return last

            def fill(p, item, h, e, more):
                i, bank = number(p, item, more)
                pe.wait_ge(S["freed"], i + 1)
                if item[0] == "V":
                    for t in range(item[1], item[2]):
                        for k in range(2):
                            last = nc.tensor.matmul(ring[:, bank, (t - item[1]) * P:(t - item[1] + 1) * P],
                                                    keep.kvn[:, k, t * P:(t + 1) * P], uv[:, k * P:(k + 1) * P],
                                                    start=k == 0, stop=k == 1)
                    last.then_inc(S["filled"], 1)
                    return
                _, _, _, a, b = item
                if item[0] == "Q":
                    for k in range(3):
                        last = passes(ring[:, bank, :], (w_hi[:, e, k * P:(k + 1) * P], w_lo[:, e, k * P:(k + 1) * P]),
                                      (keep.qn_hi[:, k, a:b], keep.qn_lo[:, k, a:b]), k == 0, k == 2)
                else:
                    for k in range(2):
                        c = 3 * P + k * NOPE
                        last = passes(ring[0:HEAD, bank, 0:b - a], (w_hi[:, e, c:c + NOPE], w_lo[:, e, c:c + NOPE]),
                                      (keep.kvn_hi[:, k, a:b], keep.kvn_lo[:, k, a:b]), k == 0, k == 1)
                last.then_inc(S["filled"], 1)

            def scores(h, e, q, last_key, piece=None):
                if q == 0 and not piece:
                    pe.wait_ge(S["freed"], last_key + 3)
                    pe.wait_ge(S["q_lo"], h * 2 + 4)
                if not piece:
                    pe.wait_ge(S["exp_done"], h * NQ + q + 1)
                c = q * P
                for a in range(0, NTOK, 512) if piece is None else [piece * 512]:
                    b = min(a + 512, NTOK)
                    last = passes(s_ps[:, q % 2, a:b], (q_hi[:, e, c:c + P], q_lo[:, e, c:c + P]),
                                  (keep.k_hi[e][:, a:b], keep.k_lo[e][:, a:b]), True, True)
                if b == NTOK:
                    last.then_inc(S["s_mm"], 1)

            def turn(p, item, more):
                _, e, q, a, b = item
                i, bank = number(p, item, more)
                pe.wait_ge(S["freed"], i + 1)
                for t in range(a, b):
                    last = nc.tensor.transpose(ring[:, bank, (t - a) * P:(t - a + 1) * P],
                                               probs[:, q % PB, t * P:(t + 1) * P], keep.ident[:])
                last.then_inc(S["filled"], 1)

            def outputs(p, item, more, newest):
                i, bank = number(p, item, more)
                pe.wait_ge(S["freed"], i + 1 + newest)
                at = slice((item[2] % 2) * 2 * P, (item[2] % 2 + 1) * 2 * P)
                for t in range(NT):
                    last = passes(ring[:, bank, 0:2 * P], (v_hi[:, t, :], v_lo[:, t, :]), (pt_hi[:, t, at], pt_lo[:, t, at]),
                                  t == 0, t == NT - 1)
                last.then_inc(S["filled"], 1)

            def body(p, more):
                for h, e, q in steps(p, more):
                    later = ahead(p, e, q, AHEAD, more)
                    last_key = number(p, head_items(e)[-1], more)[0] if q >= NQ - AHEAD and later else None
                    items = step_items(e, q, more)
                    place = {0: 0, 1: 2, 2: 2} if q == NQ - 1 else {0: 0, 1: 1, 2: 3}
                    for n, item in enumerate(items + [None] * (4 - len(items))):
                        if item and item[0] == "T":
                            if n == 0:
                                pe.wait_ge(S["probs_done"], h * NQ + q + 1)
                            turn(p, item, more)
                        elif item and item[0] == "O":
                            outputs(p, item, more, 1 if n == 3 else 0)
                        elif item:
                            if item == VALUES[0]:
                                pe.wait_ge(S["uv_land"], p * 16 + 16)
                            if item[0] == "Q" and item[3] == 0:
                                pe.wait_ge(S["w_lo_done"], h + 2)
                            fill(p, item, h + 1, 1 - e, more)
                        for piece in place:
                            if place[piece] == n and later:
                                scores(*later, last_key, piece=piece)

            pe.wait_ge(S["w_lo_done"], 1)
            for item in FIRST:
                fill(0, item, 0, 0, True)
            for q in range(AHEAD):
                scores(0, 0, q, number(0, FIRST[-1])[0])
            rounds(pe, None, body)

        @block.scalar
        def _(act):
            def split_hi(h, p, e):
                act.wait_ge(w_land[e], p * 32 + 32)
                nc.scalar.activation(w_hi[:, e, :], raw[:, e, :], ACT.Copy).then_inc(S["w_hi_done"], 1)

            def hi(p, item, e, more):
                i, bank = number(p, item, more)
                if item[0] == "Q":
                    act.wait_ge(S["freed"], i + 3)
                    _, _, _, a, b = item
                    dst, src = q_hi[:, e, a:b], q_val[:, a:b]
                elif item[0] == "K":
                    act.wait_ge(S["filled"], i + 1)
                    _, _, _, a, b = item
                    dst, src = keep.k_hi[e][0:HEAD, a:b], ring[0:HEAD, bank, 0:b - a]
                else:
                    act.wait_ge(S["filled"], i + 1)
                    a, b = item[-2:]
                    src = ring[:, bank, 0:(b - a) * P].rearrange("p (t c) -> p t c", c=P)
                    dst = v_hi[:, a:b, :] if item[0] == "V" else pt_hi[:, a:b, (item[2] % 4) * P:(item[2] % 4 + 1) * P]
                nc.scalar.activation(dst, src, ACT.Copy).then_inc(S["hi_done"], 1)

            def exponentials(h, q):
                act.wait_ge(S["top_done"], h * NQ + q + 1)
                b = q % PB
                nc.scalar.activation(probs[:, b, :], s_ps[:, q % 2, 0:NTOK], ACT.Exp, scale=SCALE,
                                     bias=top[:, b, :], accum_out=total[:, b, :]).then_inc(S["exp_done"], 1)

            def body(p, more):
                for h, e, q in steps(p, more):
                    if q == 0 and (more or e == 0):
                        split_hi(h + 1, p + e, 1 - e)
                    items = step_items(e, q, more)
                    for n, item in enumerate(items):
                        if item[0] == "O":
                            out(p, h, e, item[2], more)
                        else:
                            hi(p, item, e if item[0] == "T" else 1 - e, more)
                        later = ahead(p, e, q, AHEAD - 1, more)
                        if n == (0 if items[2][0] == "O" else 2) and later:
                            exponentials(later[0], later[2])

            def out(p, h, e, g, more):
                i, bank = number(p, ("O", e, g), more)
                act.wait_ge(S["filled"], i + 1)
                act.wait_ge(o_sent[g], h * 16 + 16)
                part = slice(e * HEAD, (e + 1) * HEAD)
                nc.scalar.activation(o_sb[part, g, :], ring[part, bank, 0:2 * P], ACT.Copy).then_inc(S["hi_done"], 1)

            for g in range(GROUPS):
                act.sem_inc(o_sent[g], 16)
            act.sem_inc(S["exp_done"], 2)
            split_hi(0, 0, 0)
            for item in FIRST:
                hi(0, item, 0, True)
            for q in range(AHEAD - 1):
                exponentials(0, q)
            rounds(act, None, body)

        @block.vector
        def _(dve):
            link = Link(S["dve"], dve)

            def lo(p, item, h, e, more):
                i, bank = number(p, item, more)
                if item[0] == "Q":
                    _, _, _, a, b = item
                    dve.wait_ge(S["filled"], i + 1)
                    dve.wait_ge(S["q_lo"], h * 2 + a // 512 + 1)
                    nc.vector.tensor_tensor(q_val[:, a:b], ring[:, bank, :], keep.rope_q[:, a:b],
                                            ALU.mult).then_inc(S["freed"], 1)
                    return
                dve.wait_ge(S["hi_done"], i + 1)
                if item[0] == "K":
                    _, _, _, a, b = item
                    part = (slice(0, HEAD), slice(a, b))
                    dst, src, hi = keep.k_lo[e][part], ring[0:HEAD, bank, 0:b - a], keep.k_hi[e][part]
                else:
                    a, b = item[-2:]
                    src = ring[:, bank, 0:(b - a) * P].rearrange("p (t c) -> p t c", c=P)
                    if item[0] == "V":
                        dst, hi = v_lo[:, a:b, :], v_hi[:, a:b, :]
                    else:
                        part = (slice(None), slice(a, b), slice((item[2] % 4) * P, (item[2] % 4 + 1) * P))
                        dst, hi = pt_lo[part], pt_hi[part]
                nc.vector.tensor_tensor(dst, src, hi.bitcast(F32), ALU.subtract).then_inc(S["freed"], 1)

            def maximum(h, q):
                b = q % PB
                dve.wait_ge(S["s_mm"], h * NQ + q + 1)
                link(nc.vector.reduce_max(top[:, b, :], s_ps[:, q % 2, 0:NTOK], AX.X))
                nc.vector.tensor_scalar(top[:, b, :], top[:, b, :], -SCALE, None, ALU.mult).then_inc(S["top_done"], 1)

            def invert(h, q):
                dve.wait_ge(S["exp_done"], h * NQ + q + 3)
                nc.vector.reciprocal(total[:, q % PB, :], total[:, q % PB, :]).then_inc(S["total_done"], 1)

            def body(p, more):
                for h, e, q in steps(p, more):
                    items = step_items(e, q, more)
                    scored = 3 if len(items) > 3 and items[3][0] != "O" else 2
                    for n, item in enumerate(items):
                        if item[0] == "O":
                            dve.wait_ge(S["hi_done"], number(p, item, more)[0] + 1)
                            dve.wait_ge(S["freed"], number(p, item, more)[0] + 2)
                            dve.sem_inc(S["freed"], 1)
                        elif item[0] == "T":
                            lo(p, item, h, e, more)
                        else:
                            lo(p, item, h + 1, 1 - e, more)
                        later = ahead(p, e, q, 1, more)
                        if n == 0 and later:
                            invert(later[0], later[2])
                        later = ahead(p, e, q, AHEAD, more)
                        if n == scored and later:
                            maximum(later[0], later[2])

            dve.sem_inc(S["freed"], 2)
            for item in FIRST:
                lo(0, item, 0, 0, True)
            for q in range(AHEAD):
                maximum(0, q)
            invert(0, 0)
            rounds(dve, link, body)


def gate_branches(nc, sem, io, keep, stack):
    sb, ps = memory(nc, stack)
    ring = WeightRing(nc, sem, stack, "gb", raws=1)
    out_ps = ps("gb_ps", [P, 3, 1024])
    pad = sb("conv_u", [P, SEQ + 2])
    conv = sb("conv_sum", [P, SEQ])
    th, val = sb("gate_th", [P, SEQ]), sb("gate_val", [P, SEQ])
    y = sb("branch_y", [P, 2, SEQ])
    cols = keep.cols
    S = {n: sem(f"gb_{n}") for n in ("drained", "in_done", "th_done", "val_done", "hi_done", "lo_done",
                                     "link", "y_used", "y_in")}
    h_in = [sem(f"gb_h_in{k}") for k in range(KD)]
    IN, C, B, GATES = 0, 1, 2, (3, 4, 5)
    ORDER = (1, 0, 2)
    def lo_part(pool, c, g):
        hi, lo = keep.branch[ORDER[g]]
        pool.wait_ge(S["hi_done"], c * 3 + g + 1)
        at = (slice(None), bass.ds(c, 1), slice(None))
        nc.gpsimd.tensor_tensor(lo[at].rearrange("p a t -> p (a t)"), val[:],
                                hi[at].rearrange("p a t -> p (a t)").bitcast(F32), ALU.subtract).then_inc(S["lo_done"], 1)

    def evacuate(act, c, t):
        if t == IN:
            act.wait_ge(ring.used, c * 6 + t + 3)
            act.wait_ge(S["val_done"], c * 3 + 1)
            nc.scalar.activation(th[:], out_ps[:, t % 3, :], ACT.Copy).then_inc(S["in_done"], 1)
        if t in GATES:
            g = t - 3
            act.wait_ge(ring.used, c * 6 + t + 3)
            if g:
                act.wait_ge(S["val_done"], c * 3 + g + 1)
            else:
                act.wait_ge(S["drained"], c * 6 + 5)
            nc.scalar.activation(th[:], out_ps[:, t % 3, :], ACT.Tanh, scale=0.5).then_inc(S["th_done"], 1)
            act.wait_ge(S["val_done"], c * 3 + g + 2)
            hi = keep.branch[ORDER[g]][0]
            nc.scalar.activation(hi[:, bass.ds(c, 1), :].rearrange("p a t -> p (a t)"), val[:],
                                 ACT.Copy).then_inc(S["hi_done"], 1)

    with nc.Block() as block:
        @block.sync
        def _(sp):
            with sp.Fori(0, PAIRS) as c:
                for t in range(6):
                    ring.load(sp, io["w_in"][c * 6 + (T_F + t), :, :], c * 6 + t, t % 2)
                    if t == 2:
                        sp.wait_ge(S["y_used"], c + 1)
                        sp.dma_start(y[:], io["branch"][:, bass.ds(c, 1)].rearrange("b a p t -> p (a b) t")).then_inc(S["y_in"], 16)

        @block.gpsimd
        def _(pool):
            pool.sem_inc(ring.lo_made, 2)
            pool.sem_inc(S["lo_done"], 1)
            def body(c, more):
                for t in range(6):
                    if t < 5 or more:
                        ring.split_lo(pool, c * 6 + t + 1, (t + 1) % 2)
                    if t in GATES:
                        lo_part(pool, c, t - 3)

            ring.split_lo(pool, 0, 0)
            with pool.Fori(0, PAIRS - 1) as c:
                body(c, True)
            body(PAIRS - 1, False)

        @block.tensor
        def _(pe):
            pe.sem_inc(ring.used, 2)
            with pe.Fori(0, PAIRS) as c:
                for t in range(6):
                    ring.wait(pe, c * 6 + t)
                    pe.wait_ge(S["drained"], c * 6 + t + 1)
                    outs = [(out_ps[:, t % 3, a:a + 512], a, a + 512) for a in (0, 512)]
                    landed = (lambda k: pe.wait_ge(h_in[k], 32)) if t == 0 else None
                    ring.products(t % 2, keep.h_hi, keep.h_lo, outs, before=landed).then_inc(ring.used, 1)

        @block.scalar
        def _(act):
            def body(c, more):
                for t in range(6):
                    if t < 5 or more:
                        ring.split_hi(act, c * 6 + t + 1, (t + 1) % 2, c * 3 + (t + 1) // 2)
                    evacuate(act, c, t)

            for k in range(KD):
                for part, h in enumerate((keep.h_hi, keep.h_lo)):
                    act.dma_start(h[:, k, :].bitcast(F32), io["h"][part, :, k, :]).then_inc(h_in[k], 16)
            ring.split_hi(act, 0, 0, 0)
            with act.Fori(0, PAIRS - 1) as c:
                body(c, True)
            body(PAIRS - 1, False)

        @block.vector
        def _(dve):
            link = Link(S["link"], dve)
            dve.sem_inc(S["drained"], 3)
            dve.sem_inc(S["val_done"], 1)
            dve.sem_inc(S["y_used"], 1)
            link(nc.vector.memset(pad[:], 0.0))
            with dve.Fori(0, PAIRS) as c:
                link.enter(c, 8)
                col = lambda name, i=0: cols[:, bass.ds(c + (COL[name] + i), 1)]
                dve.wait_ge(S["in_done"], c + 1)
                dve.sem_inc(S["drained"], 1)
                dve.wait_ge(ring.used, c * 6 + C + 3)
                link(nc.vector.tensor_tensor(pad[:, 1:SEQ + 1], out_ps[:, C % 3, :], th[:], ALU.mult))
                dve.sem_inc(S["drained"], 1)
                link(nc.vector.tensor_scalar(conv[:], pad[:, 0:SEQ], col("conv_w"), col("conv_b"), ALU.mult, ALU.add))
                link(nc.vector.scalar_tensor_tensor(conv[:], pad[:, 1:SEQ + 1], col("conv_w", 4), conv[:], ALU.mult, ALU.add))
                link(nc.vector.scalar_tensor_tensor(conv[:], pad[:, 2:SEQ + 2], col("conv_w", 8), conv[:], ALU.mult, ALU.add))
                dve.wait_ge(ring.used, c * 6 + B + 3)
                link(nc.vector.tensor_tensor(conv[:], out_ps[:, B % 3, :], conv[:], ALU.mult))
                dve.sem_inc(S["drained"], 1)
                for g in range(3):
                    t = 3 + g
                    dve.wait_ge(S["th_done"], c * 3 + g + 1)
                    link(nc.vector.scalar_tensor_tensor(th[:], th[:], 1.0, out_ps[:, t % 3, :], ALU.add, ALU.mult))
                    dve.sem_inc(S["drained"], 1)
                    dve.wait_ge(S["lo_done"], c * 3 + g + 1)
                    src = conv[:] if g == 0 else y[:, g - 1, :]
                    if g:
                        dve.wait_ge(S["y_in"], c * 16 + 16)
                    nc.vector.scalar_tensor_tensor(val[:], src, 0.5, th[:], ALU.mult, ALU.mult).then_inc(S["val_done"], 1)
                    dve.wait_ge(S["val_done"], c * 3 + g + 2)
                dve.sem_inc(S["y_used"], 1)
            link.leave(PAIRS)


def merge(nc, sem, io, keep, stack):
    sb, ps = memory(nc, stack)
    ring = WeightRing(nc, sem, stack, "mg", D + W, raws=1)
    out_ps = ps("mg_ps", [P, 2, 2, 1024])
    th, term = sb("mg_th", [P, 2, SEQ]), sb("mg_term", [P, SEQ])
    acc = sb("mg_acc", [P, SEQ])
    S = {n: sem(f"mg_{n}") for n in ("th_done", "drained", "link", "acc_done", "summed")}
    sent = sem("mg_sent")
    TILES = 6
    def gate(act, i, t):
        act.wait_ge(ring.used, i * TILES + t + 3)
        act.wait_ge(S["drained"], i * TILES + t + 1)
        nc.scalar.activation(th[:, t % 2, :], out_ps[:, t % 2, 0, :], ACT.Tanh, scale=0.5).then_inc(S["th_done"], 1)

    def store(act, i, b):
        act.wait_ge(S["acc_done"], i * 2 + b + 1)
        act.dma_start(io["merged"][bass.ds(i * 2 + b, 1)].rearrange("a p t -> p (a t)"), acc[:]).then_inc(sent, 16)

    with nc.Block() as block:
        @block.sync
        def _(sp):
            with sp.Fori(0, KD // 2) as i:
                for t in range(TILES):
                    ring.load(sp, io["w_merge"][i * TILES + t, :, :], i * TILES + t, t % 2)

        @block.gpsimd
        def _(pool):
            pool.sem_inc(ring.lo_made, 2)
            with pool.Fori(0, KD // 2) as i:
                for t in range(TILES):
                    ring.split_lo(pool, i * TILES + t, t % 2)

        @block.tensor
        def _(pe):
            pe.sem_inc(ring.used, 2)
            with pe.Fori(0, KD // 2) as i:
                for t in range(TILES):
                    ring.wait(pe, i * TILES + t)
                    pe.wait_ge(S["drained"], i * TILES + t + 1)
                    b = t % 2
                    outs = lambda j: [(out_ps[:, b, j, a:a + 512], a, a + 512) for a in (0, 512)]
                    ring.products(b, keep.h_hi, keep.h_lo, outs(0))
                    ring.products(b, *keep.branch[t % 3], outs(1), at=D, tiles=PAIRS).then_inc(ring.used, 1)

        @block.scalar
        def _(act):
            act.sem_inc(sent, 16)
            def body(i, more):
                for t in range(TILES):
                    if t < TILES - 1 or more:
                        ring.split_hi(act, i * TILES + t + 1, (t + 1) % 2, i * 3 + (t + 1) // 2)
                    gate(act, i, t)
                    if t % 3 == 2:
                        store(act, i, t // 3)

            ring.split_hi(act, 0, 0, 0)
            with act.Fori(0, KD // 2 - 1) as i:
                body(i, True)
            body(KD // 2 - 1, False)
            act.wait_ge(sent, 16 + 16 * KD)

        @block.vector
        def _(dve):
            link = Link(S["link"], dve)
            dve.sem_inc(S["drained"], 2)
            with dve.Fori(0, KD // 2) as i:
                link.enter(i, 6)
                for t in range(TILES):
                    b = t // 3
                    dve.wait_ge(S["th_done"], i * TILES + t + 1)
                    if t % 3 == 0:
                        dve.wait_ge(sent, (i * 2 + b) * 16 + 16)
                    dst = term[:] if t % 3 else acc[:]
                    link(nc.vector.scalar_tensor_tensor(dst, th[:, t % 2, :], 1.0, out_ps[:, t % 2, 1, :],
                                                        ALU.add, ALU.mult))
                    dve.sem_inc(S["drained"], 1)
                    if t % 3:
                        last = nc.vector.tensor_tensor(acc[:], acc[:], term[:], ALU.add)
                        if t % 3 == 2:
                            last.then_inc(S["acc_done"], 1)
                            dve.wait_ge(S["acc_done"], i * 2 + b + 1)
                        else:
                            last.then_inc(S["summed"], 1)
                            dve.wait_ge(S["summed"], i * 2 + b + 1)
            link.leave(KD // 2)


def project_out(nc, sem, io, keep, stack):
    sb, ps = memory(nc, stack)
    RAWS, FIRST = 4, 3
    raw = sb("po_raw", [P, RAWS, D])
    w_hi, w_lo = sb("po_w_hi", [P, KD, D], F32R), sb("po_w_lo", [P, KD, D], F32R)
    m_hi, m_lo = sb("po_m_hi", [P, KD, SEQ], F32R), sb("po_m_lo", [P, KD, SEQ], F32R)
    gate, wide = sb("po_gate", [P, D]), sb("po_wide", [P, KD, P])
    res, x_in, junk = sb("po_res", [P, 2, D]), sb("po_x", [P, 2, D]), sb("po_junk", [P, D])
    ss = sb("po_ss", [P, 2, 2])
    out_ps = ps("po_ps", [P, FIRST, 1024])
    gate_ps = ps("po_gate_ps", [P, 1024])
    S = {n: sem(f"po_{n}") for n in ("hi_done", "w_parts", "m_parts", "wide_done", "gate_mm", "mm", "sq_done",
                                     "root_done", "res_done", "link")}
    land = [sem(f"po_land{b}") for b in range(RAWS)]
    x_land = [sem(f"po_x_land{b}") for b in range(2)]
    sent = [sem(f"po_sent{b}") for b in range(2)]
    items = [(kind, k) for k in range(KD) for kind in ("w", "m")]
    NQ = SEQ // P
    with nc.Block() as block:
        @block.sync
        def _(sp):
            for n, (kind, k) in enumerate(items):
                if n >= RAWS:
                    sp.wait_ge(S["w_parts" if kind == "w" else "m_parts"], (n - RAWS) // 2 + 1)
                src = io["w_out"][k * P:(k + 1) * P, :] if kind == "w" else io["merged"][k]
                sp.dma_start(raw[:, n % RAWS, :], src).then_inc(land[n % RAWS], 16)
            for t in range(NQ):
                if t >= 2:
                    sp.wait_ge(S["res_done"], t - 1)
                sp.dma_start(x_in[:, t % 2, :], io["x"][t * P:(t + 1) * P, :]).then_inc(x_land[t % 2], 16)
            for b in range(2):
                sp.wait_ge(sent[b], 16 * NQ // 2)

        @block.gpsimd
        def _(pool):
            for n, (kind, k) in enumerate(items):
                if kind == "w":
                    pool.wait_ge(S["hi_done"], n + 1)
                    nc.gpsimd.tensor_tensor(w_lo[:, k, :], raw[:, n % RAWS, :], w_hi[:, k, :].bitcast(F32),
                                            ALU.subtract).then_inc(S["w_parts"], 1)

        @block.scalar
        def _(act):
            for n, (kind, k) in enumerate(items):
                act.wait_ge(land[n % RAWS], 16 * (n // RAWS + 1))
                nc.scalar.activation((w_hi if kind == "w" else m_hi)[:, k, :], raw[:, n % RAWS, :], ACT.Copy).then_inc(S["hi_done"], 1)
            for t in range(NQ):
                act.wait_ge(S["mm"], t + 1)
                if t >= 2:
                    act.wait_ge(S["res_done"], t - 1)
                nc.scalar.activation(junk[:], out_ps[:, t % FIRST, :], ACT.Square, scale=0.5,
                                     accum_out=ss[:, t % 2, 0:1]).then_inc(S["sq_done"], 1)
                act.wait_ge(S["sq_done"], t + 1)
                nc.scalar.activation(ss[:, t % 2, 1:2], ss[:, t % 2, 0:1], ACT.Sqrt, scale=1.0 / D,
                                     bias=keep.eps[:, 0:1]).then_inc(S["root_done"], 1)
                act.wait_ge(S["res_done"], t + 1)
                act.dma_start(io["out"][t * P:(t + 1) * P, :], res[:, t % 2, :]).then_inc(sent[t % 2], 16)

        @block.tensor
        def _(pe):
            pe.wait_ge(S["wide_done"], 1)
            for k in range(KD):
                last = nc.tensor.matmul(gate_ps[:, k * P:(k + 1) * P], wide[:, k, :], keep.ident[:], start=True, stop=True)
            last.then_inc(S["gate_mm"], 1)

            def products(t, k):
                for m, w in ((m_hi, w_hi), (m_hi, w_lo), (m_lo, w_hi)):
                    for a in (0, 512):
                        last = nc.tensor.matmul(out_ps[:, t % FIRST, a:a + 512], m[:, k, t * P:(t + 1) * P], w[:, k, a:a + 512],
                                                start=k == 0 and m is m_hi and w is w_hi, stop=k == KD - 1 and m is m_lo)
                if k == KD - 1:
                    last.then_inc(S["mm"], 1)

            for k in range(KD):
                pe.wait_ge(S["w_parts"], k + 1)
                pe.wait_ge(S["m_parts"], k + 1)
                for t in range(FIRST):
                    products(t, k)
            for t in range(FIRST, NQ):
                pe.wait_ge(S["res_done"], t - FIRST + 1)
                for k in range(KD):
                    products(t, k)

        @block.vector
        def _(dve):
            link = Link(S["link"], dve)
            link(nc.vector.memset(wide[:], 1.0))
            for k in range(KD):
                last = nc.vector.tensor_scalar(wide[:, k, :], wide[:, k, :], keep.gate_cols[:, k:k + 1], None, ALU.mult)
            last.then_inc(S["wide_done"], 1)
            for n, (kind, k) in enumerate(items):
                if kind == "m":
                    dve.wait_ge(S["hi_done"], n + 1)
                    nc.vector.tensor_tensor(m_lo[:, k, :], raw[:, n % RAWS, :], m_hi[:, k, :].bitcast(F32),
                                            ALU.subtract).then_inc(S["m_parts"], 1)
            dve.wait_ge(S["gate_mm"], 1)
            link(nc.vector.tensor_copy(gate[:], gate_ps[:]))
            for t in range(NQ):
                dve.wait_ge(S["root_done"], t + 1)
                link(nc.vector.reciprocal(ss[:, t % 2, 1:2], ss[:, t % 2, 1:2]))
                if t >= 2:
                    dve.wait_ge(sent[t % 2], 16 * (t // 2))
                link(nc.vector.scalar_tensor_tensor(res[:, t % 2, :], out_ps[:, t % FIRST, :], ss[:, t % 2, 1:2], gate[:],
                                                    ALU.mult, ALU.mult))
                dve.wait_ge(x_land[t % 2], 16 * (t // 2 + 1))
                nc.vector.tensor_tensor(res[:, t % 2, :], res[:, t % 2, :], x_in[:, t % 2, :], ALU.add).then_inc(S["res_done"], 1)


def phases(nc, io, keep):
    def run(phase, stack):
        sems = []

        def sem(name):
            sems.append(nc.alloc_semaphore(name))
            return sems[-1]

        phase(nc, sem, io, keep, stack)
        nc.clear_and_free_semaphores(sems)
        nc.all_engine_barrier()

    with ExitStack() as first:
        sb, _ = memory(nc, first)
        keep.rk = sb("rk", [P, T_KV, NTOK])
        keep.r = sb("r", [P, PAIRS, SEQ])
        keep.m_strict = sb("m_strict", [P, 4, P], U8)
        keep.m_level = [sb(f"m_level{j}", [P, 4, P], U8) for j in range(7)]
        with ExitStack() as hbuf:
            sbh, _ = memory(nc, hbuf)
            keep.h_hi, keep.h_lo = sbh("h_hi", [P, KD, NTOK], F32R), sbh("h_lo", [P, KD, NTOK], F32R)
            with ExitStack() as own:
                run(start, own)
            with ExitStack() as own:
                run(project, own)
        keep.up = sb("up", [P, 4 * W])
        keep.head_ones, keep.ones = sb("head_ones", [P, P]), sb("ones", [P, P])
        keep.half_w0, keep.half_a0 = sb("half_w0", [P, 8]), sb("half_a0", [P, 8])
        keep.half_ka, keep.rest_ka, keep.rest_ka2 = (sb(n, [P, 4]) for n in ("half_ka", "rest_ka", "rest_ka2"))
        with ExitStack() as own:
            sb, _ = memory(nc, own)
            keep.kk = sb("kk", [P, PAIRS, NTOK])
            keep.state = sb("state", [P, 2 * PAIRS, P])
            keep.nt, keep.x1t = ([sb(f"{name}{s}", [P, 4, P]) for s in range(2)] for name in ("nt", "x1t"))
            keep.wp = [[sb(f"wp{s}{j}", [P, 4, P]) for j in range(6)] for s in range(2)]
            keep.bkz = [sb(f"bkz{s}", [P, 2, 2, 2, P]) for s in range(2)]
            with ExitStack() as prep:
                run(prepare_rwkv, prep)
            with ExitStack() as prep:
                run(recurrence, prep)
        with ExitStack() as own:
            run(finish_rwkv, own)
    with ExitStack() as second:
        sb, _ = memory(nc, second)
        keep.kvn, keep.rope_q = sb("kvn", [P, 2, NTOK]), sb("rope_q", [P, SEQ])
        keep.kvn_hi, keep.kvn_lo = sb("kvn_hi", [P, 2, NTOK], F32R), sb("kvn_lo", [P, 2, NTOK], F32R)
        keep.qn_hi, keep.qn_lo = sb("qn_hi", [P, 3, SEQ], F32R), sb("qn_lo", [P, 3, SEQ], F32R)
        keep.k_hi = [sb(f"k_hi{b}", [P, NTOK], F32R) for b in range(2)]
        keep.k_lo = [sb(f"k_lo{b}", [P, NTOK], F32R) for b in range(2)]
        with ExitStack() as own:
            run(normalise_latents, own)
        with ExitStack() as own:
            run(attention, own)
    with ExitStack() as third:
        sb, _ = memory(nc, third)
        keep.h_hi, keep.h_lo = sb("hx_hi", [P, KD, SEQ], F32R), sb("hx_lo", [P, KD, SEQ], F32R)
        keep.branch = [(sb(f"b{b}_hi", [P, PAIRS, SEQ], F32R), sb(f"b{b}_lo", [P, PAIRS, SEQ], F32R)) for b in range(3)]
        with ExitStack() as own:
            run(gate_branches, own)
        with ExitStack() as own:
            run(merge, own)
    with ExitStack() as own:
        run(project_out, own)


def build(nc, io):
    with ExitStack() as always:
        sb, _ = memory(nc, always)
        keep = Kept()
        keep.cols, keep.ident = sb("cols", [P, NCOL]), sb("ident", [P, P])
        keep.silu_c, keep.eps = sb("silu_c", [P, KD, 2]), sb("eps", [P, len(EPS)])
        keep.gate_cols = sb("gate_cols", [P, KD])
        phases(nc, io, keep)


def scratch(nc, io):
    new = lambda name, shape, dt=F32: nc.dram_tensor(name, shape, dt).ap()
    io["y"] = new("y_scratch", (2, PAIRS, P, SEQ))
    io["h"] = new("h_scratch", (2, P, KD, SEQ))
    io["lat"] = new("lat_scratch", (3, P, NTOK))
    io["ql"] = new("ql_scratch", (3, P, SEQ))
    io["branch"] = new("branch_scratch", (2, PAIRS, P, SEQ))
    io["merged"] = new("merged_scratch", (KD, P, SEQ))


def vectors(a):
    import numpy as np
    rows = [a["c"], a["c_ctx"], a["b_mod"], a["g_pre"]] + [a[n] for n, _ in COLS[4:]]
    return np.ascontiguousarray(np.concatenate([np.reshape(r, (-1, P)) for r in rows]).T)


def feature_tiles(w, n=P):
    import numpy as np
    c, f = w.shape
    return np.ascontiguousarray(w.reshape(c // P, P, f // n, n).transpose(2, 1, 0, 3).reshape(f // n, P, -1))


def laid_out(a):
    import numpy as np
    w = a["w_in"][0]
    at = np.cumsum([0, 384, 256, 32, 512, 512, 512, 512, 512, 512, 512, 512, 64, 64, 64, 64, 512, 3072])
    (ql, kv, kr, gm, ci, cb, cc, gc, r, k, v, wdf, wdb, adf, adb, gr, gl) = [w[:, s:e] for s, e in zip(at, at[1:])]
    rot, swap = (np.concatenate([kr[:, a::2], kr[:, 1 - a::2]], 1) for a in (0, 1))
    quarters = np.concatenate([z[:, s:s + P] for s in range(0, W, P) for z in (ci, cc, cb, gc, gm, gr)], 1)
    w_in = np.concatenate([k, v, wdf, wdb, adf, adb, kv, rot, rot, swap, swap, r, ql, quarters], 1)
    branches = [feature_tiles(a[n][0]) for n in ("w_br_mla", "w_br_conv", "w_br_rwkv")]
    gates = [feature_tiles(gl[:, b * D:(b + 1) * D]) for b in range(3)]
    merge = np.concatenate([np.stack(gates, 1), np.stack(branches, 1)], 3).reshape(3 * KD, P, D + W)
    uq = a["w_uq"][0].reshape(Q_LORA, HEADS, QK_HEAD)
    e, o = uq[:, :, NOPE::2], uq[:, :, NOPE + 1::2]
    uq = np.concatenate([uq[:, :, :NOPE], e, o, o, e], 2).reshape(Q_LORA, HEADS * P)
    ukv = a["w_ukv"][0].reshape(KV_LORA, HEADS, 2, HEAD).transpose(0, 2, 1, 3).reshape(KV_LORA, 2 * W)
    zero = np.zeros((HEAD, W), np.float32)
    up = [np.concatenate([m[0, 0], zero, zero, m[0, 1]], 0) for m in (a["w_up"], a["a_up"])]
    up = np.concatenate([u.reshape(2, P, W).transpose(1, 0, 2).reshape(P, 2 * W) for u in up], 1)
    freq = THETA ** (-np.arange(ROPE // 4, dtype=np.float32) / (ROPE // 4))
    tok = np.arange(SEQ)
    ang = np.concatenate([(tok // GRID_W).astype(np.float32)[None] * freq[:, None],
                          (tok % GRID_W).astype(np.float32)[None] * freq[:, None]]).astype(np.float32)
    cos, sin = np.cos(ang), np.sin(ang)
    rope = np.concatenate([cos, cos, -sin, sin]).astype(np.float32)
    return {
        "x": a["x"][0], "ctx": a["ctx"][0], "cols": vectors(a), "w_in": feature_tiles(w_in),
        "wm": a["w_mod"][0],
        "up": up, "rope": rope,
        "uq": feature_tiles(uq), "uk": feature_tiles(ukv[:, :W], NOPE), "uv": feature_tiles(ukv[:, W:]),
        "w_merge": merge, "w_out": a["w_out"][0],
    }


def kernel(**inputs):
    import numpy as np
    import concourse.bacc as bacc
    from concourse.bass_utils import run_bass_kernel_spmd

    nc = bacc.Bacc("TRN2", target_bir_lowering=False, num_devices=1)
    arrays, io = {}, {}
    for name, v in laid_out({k: np.asarray(v) for k, v in inputs.items()}).items():
        arrays[f"{name}_dram"] = np.ascontiguousarray(v)
        io[name] = nc.dram_tensor(f"{name}_dram", v.shape, mybir.dt.from_np(v.dtype), kind="ExternalInput").ap()
    io["out"] = nc.dram_tensor("out_dram", (SEQ, D), F32, kind="ExternalOutput").ap()
    scratch(nc, io)
    build(nc, io)
    got = run_bass_kernel_spmd(nc, [arrays], core_ids=[0]).results[0]["out_dram"]
    return got.reshape(1, SEQ, D)
```
